# Optimizing a Trainium2 kernel written in Bass

```python
import jax, jax.numpy as jnp
from jax import lax
import numpy as np
import math

D_MODEL = 1024
BATCH = 1
SEQ = 1024
DEPTH = 1

CHUNK = 64
Q_BLOCK = 128
NORM_EPS = 1e-6

GDN_HEADS = 4
GDN_HEAD_DIM = 128
GDN_WIDTH = GDN_HEADS * GDN_HEAD_DIM
CONV_WIDTH = 4

MLA_HEADS = 8
MLA_NOPE_DIM = 64
MLA_ROPE_DIM = 32
MLA_V_DIM = 64
MLA_Q_RANK = 256
MLA_KV_RANK = 128
MLA_WIDTH = MLA_HEADS * MLA_V_DIM
ROPE_THETA = 10000.0

MIX_WIDTH = GDN_WIDTH + MLA_WIDTH
D_FF = 4 * D_MODEL

IN_SIZES = (GDN_WIDTH, GDN_WIDTH, GDN_WIDTH, GDN_WIDTH, GDN_HEADS, GDN_HEADS,
            MLA_Q_RANK, MLA_KV_RANK, MLA_ROPE_DIM)
IN_WIDTH = 4 * GDN_WIDTH + 2 * GDN_HEADS + MLA_Q_RANK + MLA_KV_RANK + MLA_ROPE_DIM


def rms_norm(x, gain):
    xf = x.astype(jnp.float32)
    y = xf * lax.rsqrt(jnp.mean(xf * xf, axis=-1, keepdims=True) + NORM_EPS)
    return (y * gain.astype(jnp.float32)).astype(x.dtype)

def l2_norm(x):
    xf = x.astype(jnp.float32)
    return xf * lax.rsqrt(jnp.sum(xf * xf, axis=-1, keepdims=True) + NORM_EPS)

def causal_depthwise_conv(x, w):
    k = w.shape[0]
    return lax.conv_general_dilated(
        x, w[:, None, :].astype(x.dtype), window_strides=(1,), padding=[(k - 1, 0)],
        dimension_numbers=("NWC", "WIO", "NWC"), feature_group_count=x.shape[-1])

def rope_angles(positions):
    inv_freq = ROPE_THETA ** (-jnp.arange(0, MLA_ROPE_DIM, 2, dtype=jnp.float32) / MLA_ROPE_DIM)
    ang = positions.astype(jnp.float32)[..., None] * inv_freq
    return jnp.cos(ang), jnp.sin(ang)

def apply_rope(x, cos, sin):
    xf = x.astype(jnp.float32)
    x1, x2 = jnp.split(xf, 2, axis=-1)
    return jnp.concatenate([x1 * cos - x2 * sin, x2 * cos + x1 * sin], axis=-1).astype(x.dtype)

def gated_delta_rule(q, k, v, beta, log_a):
    b, s, h, dk = q.shape
    dv = v.shape[-1]
    n = s // CHUNK

    def chunks(t):
        t = t.reshape((b, n, CHUNK, h) + t.shape[3:])
        return jnp.moveaxis(t, 3, 1)

    q, k, v = chunks(q), chunks(k), chunks(v)
    beta, log_a = chunks(beta), chunks(log_a)
    g = jnp.cumsum(log_a, axis=-1)
    idx = jnp.arange(CHUNK)
    strict = idx[:, None] > idx[None, :]
    causal = idx[:, None] >= idx[None, :]
    gdiff = g[..., :, None] - g[..., None, :]
    decay_strict = jnp.exp(jnp.where(strict, gdiff, -jnp.inf))
    decay_causal = jnp.exp(jnp.where(causal, gdiff, -jnp.inf))

    k_beta = k * beta[..., None]
    a_mat = jnp.einsum("bhnid,bhnjd->bhnij", k_beta, k) * decay_strict
    eye = jnp.eye(CHUNK, dtype=jnp.float32)
    t_inv = lax.linalg.triangular_solve(eye + a_mat, jnp.broadcast_to(eye, a_mat.shape),
                                        left_side=True, lower=True)
    u = t_inv @ (v * beta[..., None])
    w = t_inv @ (k_beta * jnp.exp(g)[..., None])
    p = jnp.einsum("bhnid,bhnjd->bhnij", q, k) * decay_causal
    q_dec = q * jnp.exp(g)[..., None]
    g_last = g[..., -1]
    k_dec = k * jnp.exp(g_last[..., None] - g)[..., None]

    def step(state, xs):
        q_c, k_c, u_c, w_c, p_c, gl = xs
        v_new = u_c - jnp.einsum("bhcd,bhde->bhce", w_c, state)
        o = (jnp.einsum("bhcd,bhde->bhce", q_c, state)
             + jnp.einsum("bhij,bhje->bhie", p_c, v_new))
        state = state * jnp.exp(gl)[..., None, None] + jnp.einsum("bhcd,bhce->bhde", k_c, v_new)
        return state, o

    xs = tuple(jnp.moveaxis(t, 2, 0) for t in (q_dec, k_dec, u, w, p, g_last))
    state0 = jnp.zeros((b, h, dk, dv), jnp.float32)
    _, o = lax.scan(step, state0, xs)
    return jnp.transpose(o, (1, 0, 3, 2, 4)).reshape(b, s, h, dv)

def gated_deltanet_group(q, k, v, gate, a_logit, b_logit, conv_w, a_log, dt_bias, out_norm):
    bsz, s, _ = q.shape
    qkv = jax.nn.silu(causal_depthwise_conv(jnp.concatenate([q, k, v], axis=-1), conv_w))
    q, k, v = jnp.split(qkv, 3, axis=-1)
    q = l2_norm(q.reshape(bsz, s, GDN_HEADS, GDN_HEAD_DIM)) * (GDN_HEAD_DIM ** -0.5)
    k = l2_norm(k.reshape(bsz, s, GDN_HEADS, GDN_HEAD_DIM))
    v = v.reshape(bsz, s, GDN_HEADS, GDN_HEAD_DIM).astype(jnp.float32)
    beta = jax.nn.sigmoid(b_logit.astype(jnp.float32))
    log_a = -jnp.exp(a_log.astype(jnp.float32)) * jax.nn.softplus(
        a_logit.astype(jnp.float32) + dt_bias.astype(jnp.float32))
    o = gated_delta_rule(q, k, v, beta, log_a)
    g = jax.nn.silu(gate.astype(jnp.float32)).reshape(bsz, s, GDN_HEADS, GDN_HEAD_DIM)
    o = rms_norm(o, out_norm) * g
    return o.reshape(bsz, s, GDN_WIDTH).astype(gate.dtype)

def mla_group(c_q, c_kv, k_rope, cos, sin, q_norm, w_q_up, kv_norm, w_kv_up):
    b, s, _ = c_q.shape
    dqk = MLA_NOPE_DIM + MLA_ROPE_DIM
    q = (rms_norm(c_q, q_norm) @ w_q_up).reshape(b, s, MLA_HEADS, dqk)
    q_nope, q_rope = q[..., :MLA_NOPE_DIM], q[..., MLA_NOPE_DIM:]
    kv = (rms_norm(c_kv, kv_norm) @ w_kv_up).reshape(b, s, MLA_HEADS, MLA_NOPE_DIM + MLA_V_DIM)
    k_nope, v = kv[..., :MLA_NOPE_DIM], kv[..., MLA_NOPE_DIM:]
    q_rope = apply_rope(q_rope, cos[:, :, None, :], sin[:, :, None, :])
    k_rope = apply_rope(k_rope, cos, sin)
    q = jnp.concatenate([q_nope, q_rope], axis=-1)
    k = jnp.concatenate(
        [k_nope, jnp.broadcast_to(k_rope[:, :, None, :], (b, s, MLA_HEADS, MLA_ROPE_DIM))], axis=-1)
    scale = dqk ** -0.5
    n_blk = s // Q_BLOCK
    q_blocks = jnp.moveaxis(q.reshape(b, n_blk, Q_BLOCK, MLA_HEADS, dqk), 1, 0)
    key_chunk = jnp.arange(s) // CHUNK

    def attend(xs):
        q_b, blk = xs
        q_chunk = (blk * Q_BLOCK + jnp.arange(Q_BLOCK)) // CHUNK
        scores = jnp.einsum("bqhd,bkhd->bhqk", q_b, k,
                            preferred_element_type=jnp.float32) * scale
        mask = key_chunk[None, :] <= q_chunk[:, None]
        probs = jax.nn.softmax(jnp.where(mask, scores, -jnp.inf), axis=-1).astype(v.dtype)
        return jnp.einsum("bhqk,bkhd->bqhd", probs, v)

    o = lax.map(attend, (q_blocks, jnp.arange(n_blk)))
    return jnp.moveaxis(o, 0, 1).reshape(b, s, MLA_WIDTH)

def first_inputs(seed: int = 0) -> dict:
    key = jax.random.key(seed)
    ks = jax.random.split(key, 20)
    f32 = jnp.float32

    def normal(k, shape, fan_in):
        return jax.random.normal(k, shape, f32) * (fan_in ** -0.5)

    def gain(k, shape):
        return 1.0 + 0.1 * jax.random.normal(k, shape, f32)

    x = jax.random.normal(ks[0], (BATCH, SEQ, D_MODEL), f32)
    offsets = jax.random.randint(ks[1], (BATCH, 1), 0, 4096)
    positions = (offsets + jnp.arange(SEQ)[None, :]).astype(jnp.int32)
    a_log = jnp.log(jax.random.uniform(ks[2], (DEPTH, GDN_HEADS), f32, 1.0, 16.0))
    dt = jnp.exp(jax.random.uniform(ks[3], (DEPTH, GDN_HEADS), f32,
                                    float(np.log(1e-3)), float(np.log(1e-1))))
    dt_bias = dt + jnp.log(-jnp.expm1(-dt))
    return {
        "x": x,
        "positions": positions,
        "mix_pre_norm": gain(ks[4], (DEPTH, D_MODEL)),
        "w_in": normal(ks[5], (DEPTH, D_MODEL, IN_WIDTH), D_MODEL),
        "conv_w": normal(ks[6], (DEPTH, CONV_WIDTH, 3 * GDN_WIDTH), CONV_WIDTH),
        "a_log": a_log,
        "dt_bias": dt_bias,
        "gdn_out_norm": gain(ks[7], (DEPTH, GDN_HEAD_DIM)),
        "q_norm": gain(ks[8], (DEPTH, MLA_Q_RANK)),
        "w_q_up": normal(ks[9], (DEPTH, MLA_Q_RANK, MLA_HEADS * (MLA_NOPE_DIM + MLA_ROPE_DIM)), MLA_Q_RANK),
        "kv_norm": gain(ks[10], (DEPTH, MLA_KV_RANK)),
        "w_kv_up": normal(ks[11], (DEPTH, MLA_KV_RANK, MLA_HEADS * (MLA_NOPE_DIM + MLA_V_DIM)), MLA_KV_RANK),
        "w_out": normal(ks[12], (DEPTH, MIX_WIDTH, D_MODEL), MIX_WIDTH),
        "mix_post_norm": gain(ks[13], (DEPTH, D_MODEL)),
        "ffn_pre_norm": gain(ks[14], (DEPTH, D_MODEL)),
        "w_up": normal(ks[15], (DEPTH, D_MODEL, D_FF), D_MODEL),
        "w_down": normal(ks[16], (DEPTH, D_FF, D_MODEL), D_FF),
        "ffn_post_norm": gain(ks[17], (DEPTH, D_MODEL)),
    }

def first_block(x, positions, mix_pre_norm, w_in, conv_w, a_log, dt_bias, gdn_out_norm,
              q_norm, w_q_up, kv_norm, w_kv_up, w_out, mix_post_norm,
              ffn_pre_norm, w_up, w_down, ffn_post_norm):
    cos, sin = rope_angles(positions)
    offsets = [int(o) for o in np.cumsum(IN_SIZES)[:-1]]
    for l in range(DEPTH):
        h = rms_norm(x, mix_pre_norm[l])
        proj = h @ w_in[l]
        gq, gk, gv, gg, ga, gb, cq, ckv, kr = jnp.split(proj, offsets, axis=-1)
        o_gdn = gated_deltanet_group(gq, gk, gv, gg, ga, gb, conv_w[l], a_log[l],
                                     dt_bias[l], gdn_out_norm[l])
        o_mla = mla_group(cq, ckv, kr, cos, sin, q_norm[l], w_q_up[l], kv_norm[l], w_kv_up[l])
        mixed = jnp.concatenate([o_gdn.astype(x.dtype), o_mla.astype(x.dtype)], axis=-1) @ w_out[l]
        x = x + rms_norm(mixed, mix_post_norm[l])
        h = rms_norm(x, ffn_pre_norm[l])
        f = jnp.square(jax.nn.relu(h @ w_up[l])) @ w_down[l]
        x = x + rms_norm(f, ffn_post_norm[l])
    return x


CONV_WIDTH_2 = 512
CONV_GROUPS = 8
CONV_TAPS = 3
N_HEADS = 8
HEAD_DIM = 64
ATTN_WIDTH = N_HEADS * HEAD_DIM
D_FF_2 = 4 * D_MODEL
N_MOD = 6
EPS = 1e-6
IN_COLS = 3 * CONV_WIDTH_2 + 3 * ATTN_WIDTH + 2 * D_MODEL


def rms_norm_2(x, g):
    xf = x.astype(jnp.float32)
    y = xf * lax.rsqrt(jnp.mean(xf * xf, axis=-1, keepdims=True) + EPS)
    return (y * g.astype(jnp.float32)).astype(x.dtype)

def modulate(h, shift, scale):
    return h * (1.0 + scale[:, None, :]) + shift[:, None, :]

def short_conv_branch(b_gate, c_gate, u, conv_w):
    s = u.shape[1]
    v = c_gate * u
    vp = jnp.pad(v, ((0, 0), (CONV_TAPS - 1, 0), (0, 0)))
    y = sum(conv_w[k] * vp[:, k:k + s, :] for k in range(CONV_TAPS))
    return b_gate * y

def stick_breaking_attention(q, k, v):
    b, s, h, dh = q.shape
    qh = jnp.transpose(q, (0, 2, 1, 3))
    kh = jnp.transpose(k, (0, 2, 1, 3))
    vh = jnp.transpose(v, (0, 2, 1, 3))
    inv_sqrt = 1.0 / math.sqrt(dh)
    key_pos = jnp.arange(s)
    n_blocks = s // Q_BLOCK

    def block(i):
        start = i * Q_BLOCK
        q_blk = lax.dynamic_slice_in_dim(qh, start, Q_BLOCK, axis=2)
        z = jnp.einsum('bhqd,bhkd->bhqk', q_blk, kh).astype(jnp.float32) * inv_sqrt
        q_pos = start + jnp.arange(Q_BLOCK)
        mask = key_pos[None, :] < q_pos[:, None]
        log_1m_beta = jnp.where(mask, jax.nn.log_sigmoid(-z), 0.0)
        suffix = lax.cumsum(log_1m_beta, axis=3, reverse=True) - log_1m_beta
        a = jnp.where(mask, jnp.exp(jax.nn.log_sigmoid(z) + suffix), 0.0)
        return jnp.einsum('bhqk,bhkd->bhqd', a, vh.astype(jnp.float32)).astype(q.dtype)

    o = lax.map(block, jnp.arange(n_blocks))
    o = jnp.transpose(o, (1, 0, 3, 2, 4))
    return o.reshape(b, s, h * dh)

def second_inputs(seed: int = 0) -> dict:
    key = jax.random.key(seed)
    ks = jax.random.split(key, 16)
    f32 = jnp.float32
    L, D = DEPTH, D_MODEL

    def nrm(k, shape, fan_in):
        return jax.random.normal(k, shape, f32) * (fan_in ** -0.5)

    def gain(k):
        return 1.0 + 0.05 * jax.random.normal(k, (L, D), f32)

    return {
        "x": jax.random.normal(ks[0], (BATCH, SEQ, D), f32),
        "c": jax.random.normal(ks[1], (BATCH, D), f32),
        "w_ada": nrm(ks[2], (L, D, N_MOD * D), D) * 0.5,
        "b_ada": 0.01 * jax.random.normal(ks[3], (L, N_MOD * D), f32),
        "g_pre_mix": gain(ks[4]),
        "g_post_mix": gain(ks[5]),
        "g_pre_mlp": gain(ks[6]),
        "g_post_mlp": gain(ks[7]),
        "w_in": nrm(ks[8], (L, D, IN_COLS), D),
        "conv_w": nrm(ks[9], (L, CONV_TAPS, CONV_WIDTH_2), CONV_TAPS),
        "w_proj_conv": nrm(ks[10], (L, CONV_WIDTH_2, D), CONV_WIDTH_2),
        "w_proj_attn": nrm(ks[11], (L, ATTN_WIDTH, D), ATTN_WIDTH),
        "w_out": nrm(ks[12], (L, D, D), D),
        "w_mlp_in": nrm(ks[13], (L, D, D_FF_2), D),
        "w_mlp_out": nrm(ks[14], (L, D_FF_2, D), D_FF_2),
    }

def second_block(x, c, w_ada, b_ada, g_pre_mix, g_post_mix, g_pre_mlp, g_post_mlp,
              w_in, conv_w, w_proj_conv, w_proj_attn, w_out, w_mlp_in, w_mlp_out):
    b, s, d = x.shape
    split_pts = np.cumsum([CONV_WIDTH_2, CONV_WIDTH_2, CONV_WIDTH_2,
                           ATTN_WIDTH, ATTN_WIDTH, ATTN_WIDTH, D_MODEL])
    for l in range(DEPTH):
        mod = c @ w_ada[l] + b_ada[l]
        sh1, sc1, gt1, sh2, sc2, gt2 = jnp.split(mod, N_MOD, axis=-1)

        h = modulate(rms_norm_2(x, g_pre_mix[l]), sh1, sc1)
        proj = h @ w_in[l]
        bg, cg, u, q, k, v, ga, gb = jnp.split(proj, split_pts, axis=-1)
        y_conv = short_conv_branch(bg, cg, u, conv_w[l]) @ w_proj_conv[l]
        o = stick_breaking_attention(q.reshape(b, s, N_HEADS, HEAD_DIM),
                                     k.reshape(b, s, N_HEADS, HEAD_DIM),
                                     v.reshape(b, s, N_HEADS, HEAD_DIM))
        y_attn = o @ w_proj_attn[l]
        merged = jax.nn.sigmoid(ga) * y_conv + jax.nn.sigmoid(gb) * y_attn
        mix_out = merged @ w_out[l]
        x = x + gt1[:, None, :] * rms_norm_2(mix_out, g_post_mix[l])

        h2 = modulate(rms_norm_2(x, g_pre_mlp[l]), sh2, sc2)
        ff = jnp.square(jax.nn.relu(h2 @ w_mlp_in[l])) @ w_mlp_out[l]
        x = x + gt2[:, None, :] * rms_norm_2(ff, g_post_mlp[l])
    return x


def setup_inputs(seed=0):
    out = dict(first_inputs(seed))
    for name, value in second_inputs(seed + 1).items():
        if name != "x":
            out[name + "_2"] = value
    return out


def reference(
    x, positions, mix_pre_norm, w_in, conv_w, a_log, dt_bias, gdn_out_norm, q_norm, w_q_up,
    kv_norm, w_kv_up, w_out, mix_post_norm, ffn_pre_norm, w_up, w_down, ffn_post_norm, c_2,
    w_ada_2, b_ada_2, g_pre_mix_2, g_post_mix_2, g_pre_mlp_2, g_post_mlp_2, w_in_2, conv_w_2,
    w_proj_conv_2, w_proj_attn_2, w_out_2, w_mlp_in_2, w_mlp_out_2,
):
    x = first_block(
        x, positions, mix_pre_norm, w_in, conv_w, a_log, dt_bias, gdn_out_norm, q_norm, w_q_up,
        kv_norm, w_kv_up, w_out, mix_post_norm, ffn_pre_norm, w_up, w_down, ffn_post_norm,
    )
    return second_block(
        x, c_2, w_ada_2, b_ada_2, g_pre_mix_2, g_post_mix_2, g_pre_mlp_2, g_post_mlp_2, w_in_2,
        conv_w_2, w_proj_conv_2, w_proj_attn_2, w_out_2, w_mlp_in_2, w_mlp_out_2,
    )


_drawn_inputs = setup_inputs


def setup_inputs(seed=0):
    import zlib

    import numpy as np

    out = dict(_drawn_inputs(seed))
    spreads = {}
    factors = {'q_norm': 3.555,
     'b_ada_2': 5.437,
     'g_post_mix_2': 4.236,
     'g_pre_mlp_2': 4.196,
     'g_post_mlp_2': 4.137}
    for name, (base, spread) in spreads.items():
        noise = np.random.default_rng([zlib.crc32(name.encode()), seed]).standard_normal(out[name].shape)
        drawn = base * np.exp(spread * noise) if base else spread * noise
        out[name] = __import__('jax').numpy.asarray(drawn.astype(out[name].dtype))
    for name, factor in factors.items():
        out[name] = (out[name] * factor).astype(out[name].dtype)
    return out
```

```python
import math
from contextlib import ExitStack

import concourse.bass as bass
import numpy as np
from concourse import mybir

F32 = mybir.dt.float32
F32R = mybir.dt.float32r
I32 = mybir.dt.int32
ALU = mybir.AluOpType
ACT = mybir.ActivationFunctionType
AX_X = mybir.AxisListType.X

P = 128
D = 1024
SEQ = 1024
NT = SEQ // P
KD = D // P
HALF = 512
EPS = 1e-6
D_FF = 4 * D

GDN_HEADS = 4
CHUNK = 64
GDN_W = GDN_HEADS * P
CONV_W = 4
MLA_HEADS = 8
NOPE = 64
ROPE = 32
DQK = NOPE + ROPE
V_DIM = 64
Q_RANK = 256
KV_RANK = 128
ROPE_THETA = 10000.0
GATE_COL = 3 * GDN_W
TAIL_COL = 4 * GDN_W
TAIL_W = 2 * GDN_HEADS + Q_RANK + KV_RANK + ROPE
LAT_CQ = 2 * GDN_HEADS
LAT_CKV = LAT_CQ + Q_RANK
LAT_KR = LAT_CKV + KV_RANK
GDN_PANELS = 3 * GDN_HEADS

CONV2 = 512
CONV2_TAPS = 3
CONV2_PANELS = CONV2 // P
SB_HEADS = 8
SB_DIM = 64
IN2_Q = 3 * CONV2
IN2_K = IN2_Q + 512
IN2_V = IN2_K + 512
IN2_GA = IN2_V + 512
IN2_GB = IN2_GA + D
N_MOD = 6

FFN_STEPS = D_FF // 256
FFN_CREDIT = 2
ADA_STEP = N_MOD * KD // FFN_STEPS
MLA_GROUPS_BY = [sum(n // 4 + 1 for n in range(t + 1)) for t in range(NT)]
MLA_GROUPS = MLA_GROUPS_BY[-1]

SB_PAIRS = SB_HEADS // 2
SB_ITEMS = 2 * NT
SB_LAG_ARG, SB_LAG_EXP, SB_LAG_TURN, SB_LAG_PV = 1, 2, 3, 4


def sb_groups(s):
    first = sum(u // 2 // 4 + 1 for u in range(s))
    return range(first, first + s // 2 // 4 + 1)


SB_GROUPS = sb_groups(SB_ITEMS - 1)[-1] + 1

TWO_PI = 2 * math.pi
TWO_PI_MID = math.floor((TWO_PI - 6.28125) * 2 ** 21) / 2 ** 21
TWO_PI_PARTS = (6.28125, TWO_PI_MID, TWO_PI - 6.28125 - TWO_PI_MID)
ROUND = 1.5 * 2.0 ** 23
PI_BELOW = 3.1415925

C_ID, C_ONES, C_CSUM, C_STRICT, C_CHUNK = 0, 128, 256, 384, 512
LEVELS = (1, 2, 4, 8, 16, 32)
C_LEVEL = 640
C_KEYLT = C_LEVEL + P * len(LEVELS)
C_KEYCAP = C_KEYLT + P
C_FREQ = C_KEYCAP + P
C_SIGN = C_FREQ + 1
N_CONST = C_SIGN + 1

V_MIXPRE, V_FFNPRE, V_QN, V_KVN, V_CONV = 0, 8, 16, 18, 19
V_GPREMIX2 = V_CONV + CONV_W * GDN_PANELS
V_GPREMLP2 = V_GPREMIX2 + KD
V_CONV2 = V_GPREMLP2 + KD
N_VEC = V_CONV2 + CONV2_TAPS * (CONV2 // P)
N_BADA = N_MOD * KD
N_VEC2 = N_BADA + KD


def constants():
    c = np.zeros((P, N_CONST), np.float32)
    r, k = np.arange(P)[:, None], np.arange(P)[None, :]
    same = r // CHUNK == k // CHUNK
    c[:, C_ID:C_ID + P] = r == k
    c[:, C_ONES:C_ONES + P] = 1.0
    c[:, C_CSUM:C_CSUM + P] = same & (r <= k)
    c[:, C_STRICT:C_STRICT + P] = same & (r < k)
    c[:, C_CHUNK:C_CHUNK + P] = same
    for n, s in enumerate(LEVELS):
        c[:, C_LEVEL + n * P:C_LEVEL + (n + 1) * P] = ((k // s) % 2 == 1) & (r // s == k // s - 1)
    c[:, C_KEYLT:C_KEYLT + P] = k < r
    c[:, C_KEYCAP:C_KEYCAP + P] = np.where(k < r, 3e38, -1e30)
    j = np.arange(ROPE // 2)
    freq = (ROPE_THETA ** (-2.0 * j / ROPE)).astype(np.float32)
    c[NOPE:DQK, C_FREQ] = np.concatenate([freq, freq])
    c[NOPE:DQK, C_SIGN] = np.concatenate([-np.ones(ROPE // 2), np.ones(ROPE // 2)])
    return c


class Ring:

    SLOTS = 4

    def __init__(self, sem, total, raws, his, los, after=None):
        self.raw, self.hi, self.lo = raws, his, los
        self.nraw, self.nslab, self.total = len(raws), len(his), total
        self.raw_full = [sem(f"w_raw_full{r}") for r in range(self.SLOTS)]
        self.load_begun, self.split_begun = sem("w_load_begun"), sem("w_split_begun")
        self.hi_done, self.split_done, self.used = sem("w_hi_done"), sem("w_split_done"), sem("w_slab_used")
        self.base = after.base + after.total if after else 0
        self.fills = after.fills_after if after else [0] * self.SLOTS
        self.fills_after = [self.fills[r] + (len(range(r, total, self.nraw)) if r < self.nraw else 0)
                            for r in range(self.SLOTS)]

    def credit(self, eng):
        eng.sem_inc(self.split_done, self.SLOTS)
        eng.sem_inc(self.used, self.SLOTS)

    def start(self, sp):
        sp.wait_ge(self.split_done, self.SLOTS + self.base)

    def start_split(self, pool):
        pool.wait_ge(self.used, self.SLOTS + self.base)

    def load(self, sp, n0, j, view, src):
        r = j % self.nraw
        sp.wait_ge(self.split_done, n0 + (self.SLOTS + self.base + j - self.nraw + 1))
        sp.sem_inc(self.load_begun, 1)
        sp.dma_start(view(self.raw[r]), src).then_inc(self.raw_full[r], 16)

    def split(self, pool, n0, trips, j, width=1024):
        r, s = j % self.nraw, j % self.nslab
        pool.wait_ge(self.raw_full[r], trips * 16 + (self.fills[r] * 16 + 16))
        pool.wait_ge(self.used, n0 + (self.SLOTS + self.base + j - self.nslab + 1))
        pool.sem_inc(self.split_begun, 1)
        pool.tensor_scalar(self.hi[s][:, 0:width], self.raw[r][:, 0:width], 1.0, 0.0, ALU.mult, ALU.add)\
            .then_inc(self.hi_done, 1)
        pool.wait_ge(self.hi_done, n0 + (self.base + j + 1))
        pool.tensor_tensor(self.lo[s][:, 0:width], self.raw[r][:, 0:width], self.hi[s][:, 0:width].bitcast(F32),
                           ALU.subtract).then_inc(self.split_done, 1)

    def ready(self, pe, n0, j):
        pe.wait_ge(self.split_done, n0 + (self.SLOTS + self.base + j + 1))

    def panel_done(self, eng, n0, j):
        eng.wait_ge(self.used, n0 + (self.SLOTS + self.base + j + 1))


class Chain:

    def __init__(self, eng, s):
        self.eng, self.s, self.base, self.n = eng, s, 0, 0

    def link(self, ins):
        ins.then_inc(self.s, 1)
        self.n += 1
        self.eng.wait_ge(self.s, self.base + self.n)

    def loop(self, i, per):
        self.start = self.base + self.n
        self.base, self.n, self.per = self.start + i * per, 0, per

    def end(self, trips):
        assert self.n == self.per, (self.n, self.per)
        self.base, self.n = self.start + trips * self.per, 0


def two_blocks(nc, d, out):
    ctx = ExitStack()
    with ctx:
        sems = {}

        def sem(name):
            if name not in sems:
                sems[name] = ctx.enter_context(nc.semaphore(name))
            return sems[name]

        SB0 = 16512

        def sb(name, kb, shape, dt=F32):
            t = nc.alloc_sbuf_tensor_at(name, list(shape), dt, offset=SB0 + int(kb * 1024))
            return t

        consts = sb("consts", 0, [P, N_CONST])
        vec = sb("vec_cols", 6.75, [P, N_VEC])
        vec2 = sb("vec2_cols", 7.25, [P, N_VEC2])
        mod = sb("mod_cols", 7.53125, [P, N_BADA])
        ssq = sb("ssq", 7.75, [P, NT])
        rstd = sb("rstd", 7.78125, [P, NT])
        mean_sq = sb("mean_sq", 7.8125, [P, NT])
        scale2 = sb("scale2_cols", 7.84375, [P, 2 * KD])
        half_neg = sb("minus_half", 7.90625, [P, 64])
        ident = consts[:, C_ID:C_ID + P]
        ones = consts[:, C_ONES:C_ONES + P]

        raws = [sb(f"raw{r}", 9 + 4 * r, [P, 1024]) for r in range(4)]
        slab_hi = [sb(f"slab_hi{s}", 25 + 8 * s, [P, 1024], F32R) for s in range(4)]
        slab_lo = [sb(f"slab_lo{s}", 29 + 8 * s, [P, 1024], F32R) for s in range(4)]

        act_hi = sb("act_hi", 57, [P, KD, SEQ], F32R)
        act_lo = sb("act_lo", 89, [P, KD, SEQ], F32R)
        acc = sb("acc", 121, [P, NT, D])
        resid = sb("resid", 153, [P, NT, D])
        norm_tmp = [sb(f"norm_tmp{i}", 203 + 2 * i, [P, HALF]) for i in range(2)]
        qkv = sb("qkv_feat", 121, [P, GDN_PANELS, SEQ])
        gate = sb("gate_tok", 169, [P, NT, GDN_W])
        lat = sb("lat_tok", 185, [P, NT, TAIL_W])
        gate_tanh = [sb(f"gate_tanh{i}", 203 + 2 * i, [P, HALF]) for i in range(2)]
        out_norm_row = sb("out_norm_row", 49, [P, P])
        xpad = sb("conv_in", 198.5, [P, SEQ + CONV_W - 1])
        conv_y = sb("conv_y", 49, [P, SEQ])
        conv_t = sb("conv_tanh", 53, [P, SEQ])
        ss_gdn = sb("ss_gdn", 203.5, [P, NT, GDN_PANELS])
        vec_rows = sb("vec_rows", 185, [P, P])
        vec2_rows = sb("vec2_rows", 185.5, [P, P])
        mix = sb("mix_tok", 57, [P, NT, D])
        cq_f = sb("cq_feat", 89, [P, 2, SEQ])
        ckv_f = sb("ckv_feat", 97, [P, SEQ])
        cos_f = sb("cos_feat", 101, [P, SEQ])
        sin_f = sb("sin_feat", 105, [P, SEQ])
        q_f = sb("q_feat", 109, [P, SEQ])
        k_f = sb("k_feat", 113, [P, SEQ])
        rope_t = sb("rope_tmp", 117, [P, SEQ])
        v_t = sb("v_tok", 9, [P, NT, MLA_HEADS, V_DIM])
        probs = [sb(f"probs{i}", 25 + 4 * i, [P, SEQ]) for i in range(2)]
        probs_t = [sb(f"probs_t{i}", 33 + 2 * i, [P, HALF]) for i in range(2)]
        wq = sb("wq_head", 37, [P, 2, DQK])
        wq_swap = sb("wq_swap_head", 37.75, [P, 2, ROPE])
        wk = sb("wk_head", 38, [P, NOPE])
        w_kv = sb("w_kv_all", 39, [P, 1024])
        sm_max = sb("sm_max", 38.25, [P, NT])
        sm_neg = sb("sm_neg", 38.28125, [P, NT])
        sm_sum = sb("sm_sum", 38.3125, [P, NT])
        sm_rec = sb("sm_rec", 38.34375, [P, NT])
        lat_n = sb("lat_norm", 57, [P, NT, 448])
        lat_junk = sb("lat_junk", 71, [P, NT, Q_RANK + KV_RANK])
        lat_ss = sb("lat_ss", 43, [P, 2 * NT])
        lat_ms = sb("lat_ms", 43.0625, [P, 2 * NT])
        lat_rstd = sb("lat_rstd", 43.125, [P, 2 * NT])
        pos_i = sb("pos_i", 45, [P, SEQ], I32)
        ang = sb("rope_ang", 49, [P, SEQ])
        turns = sb("rope_turns", 53, [P, SEQ])

        def small(name, slot):
            return sb(name, 205.5 + 0.125 * slot, [P, NT, GDN_HEADS])

        g_arg, g_exp, g_sp, g_la, g_beta, g_cum, g_tot, g_eg, g_ekd, g_rk, g_rq, g_bk, g_cw, g_cd, g_cv = [
            small(n, i) for i, n in enumerate(
                ["g_arg", "g_exp", "g_softplus", "g_log_a", "g_beta", "g_cumsum", "g_total", "g_exp_cum",
                 "g_exp_tail", "g_rk", "g_rq", "g_beta_rk", "g_w_scale", "g_kdec_scale", "g_v_scale"])]
        a_log_b = sb("a_log_bc", 207.375, [P, GDN_HEADS])
        dt_b = sb("dt_bias_bc", 207.40625, [P, GDN_HEADS])
        ea_b = sb("exp_a_log", 207.4375, [P, GDN_HEADS])

        def head_tile(name, kb):
            return sb(name, kb, [P, GDN_HEADS, P])

        k_s, q_s, v_s = head_tile("k_tile", 9), head_tile("q_tile", 11), head_tile("v_tile", 13)
        u_g, i_b = head_tile("cumsum_la", 15), head_tile("ident_bk", 17)
        e_d, e_g, e_m = head_tile("decay", 19), head_tile("exp_g_row", 21), head_tile("decay_rk", 23)
        p_t, a_t = head_tile("p_T", 25), head_tile("a_T", 27)
        m_s = [head_tile(f"a_level{n}", 29 + 2 * n) for n in range(len(LEVELS))]
        t_f = [head_tile(f"t_inv{i}", 41 + 2 * i) for i in range(2)]
        t_r = [head_tile(f"t_inv_T{i}", 45 + 2 * i) for i in range(2)]
        y_s = head_tile("level_y", 49)
        k_w, k_d, v_b = head_tile("k_w", 51), head_tile("k_dec", 53), head_tile("v_beta", 55)
        w_t, u_s, q_d = head_tile("w_T", 89), head_tile("u", 91), head_tile("q_dec", 93)
        v_n, s_dec = head_tile("v_new", 95), head_tile("state_decayed", 97)
        state = [head_tile(f"state{i}", 99 + 2 * i) for i in range(2)]
        o_s, o_sq = head_tile("o_tok", 103), head_tile("o_sq", 105)
        o_ss = sb("o_ss", 107, [P, GDN_HEADS])
        o_ms = sb("o_ms", 107.03125, [P, GDN_HEADS])
        o_rstd = sb("o_rstd", 107.0625, [P, GDN_HEADS])

        act_hi_junk = sb("squares_junk_hi", 57, [P, NT, D])
        act_lo_junk = sb("squares_junk_lo", 89, [P, NT, D])
        hid_hi = sb("hid_hi", 185, [P, 2, SEQ], F32R)
        hid_lo = sb("hid_lo", 193, [P, 2, SEQ], F32R)
        relu_t = [sb(f"relu{i}", 201 + 2 * i, [P, HALF]) for i in range(2)]
        relu_sq = sb("relu_sq", 205, [P, HALF])
        mixt_hi = sb("mixt_hi", 89, [P, KD, SEQ], F32R)
        mixt_lo = sb("mixt_lo", 121, [P, KD, SEQ], F32R)
        mixed = sb("mixed", 57, [P, NT, D])
        post_row = sb("post_norm_row", 185, [P, D])
        post_tmp = [sb(f"post_tmp{i}", 189 + 4 * i, [P, D]) for i in range(2)]

        ada = [sb(f"w_ada{i}", 17 + 4 * i, [P, KD, P]) for i in range(2)]
        cg_t = sb("c_gate", 21, [P, SEQ])
        conv2_y = sb("conv2_y", 49, [P, SEQ])
        vpad = sb("conv2_in", 203, [P, SEQ + CONV2_TAPS - 1])
        y_hi = sb("conv2_out_hi", 121, [P, CONV2_PANELS, SEQ], F32R)
        y_lo = sb("conv2_out_lo", 137, [P, CONV2_PANELS, SEQ], F32R)
        merged = sb("merged_feat", 153, [P, KD, SEQ])
        conv_gate = [sb(f"conv_gate{i}", 185 + 4 * i, [P, SEQ]) for i in range(2)]
        v2 = sb("v2_tok", 185, [P, NT, SB_HEADS, SB_DIM])
        q2, k2 = sb("q2_feat", 17, [P, SEQ]), sb("k2_feat", 21, [P, SEQ])
        sb_z = [sb(f"sb_z{i}", 41 + 4 * i, [P, SEQ]) for i in range(2)]
        sb_sp = [sb(f"sb_softplus{i}", 49 + 4 * i, [P, SEQ]) for i in range(2)]
        sb_a = [sb(f"sb_weights{i}", 137 + 4 * i, [P, SEQ]) for i in range(3)]
        sb_at = [sb(f"sb_weights_t{i}", 201 + 2 * i, [P, HALF]) for i in range(2)]
        o2 = sb("o2_tok", 121, [P, NT, CONV2])
        o2_hi = sb("o2_feat_hi", 137, [P, CONV2_PANELS, SEQ], F32R)
        o2_lo = sb("o2_feat_lo", 185, [P, CONV2_PANELS, SEQ], F32R)
        attn_gate = [sb(f"attn_gate{i}", 121 + 4 * i, [P, SEQ]) for i in range(2)]
        attn_part = [sb(f"attn_part{i}", 129 + 4 * i, [P, SEQ]) for i in range(2)]
        gain_row = sb("post_gain_row", 199, [P, D])
        diag = sb("gate_diag", 189, [P, KD, P])

        ps = ctx.enter_context(nc.psum_tensor("ps", [P, 8, HALF], F32))

        R1 = Ring(sem, 8, raws, slab_hi[:3], slab_lo[:3])
        R2 = Ring(sem, GDN_PANELS, raws[:3], slab_hi[:3], slab_lo[:3], R1)
        R3 = Ring(sem, 8, raws, slab_hi, slab_lo, R2)
        R4 = Ring(sem, 4 * FFN_STEPS, raws[:2], slab_hi, slab_lo, R3)
        R5 = Ring(sem, 3 * CONV2_PANELS, raws[:3], slab_hi[:3], slab_lo[:3], R4)
        R6 = Ring(sem, 2 * KD, raws, slab_hi, slab_lo, R5)
        R7 = Ring(sem, 4, raws, slab_hi, slab_lo, R6)
        R8 = Ring(sem, SB_HEADS, raws[:2], slab_hi[:2], slab_lo[:2], R7)
        R9 = Ring(sem, 2 * KD, raws, slab_hi, slab_lo, R8)
        R10 = Ring(sem, 8, raws, slab_hi, slab_lo, R9)
        R11 = Ring(sem, 4 * FFN_STEPS, raws, slab_hi, slab_lo, R10)

        NORMS = ["n1", "mix_post", "n2", "ffn_post", "n3", "mix_post2", "n4", "ffn_post2"]
        TURNS = {"n1": 0, "mixt": 16, "n2": 32, "n3": 48, "sb_o": 64, "n4": 72}
        SCALES = ["n1", "n2", "n3", "n4"]
        FFNS = ["ffn", "ffn2"]

        x1_spill = nc.dram_tensor("x1_spill", [NT, P, D], F32, kind="Internal").ap()
        w_in2 = d["w_in_2"][0].rearrange("(k p) n -> p k n", p=P)
        w_pc = d["w_proj_conv_2"][0].rearrange("(k p) n -> p k n", p=P)
        w_pa = d["w_proj_attn_2"][0].rearrange("(k p) n -> p k n", p=P)
        w_out2 = d["w_out_2"][0].rearrange("(k p) n -> p k n", p=P)
        w_up2 = d["w_mlp_in_2"][0].rearrange("(k p) n -> p k n", p=P)
        w_ada = d["w_ada_2"][0].rearrange("(k p) n -> p k n", p=P)
        w_in = d["w_in"][0].rearrange("(k p) n -> p k n", p=P)
        w_out = d["w_out"][0].rearrange("(k p) n -> p k n", p=P)
        w_up = d["w_up"][0].rearrange("(k p) n -> p k n", p=P)
        w_down = d["w_down"][0].rearrange("(s p) n -> s p n", p=P)
        w_down2 = d["w_mlp_out_2"][0].rearrange("(s p) n -> s p n", p=P)
        x_tiles = d["x"][0].rearrange("(t p) d -> t p d", p=P)
        T_COLS = [(GATE_COL, HALF), (TAIL_COL, TAIL_W)]

        def half_view(n):
            return lambda raw: raw[:, 0:2 * n].rearrange("p (j n) -> p j n", j=2)

        def panel_view(raw):
            return raw[:, :].rearrange("p (k n) -> p k n", n=P)

        block = ctx.enter_context(nc.Block())

        @block.sync
        def _(sp):
            for t in range(NT):
                sp.dma_start(acc[:, t, :], x_tiles[t]).then_inc(sem(f"x_in{t}"), 16)
            for name, row, n in (("mix_pre_norm", V_MIXPRE, KD), ("ffn_pre_norm", V_FFNPRE, KD), ("q_norm", V_QN, 2),
                                 ("kv_norm", V_KVN, 1), ("g_pre_mix_2", V_GPREMIX2, KD),
                                 ("g_pre_mlp_2", V_GPREMLP2, KD)):
                sp.dma_start(vec_rows[row:row + n, :], d[name][0].rearrange("(k p) -> k p", p=P))\
                    .then_inc(sem("vec_in"), 16)
            sp.dma_start(vec_rows[V_CONV:V_CONV + CONV_W * GDN_PANELS, :],
                         d["conv_w"][0].rearrange("w (k p) -> (w k) p", p=P)).then_inc(sem("vec_in"), 16)
            sp.dma_start(vec_rows[V_CONV2:N_VEC, :],
                         d["conv_w_2"][0].rearrange("w (k p) -> (w k) p", p=P)).then_inc(sem("vec_in"), 16)
            sp.dma_start(vec2_rows[0:N_BADA, :], d["b_ada_2"][0].rearrange("(k p) -> k p", p=P))\
                .then_inc(sem("vec_in"), 16)
            sp.dma_start(vec2_rows[N_BADA:N_VEC2, :], d["c_2"][0].rearrange("(k p) -> k p", p=P))\
                .then_inc(sem("vec_in"), 16)
            sp.dma_start(a_log_b[:], d["a_log"][0].partition_broadcast(P)).then_inc(sem("gdn_vec_in"), 16)
            sp.dma_start(dt_b[:], d["dt_bias"][0].partition_broadcast(P)).then_inc(sem("gdn_vec_in"), 16)
            sp.dma_start(out_norm_row[:], d["gdn_out_norm"][0].partition_broadcast(P)).then_inc(sem("gdn_vec_in"), 16)

            for c, (col, n) in enumerate(T_COLS):
                for j in range(4):
                    R1.load(sp, 0, 4 * c + j, half_view(n), w_in[:, 2 * j:2 * j + 2, col:col + n])
            R2.start(sp)
            with sp.Fori(0, GDN_PANELS // 3) as i:
                for j in range(3):
                    R2.load(sp, 3 * i, j, panel_view, w_in[:, :, bass.ds((3 * i + j) * P, P)])
            R2.panel_done(sp, 0, GDN_PANELS - 1)
            sp.dma_start(pos_i[NOPE:DQK, :], d["positions"][0].partition_broadcast(ROPE)).then_inc(sem("pos_in"), 16)
            sp.dma_start(w_kv[:], d["w_kv_up"][0]).then_inc(sem("w_kv_in"), 16)
            w_q_up = d["w_q_up"][0].rearrange("(k p) n -> p k n", p=P)
            with sp.Fori(0, MLA_HEADS) as h:
                c = h * DQK
                parts = ((wq[:], w_q_up[:, :, bass.ds(c, DQK)]),
                         (wq_swap[:, :, 0:ROPE // 2], w_q_up[:, :, bass.ds(c + NOPE + ROPE // 2, ROPE // 2)]),
                         (wq_swap[:, :, ROPE // 2:ROPE], w_q_up[:, :, bass.ds(c + NOPE, ROPE // 2)]),
                         (wk[:], d["w_kv_up"][0][:, bass.ds(h * P, NOPE)]))
                sp.wait_ge(sem("mla_proj_done"), h + 1)
                for dst, src in parts:
                    sp.dma_start(dst, src).then_inc(sem("mla_w_in"), 16)

            sp.wait_ge(sem("gdn_out_done"), NT)
            for t in range(NT):
                sp.dma_start(resid[:, t, :], x_tiles[t]).then_inc(sem(f"x_in{t}"), 16)
            sp.dma_start(post_row[:], d["mix_post_norm"][0].partition_broadcast(P)).then_inc(sem("mix_post_in"), 16)
            R3.start(sp)
            for c in range(2):
                for j in range(4):
                    R3.load(sp, 0, 4 * c + j, half_view(HALF), w_out[:, 2 * j:2 * j + 2, c * HALF:(c + 1) * HALF])

            def ffn_loads(ring, up, down):
                with sp.Fori(0, FFN_STEPS) as i:
                    for j in range(2):
                        ring.load(sp, 4 * i, j, panel_view, up[:, :, bass.ds((2 * i + j) * P, P)])
                    for j in range(2):
                        ring.load(sp, 4 * i, 2 + j, lambda raw: raw[:, :], down[2 * i + j])

            R4.start(sp)
            ffn_loads(R4, w_up, w_down)
            def w2_panel(col, j):
                return w_in2[:, :, bass.ds(col + j * P, P)]

            R5.start(sp)
            sp.wait_ge(sem("ada_used"), N_MOD * KD + 2)
            with sp.Fori(0, CONV2_PANELS) as i:
                for j in range(3):
                    R5.load(sp, 3 * i, j, panel_view, w2_panel(j * CONV2, i))

            def merge_loads(ring, gate_col, proj):
                with sp.Fori(0, KD // 2) as i:
                    for j in range(2):
                        ring.load(sp, 4 * i, 2 * j, panel_view, w2_panel(gate_col, 2 * i + j))
                        ring.load(sp, 4 * i, 2 * j + 1, lambda raw: raw[:, 0:HALF].rearrange("p (k n) -> p k n", n=P),
                                  proj[:, :, bass.ds((2 * i + j) * P, P)])

            R6.start(sp)
            sp.wait_ge(sem("c2_y_done"), CONV2_PANELS + 1)
            merge_loads(R6, IN2_GA, w_pc)
            for j in range(4):
                R7.load(sp, 0, j, half_view(HALF), w_in2[:, 2 * j:2 * j + 2, IN2_V:IN2_V + HALF])
            R8.start(sp)
            with sp.Fori(0, SB_HEADS // 2) as i:
                R8.load(sp, 2 * i, 0, panel_view, w2_panel(IN2_Q, i))
                R8.load(sp, 2 * i, 1, panel_view, w2_panel(IN2_K, i))
            R9.start(sp)
            sp.wait_ge(sem("sb_o_done"), SB_HEADS + 2)
            merge_loads(R9, IN2_GB, w_pa)
            for c in range(2):
                for j in range(4):
                    R10.load(sp, 0, 4 * c + j, half_view(HALF), w_out2[:, 2 * j:2 * j + 2, c * HALF:(c + 1) * HALF])
            ffn_loads(R11, w_up2, w_down2)

            out_tiles = out[0].rearrange("(t p) d -> t p d", p=P)
            for t in range(NT):
                sp.wait_ge(sem("resid_done"), 3 * NT + t + 1)
                sp.dma_start(out_tiles[t], resid[:, t, :]).then_inc(sem("out_stored"), 16)
            sp.wait_ge(sem("out_stored"), NT * 16)

        @block.gpsimd
        def _(pool):
            R1.credit(pool)
            pool.sem_inc(sem("conv_done"), 1)
            pool.sem_inc(sem("conv_in_done"), 2)
            pool.sem_inc(sem("ss_gdn_done"), 2)
            pool.sem_inc(sem("mla_proj_done"), 1)
            pool.sem_inc(sem("mla_o_done"), NT)
            pool.sem_inc(sem("mla_pv"), 2)
            pool.sem_inc(sem("ffn_hid"), FFN_CREDIT)
            for name, credit in (("ada_used", 2), ("ada_read", 1), ("c2_cg_read", 1), ("c2_v_done", 1), ("c2_y_done", 1),
                                 ("m_gate_read", 2), ("m_done", 2), ("sb_z_done", 2), ("sb_o_done", 2), ("sb_pv", 2)):
                pool.sem_inc(sem(name), credit)
            pool.memset(half_neg[:], -0.5).then_inc(sem("minus_half_done"), 1)
            pool.wait_ge(sem("minus_half_done"), 1)

            def norm_rstd(tag):
                b = NORMS.index(tag)
                for h in range(2):
                    pool.wait_ge(sem("norm_sq_done"), NT * b + 4 * h + 4)
                    pool.tensor_scalar(mean_sq[:, 4 * h:4 * h + 4], ssq[:, 4 * h:4 * h + 4], 1.0 / D, EPS,
                                       ALU.mult, ALU.add).then_inc(sem("norm_mean_done"), 1)
                    pool.wait_ge(sem("norm_mean_done"), 2 * b + h + 1)
                    pool.tensor_tensor(rstd[:, 4 * h:4 * h + 4], mean_sq[:, 4 * h:4 * h + 4], half_neg[:, 0:4],
                                       ALU.pow).then_inc(sem("norm_rstd_done"), 1)

            norm_rstd("n1")
            for c, (col, n) in enumerate(T_COLS):
                for j in range(4):
                    R1.split(pool, 0, (4 * c + j) // 4, 4 * c + j, 2 * n)
            R2.start_split(pool)
            with pool.Fori(0, GDN_PANELS // 3) as i:
                for j in range(3):
                    R2.split(pool, 3 * i, i, j)
            pool.wait_ge(sem("lat_sq_done"), 2 * NT)
            pool.tensor_scalar(lat_ms[:, 0:NT], lat_ss[:, 0:NT], 1.0 / Q_RANK, EPS, ALU.mult, ALU.add)\
                .then_inc(sem("lat_ms_done"), 1)
            pool.tensor_scalar(lat_ms[:, NT:], lat_ss[:, NT:], 1.0 / KV_RANK, EPS, ALU.mult, ALU.add)\
                .then_inc(sem("lat_ms_done"), 1)
            pool.wait_ge(sem("lat_ms_done"), 2)
            pool.tensor_tensor(lat_rstd[:], lat_ms[:], half_neg[:, 0:2 * NT], ALU.pow).then_inc(sem("lat_rstd_done"), 1)
            pool.wait_ge(sem("ss_gdn_done"), GDN_PANELS + 2)
            pool.tensor_scalar(g_rq[:], ss_gdn[:, :, 1:1 + GDN_HEADS], float(P), 4 * EPS * P, ALU.mult, ALU.add)\
                .then_inc(sem("qk_ms_done"), 1)
            pool.tensor_scalar(g_rk[:], ss_gdn[:, :, 1 + GDN_HEADS:1 + 2 * GDN_HEADS], 1.0, 4 * EPS, ALU.mult, ALU.add)\
                .then_inc(sem("qk_ms_done"), 1)
            expo = half_neg[:, 0:NT * GDN_HEADS].rearrange("p (t h) -> p t h", h=GDN_HEADS)
            pool.wait_ge(sem("qk_ms_done"), 2)
            pool.tensor_tensor(g_rk[:], g_rk[:], expo, ALU.pow).then_inc(sem("qk_norm_done"), 1)
            pool.tensor_tensor(g_rq[:], g_rq[:], expo, ALU.pow).then_inc(sem("qk_norm_done"), 1)

            with pool.Fori(0, NT) as i:
                pool.wait_ge(sem("o_ss_done"), i + 1)
                pool.sem_inc(sem("o_norm_begun"), 1)
                pool.tensor_scalar(o_ms[:], o_ss[:], 1.0 / P, EPS, ALU.mult, ALU.add).then_inc(sem("o_ms_done"), 1)
                pool.wait_ge(sem("o_ms_done"), i + 1)
                pool.tensor_tensor(o_rstd[:], o_ms[:], half_neg[:, 0:GDN_HEADS], ALU.pow)\
                    .then_inc(sem("o_rstd_done"), 1)

            R3.start_split(pool)
            for j in range(8):
                R3.split(pool, 0, j // 4, j)
            norm_rstd("mix_post")
            norm_rstd("n2")

            def ffn_splits(ring):
                with pool.Fori(0, FFN_STEPS) as i:
                    for j in range(4):
                        ring.split(pool, 4 * i, (4 // ring.nraw) * i + j // ring.nraw, j)

            R4.start_split(pool)
            ffn_splits(R4)
            norm_rstd("ffn_post")
            norm_rstd("n3")
            R5.start_split(pool)
            with pool.Fori(0, CONV2_PANELS) as i:
                for j in range(3):
                    R5.split(pool, 3 * i, i, j)

            def merge_splits(ring):
                with pool.Fori(0, KD // 2) as i:
                    for j in range(4):
                        ring.split(pool, 4 * i, i, j, 1024 if j % 2 == 0 else HALF)

            R6.start_split(pool)
            pool.wait_ge(sem("c2_split"), CONV2_PANELS)
            merge_splits(R6)
            for j in range(4):
                R7.split(pool, 0, 0, j)
            R8.start_split(pool)
            with pool.Fori(0, SB_HEADS // 2) as i:
                for j in range(2):
                    R8.split(pool, 2 * i, i, j)
            R9.start_split(pool)
            pool.wait_ge(sem("sb_o_done"), SB_HEADS + 2)
            merge_splits(R9)
            for j in range(8):
                R10.split(pool, 0, j // 4, j)
            norm_rstd("mix_post2")
            norm_rstd("n4")
            ffn_splits(R11)
            norm_rstd("ffn_post2")

        @block.tensor
        def _(pe):
            def turn(tag, src, ready, nk=KD):
                base = TURNS[tag]
                for h in range(2):
                    for k in range(nk):
                        n = h * nk + k
                        ready(h)
                        if n >= 4:
                            pe.wait_ge(sem("turn_read"), base + n - 3)
                        for j in range(4):
                            mm = pe.transpose(ps[:, n % 4, j * P:(j + 1) * P],
                                              src[:, 4 * h + j, k * P:(k + 1) * P], ident)
                        mm.then_inc(sem("turned"), 1)

            def scaled(tag, t):
                pe.wait_ge(sem("norm_scaled"), NT * SCALES.index(tag) + t + 1)

            def turn_done(tag, nk=KD):
                base = TURNS[tag]
                pe.wait_ge(sem("turn_read"), base + 2 * nk)
                pe.wait_ge(sem("turn_split"), base + 2 * nk)

            def panel(hi, lo, a_hi, a_lo, banks, nk, done, halves=(0, 1)):
                for h in halves:
                    o = ps[:, banks[h], :]
                    cols = slice(h * HALF, (h + 1) * HALF)
                    for k in range(nk):
                        w = slice(k * P, (k + 1) * P)
                        pe.matmul(o, hi[:, w], a_hi[:, k, cols], start=(k == 0), stop=False)
                        pe.matmul(o, hi[:, w], a_lo[:, k, cols], start=False, stop=False)
                        mm = pe.matmul(o, lo[:, w], a_hi[:, k, cols], start=False, stop=(k == nk - 1))
                    if done[h]:
                        mm.then_inc(done[h], 1)

            def token_chunk(ring, n0, width, a_hi, a_lo, bank_free, done):
                for j in range(4):
                    ring.ready(pe, 0, n0 + j)
                    hi, lo = ring.hi[(n0 + j) % ring.nslab], ring.lo[(n0 + j) % ring.nslab]
                    for t in range(NT):
                        o = ps[:, t, 0:width]
                        if j == 0:
                            bank_free(t)
                        for m in range(2):
                            k = 2 * j + m
                            w = slice(m * width, (m + 1) * width)
                            a = slice(t * P, (t + 1) * P)
                            pe.matmul(o, a_hi[:, k, a], hi[:, w], start=(k == 0), stop=False)
                            pe.matmul(o, a_lo[:, k, a], hi[:, w], start=False, stop=False)
                            mm = pe.matmul(o, a_hi[:, k, a], lo[:, w], start=False, stop=(k == KD - 1))
                        if t == NT - 1:
                            mm.then_inc(ring.used, 1)
                        elif j == 3:
                            mm.then_inc(done, 1)

            pe.wait_ge(sem("consts_in"), 16)
            pe.wait_ge(sem("vec_in"), 160)
            pe.transpose(ps[:, 4, 0:N_VEC], vec_rows[0:N_VEC, :], consts[0:N_VEC, C_ID:C_ID + N_VEC])
            pe.transpose(ps[:, 4, 256:256 + N_VEC2], vec2_rows[0:N_VEC2, :], consts[0:N_VEC2, C_ID:C_ID + N_VEC2])\
                .then_inc(sem("vec_turned"), 1)
            turn("n1", acc, lambda h: scaled("n1", 4 * h + 3))
            turn_done("n1")
            pe.wait_ge(sem("vec_cols_done"), 2)
            token_chunk(R1, 0, HALF, act_hi, act_lo, lambda t: None, sem("gate_prod"))
            token_chunk(R1, 4, TAIL_W, act_hi, act_lo, lambda t: pe.wait_ge(sem("gate_silu"), t + 1), sem("tail_prod"))
            pe.wait_ge(sem("lat_done"), NT)
            with pe.Fori(0, GDN_PANELS // 3) as i:
                for j in range(3):
                    p = 3 * i + j
                    R2.ready(pe, 3 * i, j)
                    pe.wait_ge(sem("conv_in_done"), p + 1)
                    b = 2 * j
                    panel(R2.hi[j], R2.lo[j], act_hi, act_lo, (b, b + 1), KD, (sem("qkv_half"), R2.used))
                    pe.wait_ge(sem("conv_sq_done"), p + 1)
                    pe.wait_ge(sem("ss_gdn_done"), p + 2)
                    for t in range(NT):
                        mm = pe.matmul(ps[:, 6, t:t + 1], conv_t[:, t * P:(t + 1) * P], ones[:, 0:1],
                                       start=True, stop=True)
                    mm.then_inc(sem("ss_prod"), 1)
            pe.wait_ge(sem("lat_norm_done"), 1)
            pe.wait_ge(sem("conv_in_done"), GDN_PANELS + 2)
            for n in range(10):
                kind, h = n // 2, n % 2
                c0, w = ((0, P), (P, P), (2 * P, P), (LAT_KR - LAT_CQ - NOPE, DQK), (LAT_KR - LAT_CQ - NOPE + ROPE, DQK))[kind]
                if n == 6:
                    pe.wait_ge(sem("ss_gdn_done"), GDN_PANELS + 2)
                if n >= 8:
                    pe.wait_ge(sem("lat_feat_done"), n - 7)
                for j in range(4):
                    mm = pe.transpose(ps[0:w, n % 8, j * P:(j + 1) * P], lat_n[:, 4 * h + j, c0:c0 + w], ident)
                mm.then_inc(sem("lat_turned"), 1)
            pe.wait_ge(sem("w_kv_in"), 16)
            pe.wait_ge(sem("lat_feat_done"), 6)
            pe.wait_ge(sem("k_rope_done"), 1)
            w_v = w_kv[:].rearrange("p (h c) -> p h c", c=P)[:, :, NOPE:P]
            for t in range(NT):
                pe.matmul(ps[:, t, :].rearrange("p (h e) -> p h e", e=V_DIM), ckv_f[:, t * P:(t + 1) * P], w_v,
                          start=True, stop=True).then_inc(sem("v_prod"), 1)
            pe.wait_ge(sem("log_a_done"), 1)
            pe.wait_ge(sem("v_done"), NT)
            n_gh = NT * GDN_HEADS
            la = g_la[:].rearrange("p t h -> p (t h)")
            pe.matmul(ps[:, 0, 0:n_gh], consts[:, C_CSUM:C_CSUM + P], la, start=True, stop=True)
            pe.matmul(ps[:, 0, n_gh:2 * n_gh], consts[:, C_CHUNK:C_CHUNK + P], la, start=True, stop=True)\
                .then_inc(sem("cumsum_prod"), 1)
            pe.wait_ge(sem("cumsum_done"), 2)

            with pe.Fori(0, MLA_HEADS) as h:
                pe.wait_ge(sem("mla_w_in"), 64 * h + 64)
                pe.wait_ge(sem("mla_o_done"), NT * h + NT)
                for f in range(2):
                    cols = slice(f * HALF, (f + 1) * HALF)
                    for k in range(2):
                        pe.matmul(ps[0:DQK, f, :], wq[:, k, :], cq_f[:, k, cols], start=(k == 0), stop=(k == 1))
                    for k in range(2):
                        mm = pe.matmul(ps[NOPE:DQK, 2 + f, :], wq_swap[:, k, :], cq_f[:, k, cols],
                                       start=(k == 0), stop=(k == 1))
                mm.then_inc(sem("mla_q_prod"), 1)
                for f in range(2):
                    mm = pe.matmul(ps[0:NOPE, 4 + f, :], wk[:], ckv_f[:, f * HALF:(f + 1) * HALF],
                                   start=True, stop=True)
                mm.then_inc(sem("mla_proj_done"), 1)
                pe.wait_ge(sem("mla_qk_done"), 2 * h + 2)
                pe.wait_ge(sem("mla_rope_done"), h + 1)

                def scores(t):
                    n = (t + 1) * P
                    for f in range((n + HALF - 1) // HALF):
                        w = min(HALF, n - f * HALF)
                        mm = pe.matmul(ps[:, 2 * (t % 2) + f, 0:w], q_f[0:DQK, t * P:(t + 1) * P],
                                       k_f[0:DQK, f * HALF:f * HALF + w], start=True, stop=True)
                    mm.then_inc(sem("mla_scores"), 1)

                scores(0)
                scores(1)
                g0 = 0
                for t in range(NT):
                    blocks = list(range(t + 1))
                    groups = [blocks[0:4], blocks[4:8]] if t >= 4 else [blocks]
                    pe.wait_ge(sem("mla_exp_done"), NT * h + t + 1)
                    for n, g in enumerate(groups):
                        for b in g:
                            mm = pe.transpose(ps[:, 4 + (g0 + n) % 2, (b % 4) * P:(b % 4 + 1) * P],
                                              probs[t % 2][:, b * P:(b + 1) * P], ident)
                        mm.then_inc(sem("mla_turned"), 1)
                    if t + 2 < NT:
                        scores(t + 2)
                    for n, g in enumerate(groups):
                        pe.wait_ge(sem("mla_pt_done"), MLA_GROUPS * h + g0 + n + 1)
                        if n == 0:
                            pe.wait_ge(sem("mla_o_done"), NT * h + NT + t - 1)
                        for b in g:
                            mm = pe.matmul(ps[:, 6 + t % 2, 0:V_DIM], probs_t[(g0 + n) % 2][:, (b % 4) * P:(b % 4 + 1) * P],
                                           v_t[:, b, h, :], start=(b == 0), stop=(b == t))
                        mm.then_inc(sem("mla_pv"), 1)
                    g0 += len(groups)
                assert g0 == MLA_GROUPS

            def heads(bank, lhs, rhs, signal=None):
                for h in range(GDN_HEADS):
                    mm = pe.matmul(ps[:, bank, h * P:(h + 1) * P], lhs(h), rhs(h), start=True, stop=True)
                if signal:
                    mm.then_inc(sem(signal), 1)

            def turn_heads(bank, src, signal):
                for h in range(GDN_HEADS):
                    mm = pe.transpose(ps[:, bank, h * P:(h + 1) * P], src[:, h, :], ident)
                mm.then_inc(sem(signal), 1)

            pe.wait_ge(sem("mla_o_done"), NT * MLA_HEADS + NT)
            pe.wait_ge(sem("state0_done"), 1)
            with pe.Fori(0, NT) as i:
                pe.wait_ge(sem("gdn_tile_in"), i + 1)
                pe.matmul(ps[:, 0, :], ones, u_g[:].rearrange("p h t -> p (h t)"), start=True, stop=True)\
                    .then_inc(sem("g_row_prod"), 1)
                pe.matmul(ps[:, 1, :], ones, i_b[:].rearrange("p h t -> p (h t)"), start=True, stop=True)
                heads(2, lambda h: k_s[:, h, :], lambda h: k_s[:, h, :])
                heads(3, lambda h: k_s[:, h, :], lambda h: q_s[:, h, :], "kk_prod")
                turn_heads(4, k_s, "kv_turned")
                turn_heads(5, v_s, "kv_turned")
                pe.wait_ge(sem("tr0_done"), i + 1)
                turn_heads(6, t_r[0], "t0_turned")
                for n in range(1, len(LEVELS)):
                    a = (n - 1) % 2
                    pe.wait_ge(sem("a_levels_done"), i + 1)
                    if n == 1:
                        pe.wait_ge(sem("t0_done"), i + 1)
                    else:
                        pe.wait_ge(sem("t_done"), 4 * i + n - 1)
                    heads(7, lambda h: m_s[n][:, h, :], lambda h: t_f[a][:, h, :], "y_prod")
                    pe.wait_ge(sem("y_done"), 5 * i + n)
                    heads(6, lambda h: y_s[:, h, :], lambda h: t_r[a][:, h, :], "zt_prod")
                    if n < len(LEVELS) - 1:
                        heads(0, lambda h: t_r[a][:, h, :], lambda h: y_s[:, h, :], "z_prod")
                pe.wait_ge(sem("kvw_done"), i + 1)
                pe.wait_ge(sem("t_last_done"), i + 1)
                heads(1, lambda h: k_w[:, h, :], lambda h: t_r[1][:, h, :], "wu_prod")
                heads(2, lambda h: t_r[1][:, h, :], lambda h: v_b[:, h, :], "wu_prod")
                pe.wait_ge(sem("wu_done"), 2 * i + 2)
                for c in range(2):
                    rows = slice(c * CHUNK, (c + 1) * CHUNK)
                    s_in = state[c]
                    if c == 1:
                        pe.wait_ge(sem("state_done"), 2 * i + 1)
                    for h in range(GDN_HEADS):
                        mm = pe.matmul(ps[rows, 3, h * P:(h + 1) * P], w_t[:, h, rows], s_in[:, h, :],
                                       start=True, stop=True)
                    mm.then_inc(sem("ws_prod"), 1)
                    pe.wait_ge(sem("v_new_done"), 2 * i + c + 1)
                    for h in range(GDN_HEADS):
                        mm = pe.matmul(ps[:, 5, h * P:(h + 1) * P], k_d[rows, h, :], v_n[rows, h, :],
                                       start=True, stop=True)
                    mm.then_inc(sem("ds_prod"), 1)
                    for h in range(GDN_HEADS):
                        o = ps[rows, 4, h * P:(h + 1) * P]
                        pe.matmul(o, q_d[:, h, rows], s_in[:, h, :], start=True, stop=False)
                        mm = pe.matmul(o, p_t[rows, h, rows], v_n[rows, h, :], start=False, stop=True)
                mm.then_inc(sem("o_prod"), 1)

            turn("mixt", mix, lambda h: pe.wait_ge(sem("gdn_out_done"), NT))
            turn_done("mixt")
            token_chunk(R3, 0, HALF, mixt_hi, mixt_lo, lambda t: None, sem("mixed_prod"))
            token_chunk(R3, 4, HALF, mixt_hi, mixt_lo, lambda t: pe.wait_ge(sem("mixed_done"), t + 1), sem("mixed_prod"))

            def ffn(ring, run):
                with pe.Fori(0, FFN_STEPS) as i:
                    for j in range(2):
                        ring.ready(pe, 4 * i, j)
                        if j == 0 and run == 0:
                            pe.wait_ge(sem("ada_read"), i + 1)
                        panel(ring.hi[j], ring.lo[j], act_hi, act_lo, (2 * j, 2 * j + 1), KD,
                              (sem("ffn_half"), ring.used))

                    def down(g, j, stop):
                        t, f = g // 2, g % 2
                        o, a, c = ps[:, 4 + g % 4, :], slice(t * P, (t + 1) * P), slice(f * HALF, (f + 1) * HALF)
                        pe.matmul(o, hid_hi[:, j, a], ring.hi[2 + j][:, c], start=(j == 0), stop=False)
                        pe.matmul(o, hid_lo[:, j, a], ring.hi[2 + j][:, c], start=False, stop=False)
                        return pe.matmul(o, hid_hi[:, j, a], ring.lo[2 + j][:, c], start=False, stop=stop)

                    ring.ready(pe, 4 * i, 2)
                    pe.wait_ge(sem("ffn_hid"), 4 * i + (4 * FFN_STEPS * run + 2 + FFN_CREDIT))
                    for g in range(4):
                        pe.wait_ge(sem("ffn_acc"), 16 * i + ((16 * FFN_STEPS + 4) * run + g + 1))
                        down(g, 0, False)
                    ring.ready(pe, 4 * i, 3)
                    pe.wait_ge(sem("ffn_hid"), 4 * i + (4 * FFN_STEPS * run + 4 + FFN_CREDIT))
                    def modulation(j):
                        pe.wait_ge(sem(f"ada_in{j % 2}"), (32 if j % 2 == 0 else 16) * i + (j // 2 + 1) * 16)
                        for k in range(KD):
                            mm = pe.matmul(ps[:, 0, j:j + 1], ada[j % 2][:, k, :], vec2[:, N_BADA + k:N_BADA + k + 1],
                                           start=(k == 0), stop=(k == KD - 1))
                        mm.then_inc(sem("ada_used"), 1)

                    if run == 0:
                        modulation(0)
                        modulation(1)
                    for g in range(16):
                        if g == 12 and run == 0:
                            modulation(2)
                        if g >= 4:
                            pe.wait_ge(sem("ffn_acc"), 16 * i + ((16 * FFN_STEPS + 4) * run + g + 1))
                            mm = down(g, 0, False)
                            if g == 15:
                                mm.then_inc(ring.used, 1)
                        mm = down(g, 1, True)
                        mm.then_inc(ring.used if g == 15 else sem("ffn_down"), 1)

            turn("n2", acc, lambda h: scaled("n2", 4 * h + 3))
            turn_done("n2")
            ffn(R4, 0)
            turn("n3", acc, lambda h: scaled("n3", 4 * h + 3))
            turn_done("n3")
            with pe.Fori(0, CONV2_PANELS) as i:
                for j, free in enumerate(("c2_y_done", "c2_cg_read", "c2_v_done")):
                    R5.ready(pe, 3 * i, j)
                    pe.wait_ge(sem(free), i + 1)
                    panel(R5.hi[j], R5.lo[j], act_hi, act_lo, (2 * j, 2 * j + 1), KD, (None, R5.used))

            def merge(ring, run, a_hi, a_lo, ready):
                with pe.Fori(0, KD // 2) as i:
                    for j in range(2):
                        b = 4 * j
                        ring.ready(pe, 4 * i, 2 * j)
                        pe.wait_ge(sem("m_gate_read"), 2 * i + (KD * run + j + 1))
                        panel(ring.hi[2 * j], ring.lo[2 * j], act_hi, act_lo, (b, b + 1), KD, (None, ring.used))
                        ring.ready(pe, 4 * i, 2 * j + 1)
                        if j == 0:
                            ready()
                        pe.wait_ge(sem("m_done"), 2 * i + (KD * run + j + 1))
                        panel(ring.hi[2 * j + 1], ring.lo[2 * j + 1], a_hi, a_lo, (b + 2, b + 3), CONV2_PANELS,
                              (None, ring.used))

            merge(R6, 0, y_hi, y_lo, lambda: pe.wait_ge(sem("c2_split"), CONV2_PANELS))
            pe.wait_ge(sem("m_done"), KD + 2)
            token_chunk(R7, 0, HALF, act_hi, act_lo, lambda t: None, sem("v2_prod"))
            pe.wait_ge(sem("v2_done"), NT)

            def sb_project(i, j, halves=(0, 1)):
                if halves[0] == 0:
                    R8.ready(pe, 2 * i, j)
                panel(R8.hi[j], R8.lo[j], act_hi, act_lo, (2 * j, 2 * j + 1), KD, (None, R8.used), halves)

            def sb_scores(i, s):
                t, rows = s // 2, slice(s % 2 * SB_DIM, (s % 2 + 1) * SB_DIM)
                n = (t + 1) * P
                pe.wait_ge(sem("sb_z_done"), SB_ITEMS * i + s + 1)
                for f in range((n + HALF - 1) // HALF):
                    w = min(HALF, n - f * HALF)
                    mm = pe.matmul(ps[:, 2 * (s % 2) + f, 0:w], q2[rows, t * P:(t + 1) * P],
                                   k2[rows, f * HALF:f * HALF + w], start=True, stop=True)
                mm.then_inc(sem("sb_scores"), 1)

            def sb_turn(i, s):
                pe.wait_ge(sem("sb_weights_done"), SB_ITEMS * i + s + 1)
                for n, g in enumerate(sb_groups(s)):
                    for b in range(4 * n, min(4 * n + 4, s // 2 + 1)):
                        mm = pe.transpose(ps[:, 4 + g % 2, (b % 4) * P:(b % 4 + 1) * P],
                                          sb_a[s % 3][:, b * P:(b + 1) * P], ident)
                    mm.then_inc(sem("sb_turned"), 1)

            def sb_outputs(i, s):
                t, half = s // 2, s // NT
                if s % NT == 0:
                    pe.wait_ge(sem("sb_o_done"), 2 * i + half + 1)
                for n, g in enumerate(sb_groups(s)):
                    pe.wait_ge(sem("sb_at_done"), SB_GROUPS * i + g + 1)
                    for b in range(4 * n, min(4 * n + 4, t + 1)):
                        mm = pe.matmul(ps[:, 6 + half, s % NT * SB_DIM:(s % NT + 1) * SB_DIM],
                                       sb_at[g % 2][:, (b % 4) * P:(b % 4 + 1) * P], v2[:, b, 2 * i + s % 2, :],
                                       start=(b == 0), stop=(b == t))
                    mm.then_inc(sem("sb_pv"), 1)

            def sb_pair(i, last):
                pe.wait_ge(sem("sb_qk_done"), 2 * i + 2)
                sb_scores(i, 0)
                for s in range(SB_ITEMS + SB_LAG_PV):
                    if s + 1 < SB_ITEMS:
                        sb_scores(i, s + 1)
                    if s >= SB_ITEMS and not last:
                        if s == SB_ITEMS:
                            pe.wait_ge(sem("sb_z_done"), SB_ITEMS * i + SB_ITEMS + 2)
                        sb_project(i + 1, (s - SB_ITEMS) // 2, ((s - SB_ITEMS) % 2,))
                    if s >= SB_LAG_PV:
                        sb_outputs(i, s - SB_LAG_PV)
                    if SB_LAG_TURN <= s < SB_ITEMS + SB_LAG_TURN:
                        sb_turn(i, s - SB_LAG_TURN)

            sb_project(0, 0)
            sb_project(0, 1)
            with pe.Fori(0, SB_PAIRS - 1) as i:
                sb_pair(i, False)
            sb_pair(SB_PAIRS - 1, True)

            turn("sb_o", o2, lambda h: pe.wait_ge(sem("sb_o_done"), SB_HEADS + 2), CONV2_PANELS)
            turn_done("sb_o", CONV2_PANELS)
            merge(R9, 1, o2_hi, o2_lo, lambda: None)

            pe.wait_ge(sem("merged_split"), KD)
            token_chunk(R10, 0, HALF, act_hi, act_lo, lambda t: None, sem("mixed_prod"))
            token_chunk(R10, 4, HALF, act_hi, act_lo, lambda t: pe.wait_ge(sem("mixed_done"), 2 * NT + t + 1),
                        sem("mixed_prod"))

            def gate_row(run):
                pe.wait_ge(sem("gate_diag_done"), run + 1)
                for f in range(2):
                    mm = pe.matmul(ps[:, f, :], ones, diag[:, 4 * f:4 * f + 4, :].rearrange("p k n -> p (k n)"),
                                   start=True, stop=True)
                mm.then_inc(sem("gate_row_prod"), 1)

            pe.wait_ge(sem("mixed_done"), 4 * NT)
            gate_row(0)
            turn("n4", acc, lambda h: scaled("n4", 4 * h + 3))
            turn_done("n4")
            ffn(R11, 1)
            gate_row(1)

        @block.scalar
        def _(act):
            act.dma_start(consts[:], d["consts"]).then_inc(sem("consts_in"), 16)

            def norm_square(src, junk, ready):
                for t in range(NT):
                    ready(t)
                    act.activation(junk[:, t, :], src[:, t, :], ACT.Square, accum_out=ssq[:, t:t + 1])\
                        .then_inc(sem("norm_sq_done"), 1)

            def norm_scale(tag, src, dst):
                for t in range(NT):
                    act.wait_ge(sem("norm_rstd_done"), 2 * NORMS.index(tag) + t // 4 + 1)
                    act.activation(dst[:, t, :], src[:, t, :], ACT.Copy, scale=rstd[:, t:t + 1])\
                        .then_inc(sem("norm_scaled"), 1)

            def norm_full(tag, scale=None, bias=None, nk=KD):
                base = TURNS[tag]
                for n in range(2 * nk):
                    k = n % nk
                    act.wait_ge(sem("turned"), base + n + 1)
                    if base + n >= 2:
                        act.wait_ge(sem("turn_split"), base + n - 1)
                    if bias:
                        ins = act.activation(norm_tmp[n % 2][:], ps[:, n % 4, :], ACT.Identity, bias=bias(k),
                                             scale=scale(k))
                    elif scale:
                        ins = act.activation(norm_tmp[n % 2][:], ps[:, n % 4, :], ACT.Copy, scale=scale(k))
                    else:
                        ins = act.copy(norm_tmp[n % 2][:], ps[:, n % 4, :])
                    ins.then_inc(sem("turn_read"), 1)

            norm_square(acc, resid, lambda t: act.wait_ge(sem(f"x_in{t}"), 16))
            act.wait_ge(sem("vec_turned"), 1)
            act.copy(vec[:], ps[:, 4, 0:N_VEC]).then_inc(sem("vec_cols_done"), 1)
            act.copy(vec2[:], ps[:, 4, 256:256 + N_VEC2]).then_inc(sem("vec_cols_done"), 1)
            norm_scale("n1", acc, acc)
            act.wait_ge(sem("vec_cols_done"), 2)
            norm_full("n1", lambda k: vec[:, V_MIXPRE + k:V_MIXPRE + k + 1])

            for t in range(NT):
                if t < NT - 1:
                    act.wait_ge(sem("gate_prod"), t + 1)
                else:
                    R1.panel_done(act, 0, 3)
                if t >= 2:
                    act.wait_ge(sem("gate_silu"), t - 1)
                act.activation(gate_tanh[t % 2][:], ps[:, t, :], ACT.Tanh, scale=0.5).then_inc(sem("gate_tanh_done"), 1)
            for t in range(NT):
                if t < NT - 1:
                    act.wait_ge(sem("tail_prod"), t + 1)
                else:
                    R1.panel_done(act, 0, 7)
                act.copy(lat[:, t, :], ps[:, t, 0:TAIL_W]).then_inc(sem("lat_done"), 1)

            with act.Fori(0, GDN_PANELS // 3) as i:
                for j in range(3):
                    p = 3 * i + j
                    b = 2 * j
                    act.wait_ge(sem("qkv_half"), p + 1)
                    act.wait_ge(sem("conv_done"), p + 1)
                    act.copy(xpad[:, CONV_W - 1:CONV_W - 1 + HALF], ps[:, b, :])
                    R2.panel_done(act, 3 * i, j)
                    act.copy(xpad[:, CONV_W - 1 + HALF:], ps[:, b + 1, :]).then_inc(sem("conv_in_done"), 1)
                    act.wait_ge(sem("conv_done"), p + 2)
                    act.wait_ge(sem("ss_prod"), p + 1)
                    act.activation(conv_t[:], conv_y[:], ACT.Tanh, scale=0.5).then_inc(sem("conv_tanh_done"), 1)
                    act.wait_ge(sem("conv_silu_done"), p + 1)
                    act.activation(conv_t[:], qkv[:, p, :], ACT.Square)\
                        .then_inc(sem("conv_sq_done"), 1)
            for t in range(NT):
                act.activation(lat_junk[:, t, 0:Q_RANK], lat[:, t, LAT_CQ:LAT_CKV], ACT.Square,
                               accum_out=lat_ss[:, t:t + 1]).then_inc(sem("lat_sq_done"), 1)
                act.activation(lat_junk[:, t, Q_RANK:], lat[:, t, LAT_CKV:LAT_KR], ACT.Square,
                               accum_out=lat_ss[:, NT + t:NT + t + 1]).then_inc(sem("lat_sq_done"), 1)
            for n, t_ in enumerate((cos_f, sin_f)):
                act.wait_ge(sem("rope_arg_done"), n + 1)
                act.activation(t_[NOPE:DQK, :], t_[NOPE:DQK, :], ACT.Sin).then_inc(sem("rope_trig_done"), 1)
            act.wait_ge(sem("g_min_done"), 1)
            act.activation(g_exp[:], g_la[:], ACT.Exp).then_inc(sem("g_exp_done"), 1)
            act.activation(ea_b[:], a_log_b[:], ACT.Exp).then_inc(sem("g_exp_done"), 1)
            act.activation(g_beta[:], lat[:, :, GDN_HEADS:2 * GDN_HEADS], ACT.Tanh, scale=0.5)\
                .then_inc(sem("g_exp_done"), 1)
            act.wait_ge(sem("g_exp_done"), 1)
            act.activation(g_sp[:], g_exp[:], ACT.Ln, bias=1.0).then_inc(sem("g_exp_done"), 1)
            for n in range(6):
                kind, h = n // 2, n % 2
                dst = (cq_f[:, 0, :], cq_f[:, 1, :], ckv_f[:])[kind][:, h * HALF:(h + 1) * HALF]
                gain = V_QN + kind if kind < 2 else V_KVN
                act.wait_ge(sem("lat_turned"), n + 1)
                act.activation(dst, ps[:, n, :], ACT.Copy, scale=vec[:, gain:gain + 1]).then_inc(sem("lat_feat_done"), 1)
            for t in range(NT):
                act.wait_ge(sem("v_prod"), t + 1)
                act.copy(v_t[:, t, :, :].rearrange("p h e -> p (h e)"), ps[:, t, :]).then_inc(sem("v_done"), 1)
            act.wait_ge(sem("cumsum_prod"), 1)
            n_gh = NT * GDN_HEADS
            act.copy(g_cum[:].rearrange("p t h -> p (t h)"), ps[:, 0, 0:n_gh]).then_inc(sem("cumsum_done"), 1)
            act.copy(g_tot[:].rearrange("p t h -> p (t h)"), ps[:, 0, n_gh:2 * n_gh]).then_inc(sem("cumsum_done"), 1)
            act.wait_ge(sem("cumsum_done"), 2)
            act.activation(g_eg[:], g_cum[:], ACT.Exp).then_inc(sem("g_exps_done"), 1)
            act.wait_ge(sem("g_tail_done"), 1)
            act.activation(g_ekd[:], g_ekd[:], ACT.Exp).then_inc(sem("g_exps_done"), 1)

            scale = float(DQK) ** -0.5
            with act.Fori(0, MLA_HEADS) as h:
                act.wait_ge(sem("mla_proj_done"), h + 2)
                act.copy(q_f[0:NOPE, :], ps[0:NOPE, 0:2, :].rearrange("p b n -> p (b n)")).then_inc(sem("mla_qk_done"), 1)
                act.copy(k_f[0:NOPE, :], ps[0:NOPE, 4:6, :].rearrange("p b n -> p (b n)")).then_inc(sem("mla_qk_done"), 1)
                for t in range(NT):
                    n = (t + 1) * P
                    act.wait_ge(sem("mla_max_done"), NT * h + t + 1)
                    if t >= 2:
                        act.wait_ge(sem("mla_turned"), MLA_GROUPS * h + MLA_GROUPS_BY[t - 2])
                    s = ps[:, 2 * (t % 2):2 * (t % 2) + 2, :].rearrange("p b n -> p (b n)")[:, 0:n]
                    act.activation(probs[t % 2][:, 0:n], s, ACT.Exp, bias=sm_neg[:, t:t + 1], scale=scale,
                                   accum_out=sm_sum[:, t:t + 1]).then_inc(sem("mla_exp_done"), 1)

            with act.Fori(0, NT) as i:
                act.wait_ge(sem("g_row_prod"), i + 1)
                act.activation(e_g[:].rearrange("p h t -> p (h t)"), ps[:, 0, :], ACT.Exp).then_inc(sem("e_g_done"), 1)
                act.wait_ge(sem("decay_arg_done"), i + 1)
                act.activation(e_d[:], e_d[:], ACT.Exp).then_inc(sem("decay_done"), 1)
                act.wait_ge(sem("t0_turned"), i + 1)
                act.copy(t_f[0][:].rearrange("p h t -> p (h t)"), ps[:, 6, :]).then_inc(sem("t0_done"), 1)
                for n in range(1, len(LEVELS)):
                    act.wait_ge(sem("y_prod"), 5 * i + n)
                    act.copy(y_s[:].rearrange("p h t -> p (h t)"), ps[:, 7, :]).then_inc(sem("y_done"), 1)
                act.wait_ge(sem("wu_prod"), 2 * i + 1)
                act.copy(w_t[:].rearrange("p h t -> p (h t)"), ps[:, 1, :]).then_inc(sem("wu_done"), 1)
                act.wait_ge(sem("wu_prod"), 2 * i + 2)
                act.copy(u_s[:].rearrange("p h t -> p (h t)"), ps[:, 2, :]).then_inc(sem("wu_done"), 1)

            norm_full("mixt")
            for c in range(2):
                for t in range(NT):
                    if t < NT - 1:
                        act.wait_ge(sem("mixed_prod"), 7 * c + t + 1)
                    else:
                        R3.panel_done(act, 0, 4 * c + 3)
                    act.copy(mixed[:, t, c * HALF:(c + 1) * HALF], ps[:, t, :]).then_inc(sem("mixed_done"), 1)
            act.wait_ge(sem("mixed_done"), 2 * NT)
            norm_square(mixed, act_lo_junk, lambda t: None)
            norm_square(resid, acc, lambda t: act.wait_ge(sem("resid_done"), t + 1))
            norm_scale("n2", resid, acc)
            norm_full("n2", lambda k: vec[:, V_FFNPRE + k:V_FFNPRE + k + 1])

            def ffn_relu(ring, run):
                def ada_load(i, j):
                    slab = w_ada[:, :, bass.ds((ADA_STEP * i + j) * P, P)]
                    act.wait_ge(sem("ada_used"), ADA_STEP * i + (2, 1, 3)[j])
                    act.dma_start(ada[j % 2][:], slab).then_inc(sem(f"ada_in{j % 2}"), 16)

                with act.Fori(0, FFN_STEPS) as i:
                    if run == 0:
                        ada_load(i, 0)
                        ada_load(i, 1)
                    for q in range(4):
                        j, f = q // 2, q % 2
                        if f == 0:
                            act.wait_ge(sem("ffn_half"), 2 * i + (2 * FFN_STEPS * run + j + 1))
                        else:
                            ring.panel_done(act, 4 * i, j)
                        act.wait_ge(sem("ffn_hid"), 4 * i + (4 * FFN_STEPS * run + q - 1 + FFN_CREDIT))
                        act.activation(relu_t[q % 2][:], ps[:, q, :], ACT.Relu).then_inc(sem("ffn_relu"), 1)
                        act.wait_ge(sem("ffn_relu"), 4 * i + (4 * FFN_STEPS * run + q + 1))
                        act.activation(hid_hi[:, j, f * HALF:(f + 1) * HALF], relu_t[q % 2][:], ACT.Square)\
                            .then_inc(sem("ffn_hid_hi"), 1)
                    if run == 0:
                        ada_load(i, 2)
                        act.wait_ge(sem("ada_used"), ADA_STEP * i + ADA_STEP + 2)
                        act.copy(mod[:, bass.ds(ADA_STEP * i, ADA_STEP)], ps[:, 0, 0:ADA_STEP]).then_inc(sem("ada_read"), 1)

            ffn_relu(R4, 0)
            act.wait_ge(sem("ffn_acc"), 16 * FFN_STEPS + 4)
            act.dma_start(post_row[:], d["ffn_post_norm"][0].partition_broadcast(P)).then_inc(sem("ffn_post_in"), 16)
            norm_square(acc, act_hi_junk, lambda t: None)
            def spill(t):
                act.wait_ge(sem("resid_done"), NT + t + 1)
                act.dma_start(x1_spill[t], resid[:, t, :]).then_inc(sem("x1_stored"), 16)

            norm_square(resid, acc, spill)
            norm_scale("n3", resid, acc)
            act.wait_ge(sem("mod_scales_done"), 1)
            norm_full("n3", lambda k: scale2[:, k:k + 1], lambda k: mod[:, k:k + 1])

            with act.Fori(0, CONV2_PANELS) as i:
                R5.panel_done(act, 3 * i, 1)
                act.wait_ge(sem("c2_v_done"), i + 1)
                act.copy(cg_t[:], ps[:, 2:4, :].rearrange("p b n -> p (b n)")).then_inc(sem("c2_cg_read"), 1)
                act.wait_ge(sem("c2_y_done"), i + 2)
                act.copy(y_hi[:, i, :], conv2_y[:]).then_inc(sem("c2_hi_done"), 1)

            def merge_gates(ring, run, gates):
                with act.Fori(0, KD // 2) as i:
                    for j in range(2):
                        ring.panel_done(act, 4 * i, 2 * j)
                        act.wait_ge(sem("m_done"), 2 * i + (KD * run + j + 1))
                        act.activation(gates[j][:], ps[:, 4 * j:4 * j + 2, :].rearrange("p b n -> p (b n)"), ACT.Tanh,
                                       scale=0.5).then_inc(sem("m_gate_read"), 1)

            merge_gates(R6, 0, conv_gate)
            for t in range(NT):
                if t < NT - 1:
                    act.wait_ge(sem("v2_prod"), t + 1)
                else:
                    R7.panel_done(act, 0, 3)
                act.copy(v2[:, t, :, :].rearrange("p h e -> p (h e)"), ps[:, t, :]).then_inc(sem("v2_done"), 1)

            act.preload_act_table_set("natural_log_exp_and_others")

            def sb_copy_qk(i):
                for j, dst in enumerate((q2, k2)):
                    R8.panel_done(act, 2 * i, j)
                    act.copy(dst[:], ps[:, 2 * j:2 * j + 2, :].rearrange("p b n -> p (b n)")).then_inc(sem("sb_qk_done"), 1)

            ach = Chain(act, sem("act_chain"))

            def sb_pair(i):
                for s in range(SB_ITEMS + SB_LAG_EXP):
                    if s >= SB_LAG_EXP:
                        u = s - SB_LAG_EXP
                        a = sb_a[u % 3][:, 0:(u // 2 + 1) * P]
                        act.wait_ge(sem("sb_arg_done"), SB_ITEMS * i + u + 1)
                        act.activation(a, a, ACT.Exp).then_inc(sem("sb_weights_done"), 1)
                    if s < SB_ITEMS:
                        n = (s // 2 + 1) * P
                        l = sb_sp[s % 2][:, 0:n]
                        act.wait_ge(sem("sb_z_done"), SB_ITEMS * i + s + 3)
                        ach.link(act.activation(l, sb_z[s % 2][:, 0:n], ACT.Abs))
                        ach.link(act.activation(l, l, ACT.Exp, scale=-1.0))
                        act.activation(l, l, ACT.Ln, bias=1.0).then_inc(sem("sb_ln_done"), 1)

            sb_copy_qk(0)
            with act.Fori(0, SB_PAIRS - 1) as i:
                ach.loop(i, 2 * SB_ITEMS)
                sb_pair(i)
                sb_copy_qk(i + 1)
            ach.end(SB_PAIRS - 1)
            sb_pair(SB_PAIRS - 1)

            norm_full("sb_o", nk=CONV2_PANELS)
            merge_gates(R9, 1, attn_gate)
            R9.panel_done(act, 0, 2 * KD - 1)
            for k in range(KD):
                act.wait_ge(sem("m_done"), KD + 2 + k + 1)
                act.activation(act_hi[:, k, :], merged[:, k, :], ACT.Copy, scale=0.5).then_inc(sem("merged_hi_done"), 1)
            for c in range(2):
                for t in range(NT):
                    if t < NT - 1:
                        act.wait_ge(sem("mixed_prod"), 14 + 7 * c + t + 1)
                    else:
                        R10.panel_done(act, 0, 4 * c + 3)
                    act.copy(acc[:, t, c * HALF:(c + 1) * HALF], ps[:, t, :]).then_inc(sem("mixed_done"), 1)
                if c == 0:
                    act.wait_ge(sem("merged_split"), KD)
                    act.wait_ge(sem("x1_stored"), 16 * NT)
                    for t in range(NT):
                        act.dma_start(resid[:, t, :], x1_spill[t]).then_inc(sem(f"x_in{t}"), 16)
                    act.dma_start(gain_row[:], d["g_post_mix_2"][0].partition_broadcast(P)).then_inc(sem("gain_in"), 16)
            act.wait_ge(sem("mixed_done"), 4 * NT)
            norm_square(acc, act_lo_junk, lambda t: None)
            norm_square(resid, acc, lambda t: act.wait_ge(sem("resid_done"), 2 * NT + t + 1))
            norm_scale("n4", resid, acc)
            norm_full("n4", lambda k: scale2[:, KD + k:KD + k + 1], lambda k: mod[:, 3 * KD + k:3 * KD + k + 1])
            ffn_relu(R11, 1)
            act.wait_ge(sem("ffn_acc"), 2 * (16 * FFN_STEPS + 4))
            act.dma_start(gain_row[:], d["g_post_mlp_2"][0].partition_broadcast(P)).then_inc(sem("gain_in"), 16)
            norm_square(acc, act_hi_junk, lambda t: None)

        @block.vector
        def _(dve):
            ch = Chain(dve, sem("dve_chain"))

            def norm_split(tag, hi, lo, nk=KD):
                base = TURNS[tag]
                for n in range(2 * nk):
                    h, k = n // nk, n % nk
                    cols = slice(h * HALF, (h + 1) * HALF)
                    dve.wait_ge(sem("turn_read"), base + n + 1)
                    dve.tensor_copy(hi[:, k, cols], norm_tmp[n % 2][:]).then_inc(sem("turn_hi_done"), 1)
                    dve.wait_ge(sem("turn_hi_done"), base + n + 1)
                    dve.tensor_tensor(lo[:, k, cols], norm_tmp[n % 2][:], hi[:, k, cols].bitcast(F32), ALU.subtract)\
                        .then_inc(sem("turn_split"), 1)

            dve.memset(conv_t[:], 0.0).then_inc(sem("conv_sq_done"), 1)
            dve.memset(xpad[:, 0:CONV_W - 1], 0.0).then_inc(sem("conv_pad_done"), 1)
            norm_split("n1", act_hi, act_lo)

            dve.wait_ge(sem("gdn_vec_in"), 48)
            ch.link(dve.tensor_scalar(out_norm_row[:], out_norm_row[:], 0.5, None, ALU.mult))
            for t in range(NT):
                dve.wait_ge(sem("gate_tanh_done"), t + 1)
                dve.scalar_tensor_tensor(gate[:, t, :], gate_tanh[t % 2][:], 1.0, ps[:, t, :], ALU.add, ALU.mult)\
                    .then_inc(sem("gate_silu"), 1)
                dve.wait_ge(sem("gate_silu"), t + 1)
                gh = gate[:, t, :].rearrange("p (h e) -> p h e", h=GDN_HEADS)
                ch.link(dve.tensor_tensor(gh, gh, out_norm_row[:].unsqueeze(1).broadcast_to([P, GDN_HEADS, P]), ALU.mult))

            with dve.Fori(0, GDN_PANELS // 3) as i:
                ch.loop(i, 9)
                for j in range(3):
                    p = 3 * i + j
                    dve.wait_ge(sem("conv_in_done"), p + 3)

                    def tap(w):
                        return vec[:, bass.ds(V_CONV + w * GDN_PANELS + p, 1)]

                    ch.link(dve.tensor_scalar(conv_y[:], xpad[:, 0:SEQ], tap(0), None, ALU.mult))
                    for w in range(1, CONV_W):
                        ins = dve.scalar_tensor_tensor(conv_y[:], xpad[:, w:w + SEQ], tap(w), conv_y[:],
                                                       ALU.mult, ALU.add)
                        if w < CONV_W - 1:
                            ch.link(ins)
                        else:
                            ins.then_inc(sem("conv_done"), 1)
                    dve.wait_ge(sem("conv_tanh_done"), p + 1)
                    dve.scalar_tensor_tensor(qkv[:, p, :], conv_t[:], 1.0, conv_y[:], ALU.add, ALU.mult)\
                        .then_inc(sem("conv_silu_done"), 1)
                    dve.wait_ge(sem("ss_prod"), p + 1)
                    dve.tensor_copy(ss_gdn[:, :, p], ps[:, 6, 0:NT]).then_inc(sem("ss_gdn_done"), 1)
                ch.end(GDN_PANELS // 3)
            rr = slice(NOPE, DQK)
            dve.wait_ge(sem("pos_in"), 16)
            dve.wait_ge(sem("conv_silu_done"), GDN_PANELS)
            dve.wait_ge(sem("conv_sq_done"), GDN_PANELS + 1)
            ch.link(dve.tensor_copy(ang[rr, :], pos_i[rr, :]))
            ch.link(dve.tensor_scalar(ang[rr, :], ang[rr, :], consts[rr, C_FREQ:C_FREQ + 1], None, ALU.mult))
            for t_, quarter in ((cos_f, 0.25), (sin_f, 0.0)):
                ch.link(dve.tensor_scalar(turns[rr, :], ang[rr, :], 1.0 / TWO_PI, quarter, ALU.mult, ALU.add))
                ch.link(dve.tensor_scalar(turns[rr, :], turns[rr, :], ROUND, ROUND, ALU.add, ALU.subtract))
                src = ang
                for part in TWO_PI_PARTS:
                    ch.link(dve.scalar_tensor_tensor(t_[rr, :], turns[rr, :], -part, src[rr, :], ALU.mult, ALU.add))
                    src = t_
                ch.link(dve.tensor_scalar(t_[rr, :], t_[rr, :], quarter * TWO_PI, PI_BELOW, ALU.add, ALU.min))
                dve.tensor_scalar(t_[rr, :], t_[rr, :], -PI_BELOW, None, ALU.max).then_inc(sem("rope_arg_done"), 1)

            dtb = dt_b[:].unsqueeze(1).broadcast_to([P, NT, GDN_HEADS])
            ch.link(dve.tensor_tensor(g_arg[:], lat[:, :, 0:GDN_HEADS], dtb, ALU.add))
            dve.tensor_scalar(g_la[:], g_arg[:], 40.0, None, ALU.min).then_inc(sem("g_min_done"), 1)

            dve.wait_ge(sem("lat_rstd_done"), 1)

            def by_tile(col, n):
                return lat_rstd[:, col:col + NT].unsqueeze(2).broadcast_to([P, NT, n])

            o_kr, half = LAT_KR - LAT_CQ, ROPE // 2
            dve.tensor_tensor(lat_n[:, :, 0:Q_RANK], lat[:, :, LAT_CQ:LAT_CKV], by_tile(0, Q_RANK), ALU.mult)
            dve.tensor_tensor(lat_n[:, :, Q_RANK:o_kr], lat[:, :, LAT_CKV:LAT_KR], by_tile(NT, KV_RANK), ALU.mult)
            dve.tensor_copy(lat_n[:, :, o_kr:o_kr + ROPE], lat[:, :, LAT_KR:LAT_KR + ROPE])
            dve.tensor_copy(lat_n[:, :, o_kr + ROPE:o_kr + ROPE + half], lat[:, :, LAT_KR + half:LAT_KR + ROPE])
            dve.tensor_copy(lat_n[:, :, o_kr + ROPE + half:o_kr + 2 * ROPE], lat[:, :, LAT_KR:LAT_KR + half])\
                .then_inc(sem("lat_norm_done"), 1)
            dve.wait_ge(sem("rope_trig_done"), 2)
            ch.link(dve.tensor_scalar(sin_f[rr, :], sin_f[rr, :], consts[rr, C_SIGN:C_SIGN + 1], None, ALU.mult))
            for n, (dst, trig) in enumerate(((k_f, cos_f), (k_f, cos_f), (rope_t, sin_f), (rope_t, sin_f))):
                cols = slice((n % 2) * HALF, (n % 2 + 1) * HALF)
                dve.wait_ge(sem("lat_turned"), 7 + n)
                ch.link(dve.tensor_tensor(dst[rr, cols], ps[rr, (6 + n) % 8, :], trig[rr, cols], ALU.mult))
            dve.tensor_tensor(k_f[rr, :], k_f[rr, :], rope_t[rr, :], ALU.add).then_inc(sem("k_rope_done"), 1)

            dve.wait_ge(sem("g_exp_done"), 4)
            ch.link(dve.tensor_tensor(g_sp[:], g_sp[:], g_arg[:], ALU.max))
            eab = ea_b[:].unsqueeze(1).broadcast_to([P, NT, GDN_HEADS])
            dve.scalar_tensor_tensor(g_la[:], g_sp[:], -1.0, eab, ALU.mult, ALU.mult).then_inc(sem("log_a_done"), 1)
            ch.link(dve.tensor_scalar(g_beta[:], g_beta[:], 0.5, 0.5, ALU.mult, ALU.add))
            dve.wait_ge(sem("qk_norm_done"), 2)
            ch.link(dve.tensor_tensor(g_bk[:], g_beta[:], g_rk[:], ALU.mult))
            ch.link(dve.tensor_scalar(g_cv[:], g_beta[:], 0.5, None, ALU.mult))
            dve.wait_ge(sem("cumsum_done"), 2)
            dve.tensor_tensor(g_ekd[:], g_tot[:], g_cum[:], ALU.subtract).then_inc(sem("g_tail_done"), 1)
            dve.wait_ge(sem("g_exps_done"), 2)
            ch.link(dve.tensor_tensor(g_cw[:], g_bk[:], g_eg[:], ALU.mult))
            ch.link(dve.tensor_tensor(g_cd[:], g_rk[:], g_ekd[:], ALU.mult))

            scale = float(DQK) ** -0.5
            with dve.Fori(0, MLA_HEADS) as h:
                ch.loop(h, 1 + 3 * NT)
                dve.wait_ge(sem("mla_q_prod"), h + 1)
                q_rot = ps[rr, 0:2, :].rearrange("p b n -> p (b n)")
                q_swp = ps[rr, 2:4, :].rearrange("p b n -> p (b n)")
                dve.wait_ge(sem("mla_qk_done"), 2 * h + 1)
                dve.tensor_tensor(rope_t[rr, :], q_swp, sin_f[rr, :], ALU.mult)
                ch.link(dve.tensor_tensor(q_f[rr, :], q_rot, cos_f[rr, :], ALU.mult))
                dve.tensor_tensor(q_f[rr, :], q_f[rr, :], rope_t[rr, :], ALU.add).then_inc(sem("mla_rope_done"), 1)

                def row_max(t):
                    n = (t + 1) * P
                    s = ps[:, 2 * (t % 2):2 * (t % 2) + 2, :].rearrange("p b n -> p (b n)")
                    dve.wait_ge(sem("mla_scores"), NT * h + t + 1)
                    ch.link(dve.memset(s[0:CHUNK, n - CHUNK:n], -1e30))
                    ch.link(dve.tensor_reduce(sm_max[:, t:t + 1], s[:, 0:n], AX_X, ALU.max))
                    dve.tensor_scalar(sm_neg[:, t:t + 1], sm_max[:, t:t + 1], -scale, None, ALU.mult)\
                        .then_inc(sem("mla_max_done"), 1)

                g0 = 0
                row_max(0)
                for t in range(NT):
                    if t + 1 < NT:
                        row_max(t + 1)
                    groups = 2 if t >= 4 else 1
                    for n in range(groups):
                        w = min(4, t + 1 - 4 * n) * P
                        dve.wait_ge(sem("mla_turned"), MLA_GROUPS * h + g0 + n + 1)
                        dve.wait_ge(sem("mla_pv"), MLA_GROUPS * h + g0 + n + 1)
                        dve.tensor_copy(probs_t[(g0 + n) % 2][:, 0:w], ps[:, 4 + (g0 + n) % 2, 0:w])\
                            .then_inc(sem("mla_pt_done"), 1)
                    g0 += groups
                    ch.link(dve.reciprocal(sm_rec[:, t:t + 1], sm_sum[:, t:t + 1]))
                    dve.wait_ge(sem("mla_pv"), MLA_GROUPS * h + g0 + 2)
                    dve.tensor_scalar(mix[:, t, bass.ds(GDN_W + h * V_DIM, V_DIM)], ps[:, 6 + t % 2, 0:V_DIM],
                                      sm_rec[:, t:t + 1], None, ALU.mult).then_inc(sem("mla_o_done"), 1)
                ch.end(MLA_HEADS)

            def by_head(cols):
                return cols.unsqueeze(2).broadcast_to([P, GDN_HEADS, P])

            def each_head(mask):
                return consts[:, mask:mask + P].unsqueeze(1).broadcast_to([P, GDN_HEADS, P])

            def bank(n):
                return ps[:, n, :].rearrange("p (h t) -> p h t", h=GDN_HEADS)

            dve.memset(state[0][:], 0.0).then_inc(sem("state0_done"), 1)
            with dve.Fori(0, NT) as i:
                ch.loop(i, 14)
                cols = bass.ts(i, P)
                dve.tensor_copy(k_s[:], qkv[:, GDN_HEADS:2 * GDN_HEADS, cols])
                dve.tensor_copy(q_s[:], qkv[:, 0:GDN_HEADS, cols])
                dve.tensor_copy(v_s[:], qkv[:, 2 * GDN_HEADS:3 * GDN_HEADS, cols])
                dve.tensor_tensor(u_g[:], each_head(C_CSUM), by_head(g_la[:, i, :]), ALU.mult)
                dve.tensor_tensor(i_b[:], each_head(C_ID), by_head(g_bk[:, i, :]), ALU.mult)\
                    .then_inc(sem("gdn_tile_in"), 1)
                dve.wait_ge(sem("e_g_done"), i + 1)
                ch.link(dve.tensor_tensor(e_d[:], bank(0), by_head(g_cum[:, i, :]), ALU.subtract))
                dve.tensor_scalar(e_d[:], e_d[:], 0.0, None, ALU.min).then_inc(sem("decay_arg_done"), 1)
                ch.link(dve.tensor_tensor(q_d[:], q_s[:], e_g[:], ALU.mult))
                dve.wait_ge(sem("decay_done"), i + 1)
                ch.link(dve.tensor_tensor(e_m[:], e_d[:], by_head(g_rk[:, i, :]), ALU.mult))
                ch.link(dve.tensor_tensor(a_t[:], e_m[:], each_head(C_STRICT), ALU.mult))
                dve.wait_ge(sem("kk_prod"), i + 1)
                ch.link(dve.tensor_tensor(a_t[:], bank(2), a_t[:], ALU.mult))
                ch.link(dve.tensor_tensor(a_t[:], bank(1), a_t[:], ALU.mult))
                ch.link(dve.tensor_tensor(m_s[0][:], a_t[:], each_head(C_LEVEL), ALU.mult))
                dve.tensor_tensor(t_r[0][:], each_head(C_ID), m_s[0][:], ALU.subtract).then_inc(sem("tr0_done"), 1)
                for n in range(1, len(LEVELS)):
                    ins = dve.tensor_tensor(m_s[n][:], a_t[:], each_head(C_LEVEL + n * P), ALU.mult)
                ins.then_inc(sem("a_levels_done"), 1)
                ch.link(dve.tensor_tensor(p_t[:], e_m[:], each_head(C_CSUM), ALU.mult))
                ch.link(dve.tensor_tensor(p_t[:], bank(3), p_t[:], ALU.mult))
                dve.wait_ge(sem("kv_turned"), 2 * i + 2)
                dve.tensor_tensor(k_w[:], bank(4), by_head(g_cw[:, i, :]), ALU.mult)
                dve.tensor_tensor(k_d[:], bank(4), by_head(g_cd[:, i, :]), ALU.mult)
                dve.tensor_tensor(v_b[:], bank(5), by_head(g_cv[:, i, :]), ALU.mult).then_inc(sem("kvw_done"), 1)
                dve.wait_ge(sem("t0_done"), i + 1)
                for n in range(1, len(LEVELS)):
                    a, b = (n - 1) % 2, n % 2
                    last = n == len(LEVELS) - 1
                    dve.wait_ge(sem("zt_prod"), 5 * i + n)
                    ins = dve.tensor_tensor(t_r[b][:], t_r[a][:], bank(6), ALU.subtract)
                    if last:
                        ins.then_inc(sem("t_last_done"), 1)
                    else:
                        dve.wait_ge(sem("z_prod"), 4 * i + n)
                        dve.tensor_tensor(t_f[b][:], t_f[a][:], bank(0), ALU.subtract).then_inc(sem("t_done"), 1)
                dve.wait_ge(sem("wu_done"), 2 * i + 2)
                for c in range(2):
                    rows = slice(c * CHUNK, (c + 1) * CHUNK)
                    last = c * CHUNK + CHUNK - 1
                    ch.link(dve.tensor_tensor(s_dec[:], state[c][:],
                                              e_g[:, :, last:last + 1].broadcast_to([P, GDN_HEADS, P]), ALU.mult))
                    dve.wait_ge(sem("ws_prod"), 2 * i + c + 1)
                    dve.tensor_tensor(v_n[rows, :, :], u_s[rows, :, :], bank(3)[rows], ALU.subtract)\
                        .then_inc(sem("v_new_done"), 1)
                    dve.wait_ge(sem("ds_prod"), 2 * i + c + 1)
                    dve.tensor_tensor(state[1 - c][:], s_dec[:], bank(5), ALU.add).then_inc(sem("state_done"), 1)
                    dve.wait_ge(sem("state_done"), 2 * i + c + 1)
                dve.wait_ge(sem("o_prod"), i + 1)
                ch.link(dve.tensor_tensor(o_s[:], bank(4), by_head(g_rq[:, i, :]), ALU.mult))
                ch.link(dve.tensor_tensor(o_sq[:], o_s[:], o_s[:], ALU.mult))
                dve.tensor_reduce(o_ss[:], o_sq[:], AX_X, ALU.add).then_inc(sem("o_ss_done"), 1)
                dve.wait_ge(sem("o_rstd_done"), i + 1)
                ch.link(dve.tensor_tensor(o_s[:], o_s[:], by_head(o_rstd[:]), ALU.mult))
                dve.tensor_tensor(mix[:, i, 0:GDN_W].rearrange("p (h e) -> p h e", h=GDN_HEADS), o_s[:],
                                  gate[:, i, :].rearrange("p (h e) -> p h e", h=GDN_HEADS), ALU.mult)\
                    .then_inc(sem("gdn_out_done"), 1)
                ch.end(NT)

            norm_split("mixt", mixt_hi, mixt_lo)

            def post_norm(tag, src, row_in, ready):
                dve.wait_ge(row_in, 16)
                for t in range(NT):
                    ready(t)
                    dve.wait_ge(sem("norm_rstd_done"), 2 * NORMS.index(tag) + t // 4 + 1)
                    ch.link(dve.scalar_tensor_tensor(post_tmp[t % 2][:], src[:, t, :], rstd[:, t:t + 1], post_row[:],
                                                     ALU.mult, ALU.mult))
                    dve.tensor_tensor(resid[:, t, :], resid[:, t, :], post_tmp[t % 2][:], ALU.add)\
                        .then_inc(sem("resid_done"), 1)

            post_norm("mix_post", mixed, sem("mix_post_in"), lambda t: dve.wait_ge(sem(f"x_in{t}"), 32))
            norm_split("n2", act_hi, act_lo)

            def ffn_sums(ring, run):
                for t in range(NT):
                    ins = dve.memset(acc[:, t, :], 0.0)
                ins.then_inc(sem("ffn_acc"), 4)
                with dve.Fori(0, FFN_STEPS) as i:
                    ch.loop(i, 4)
                    for q in range(4):
                        j, cols = q // 2, slice((q % 2) * HALF, (q % 2 + 1) * HALF)
                        dve.wait_ge(sem("ffn_relu"), 4 * i + (4 * FFN_STEPS * run + q + 1))
                        dve.wait_ge(sem("ffn_hid"), 4 * i + (4 * FFN_STEPS * run + q + FFN_CREDIT))
                        ch.link(dve.tensor_tensor(relu_sq[:], relu_t[q % 2][:], relu_t[q % 2][:], ALU.mult))
                        dve.wait_ge(sem("ffn_hid_hi"), 4 * i + (4 * FFN_STEPS * run + q + 1))
                        dve.tensor_tensor(hid_lo[:, j, cols], relu_sq[:], hid_hi[:, j, cols].bitcast(F32), ALU.subtract)\
                            .then_inc(sem("ffn_hid"), 1)
                    for g in range(16):
                        t, cols = g // 2, slice((g % 2) * HALF, (g % 2 + 1) * HALF)
                        if g < 15:
                            dve.wait_ge(sem("ffn_down"), 15 * i + (15 * FFN_STEPS * run + g + 1))
                        else:
                            ring.panel_done(dve, 4 * i, 3)
                        dve.tensor_tensor(acc[:, t, cols], ps[:, 4 + g % 4, :], acc[:, t, cols], ALU.add)\
                            .then_inc(sem("ffn_acc"), 1)
                    dve.wait_ge(sem("ffn_acc"), 16 * i + ((16 * FFN_STEPS + 4) * run + 20))
                ch.end(FFN_STEPS)

            ffn_sums(R4, 0)
            post_norm("ffn_post", acc, sem("ffn_post_in"), lambda t: None)
            dve.wait_ge(sem("ada_read"), FFN_STEPS + 1)
            ch.link(dve.tensor_tensor(mod[:], mod[:], vec2[:, 0:N_BADA], ALU.add))
            for n, (gain, col) in enumerate(((V_GPREMIX2, KD), (V_GPREMLP2, 4 * KD))):
                ch.link(dve.scalar_tensor_tensor(scale2[:, n * KD:(n + 1) * KD], mod[:, col:col + KD], 1.0,
                                                 vec[:, gain:gain + KD], ALU.add, ALU.mult))
            dve.sem_inc(sem("mod_scales_done"), 1)
            norm_split("n3", act_hi, act_lo)

            ch.link(dve.memset(vpad[:, 0:CONV2_TAPS - 1], 0.0))
            with dve.Fori(0, CONV2_PANELS) as i:
                ch.loop(i, 3)

                def tap(w):
                    return vec[:, bass.ds(V_CONV2 + w * CONV2_PANELS + i, 1)]

                R5.panel_done(dve, 3 * i, 2)
                dve.wait_ge(sem("c2_cg_read"), i + 2)
                dve.tensor_tensor(vpad[:, CONV2_TAPS - 1:], ps[:, 4:6, :].rearrange("p b n -> p (b n)"), cg_t[:], ALU.mult)\
                    .then_inc(sem("c2_v_done"), 1)
                dve.wait_ge(sem("c2_v_done"), i + 2)
                ch.link(dve.tensor_scalar(conv2_y[:], vpad[:, 0:SEQ], tap(0), None, ALU.mult))
                for w in range(1, CONV2_TAPS):
                    ch.link(dve.scalar_tensor_tensor(conv2_y[:], vpad[:, w:w + SEQ], tap(w), conv2_y[:], ALU.mult, ALU.add))
                dve.tensor_tensor(conv2_y[:], ps[:, 0:2, :].rearrange("p b n -> p (b n)"), conv2_y[:], ALU.mult)\
                    .then_inc(sem("c2_y_done"), 1)
                dve.wait_ge(sem("c2_hi_done"), i + 1)
                dve.wait_ge(sem("c2_y_done"), i + 2)
                dve.tensor_tensor(y_lo[:, i, :], conv2_y[:], y_hi[:, i, :].bitcast(F32), ALU.subtract)\
                    .then_inc(sem("c2_split"), 1)
                dve.wait_ge(sem("c2_split"), i + 1)
            ch.end(CONV2_PANELS)

            dve.wait_ge(sem("x1_stored"), 16 * NT)
            with dve.Fori(0, KD // 2) as i:
                for j in range(2):
                    R6.panel_done(dve, 4 * i, 2 * j + 1)
                    dve.wait_ge(sem("m_gate_read"), 2 * i + (j + 3))
                    dve.scalar_tensor_tensor(merged[:, 2 * i + j, :], conv_gate[j][:], 1.0,
                                             ps[:, 4 * j + 2:4 * j + 4, :].rearrange("p b n -> p (b n)"), ALU.add, ALU.mult)\
                        .then_inc(sem("m_done"), 1)

            z_scale = float(SB_DIM) ** -0.5

            def sb_take(i, s):
                t = s // 2
                n, z = (t + 1) * P, sb_z[s % 2]
                dve.wait_ge(sem("sb_scores"), SB_ITEMS * i + s + 1)
                ch.link(dve.tensor_scalar(z[:, 0:n], ps[:, 2 * (s % 2):2 * (s % 2) + 2, :].rearrange("p b n -> p (b n)")[:, 0:n],
                                          z_scale, None, ALU.mult))
                dve.tensor_tensor(z[:, t * P:n], z[:, t * P:n], consts[:, C_KEYCAP:C_KEYCAP + P], ALU.min)\
                    .then_inc(sem("sb_z_done"), 1)

            def sb_log_weights(i, s):
                n = (s // 2 + 1) * P
                z, l, a = (x[:, 0:n] for x in (sb_z[s % 2], sb_sp[s % 2], sb_a[s % 3]))
                dve.wait_ge(sem("sb_ln_done"), SB_ITEMS * i + s + 1)
                ch.link(dve.scalar_tensor_tensor(l, z, 0.0, l, ALU.max, ALU.add))
                ch.link(dve.tensor_tensor_scan(a[:, ::-1], l[:, ::-1], l[:, ::-1], 0.0, ALU.add, ALU.bypass))
                dve.tensor_tensor(a, z, a, ALU.subtract).then_inc(sem("sb_arg_done"), 1)
                dve.wait_ge(sem("sb_arg_done"), SB_ITEMS * i + s + 1)

            def sb_weights_out(i, s):
                for n, g in enumerate(sb_groups(s)):
                    w = min(4, s // 2 + 1 - 4 * n) * P
                    dve.wait_ge(sem("sb_turned"), SB_GROUPS * i + g + 1)
                    dve.wait_ge(sem("sb_pv"), SB_GROUPS * i + g + 1)
                    dve.tensor_copy(sb_at[g % 2][:, 0:w], ps[:, 4 + g % 2, 0:w]).then_inc(sem("sb_at_done"), 1)

            def sb_out(i, half):
                dve.wait_ge(sem("sb_pv"), SB_GROUPS * i + (sb_groups(half * NT + NT - 1)[-1] + 3))
                dve.tensor_copy(o2[:, 4 * half:4 * half + 4, bass.ds(P * i, P)],
                                ps[:, 6 + half, :].rearrange("p (t e) -> p t e", t=4)).then_inc(sem("sb_o_done"), 1)

            def sb_pair(i):
                for s in range(SB_ITEMS + SB_LAG_TURN):
                    if s < SB_ITEMS:
                        sb_take(i, s)
                    if SB_LAG_ARG <= s < SB_ITEMS + SB_LAG_ARG:
                        sb_log_weights(i, s - SB_LAG_ARG)
                    if s >= SB_LAG_TURN:
                        sb_weights_out(i, s - SB_LAG_TURN)
                    if s == NT + SB_LAG_PV:
                        sb_out(i, 0)
                sb_out(i, 1)

            with dve.Fori(0, SB_PAIRS - 1) as i:
                ch.loop(i, 3 * SB_ITEMS)
                sb_pair(i)
            ch.end(SB_PAIRS - 1)
            sb_pair(SB_PAIRS - 1)

            norm_split("sb_o", o2_hi, o2_lo, CONV2_PANELS)
            with dve.Fori(0, KD // 2) as i:
                ch.loop(i, 2)
                for j in range(2):
                    p = 2 * i + j
                    R9.panel_done(dve, 4 * i, 2 * j + 1)
                    dve.wait_ge(sem("m_gate_read"), p + KD + 3)
                    ch.link(dve.scalar_tensor_tensor(attn_part[j][:], attn_gate[j][:], 1.0,
                                                     ps[:, 4 * j + 2:4 * j + 4, :].rearrange("p b n -> p (b n)"),
                                                     ALU.add, ALU.mult))
                    dve.tensor_tensor(merged[:, p, :], merged[:, p, :], attn_part[j][:], ALU.add).then_inc(sem("m_done"), 1)
                    dve.wait_ge(sem("m_done"), p + KD + 3)
            ch.end(KD // 2)
            for k in range(KD):
                dve.wait_ge(sem("merged_hi_done"), k + 1)
                dve.scalar_tensor_tensor(act_lo[:, k, :], merged[:, k, :], 0.5, act_hi[:, k, :].bitcast(F32),
                                         ALU.mult, ALU.subtract).then_inc(sem("merged_split"), 1)

            def gate_row(run):
                col = mod[:, (2 + 3 * run) * KD:(3 + 3 * run) * KD]
                dve.tensor_tensor(diag[:], consts[:, C_ID:C_ID + P].unsqueeze(1).broadcast_to([P, KD, P]),
                                  col.unsqueeze(2).broadcast_to([P, KD, P]), ALU.mult).then_inc(sem("gate_diag_done"), 1)
                dve.wait_ge(sem("gain_in"), 16 * run + 16)
                dve.wait_ge(sem("gate_row_prod"), run + 1)
                ch.link(dve.tensor_tensor(post_row[:], ps[:, 0:2, :].rearrange("p b n -> p (b n)"), gain_row[:], ALU.mult))

            R10.panel_done(dve, 0, 7)
            gate_row(0)
            post_norm("mix_post2", acc, sem("gain_in"), lambda t: dve.wait_ge(sem(f"x_in{t}"), 48))
            norm_split("n4", act_hi, act_lo)
            ffn_sums(R11, 1)
            gate_row(1)
            post_norm("ffn_post2", acc, sem("gain_in"), lambda t: None)


def kernel(**inputs):
    from concourse import bacc
    from concourse.bass_utils import run_bass_kernel_spmd

    nc = bacc.Bacc("TRN2", target_bir_lowering=False, num_devices=1)
    arrays, d = {}, {}
    for name, value in list(inputs.items()) + [("consts", constants())]:
        a = np.ascontiguousarray(value)
        arrays[f"in_{name}"] = a
        d[name] = nc.dram_tensor(f"in_{name}", a.shape, mybir.dt.from_np(a.dtype), kind="ExternalInput").ap()
    out = nc.dram_tensor("out_0", [1, SEQ, D], F32, kind="ExternalOutput").ap()
    two_blocks(nc, d, out)
    r = run_bass_kernel_spmd(nc, [arrays], core_ids=[0])
    return r.results[0]["out_0"]
```

```python
import math
from contextlib import ExitStack

import concourse.bass as bass
import numpy as np
from concourse import mybir

F32 = mybir.dt.float32
F32R = mybir.dt.float32r
I32 = mybir.dt.int32
ALU = mybir.AluOpType
ACT = mybir.ActivationFunctionType
AX_X = mybir.AxisListType.X

P = 128
D = 1024
SEQ = 1024
NT = SEQ // P
KD = D // P
HALF = 512
EPS = 1e-6
D_FF = 4 * D

GDN_HEADS = 4
CHUNK = 64
GDN_W = GDN_HEADS * P
CONV_W = 4
MLA_HEADS = 8
NOPE = 64
ROPE = 32
DQK = NOPE + ROPE
V_DIM = 64
Q_RANK = 256
KV_RANK = 128
ROPE_THETA = 10000.0
GATE_COL = 3 * GDN_W
TAIL_COL = 4 * GDN_W
TAIL_W = 2 * GDN_HEADS + Q_RANK + KV_RANK + ROPE
LAT_CQ = 2 * GDN_HEADS
LAT_CKV = LAT_CQ + Q_RANK
LAT_KR = LAT_CKV + KV_RANK
GDN_PANELS = 3 * GDN_HEADS

CONV2 = 512
CONV2_TAPS = 3
CONV2_PANELS = CONV2 // P
SB_HEADS = 8
SB_DIM = 64
IN2_Q = 3 * CONV2
IN2_K = IN2_Q + 512
IN2_V = IN2_K + 512
IN2_GA = IN2_V + 512
IN2_GB = IN2_GA + D
N_MOD = 6

FFN_STEPS = D_FF // 256
FFN_CREDIT = 2
ADA_STEP = N_MOD * KD // FFN_STEPS
MLA_GROUPS = sum(2 * (t // 4 + 1) for t in range(NT))

SB_PAIRS = SB_HEADS // 2
SB_ITEMS = 2 * NT
SB_LAG_ARG, SB_LAG_EXP, SB_LAG_TURN, SB_LAG_PV = 1, 2, 3, 4


def sb_groups(s):
    first = sum(u // 2 // 4 + 1 for u in range(s))
    return range(first, first + s // 2 // 4 + 1)


SB_GROUPS = sb_groups(SB_ITEMS - 1)[-1] + 1

GDN_PAIRS = NT // 2

MLA_PAIRS = MLA_HEADS // 2
MLA_ITEMS = 2 * NT
MLA_LAG_TURN, MLA_LAG_PV = 2, 3
PROBS = 4
LAT_BANKS = (7, 0, 1, 2, 3, 6, 4, 5)


def mla_groups(s):
    first = sum(u % NT // 4 + 1 for u in range(s))
    return range(first, first + s % NT // 4 + 1)


def lagged(i, before, s, lag, items):
    if s >= lag:
        return i, s - lag
    return None if before is None else (before, items + s - lag)


TWO_PI = 2 * math.pi
TWO_PI_MID = math.floor((TWO_PI - 6.28125) * 2 ** 21) / 2 ** 21
TWO_PI_PARTS = (6.28125, TWO_PI_MID, TWO_PI - 6.28125 - TWO_PI_MID)
ROUND = 1.5 * 2.0 ** 23
PI_BELOW = 3.1415925

C_ID, C_ONES, C_CSUM, C_STRICT, C_CHUNK = 0, 128, 256, 384, 512
LEVELS = (1, 2, 4, 8, 16, 32)
C_LEVEL = 640
C_KEYCAP = C_LEVEL + P * len(LEVELS)
C_FREQ = C_KEYCAP + P
C_SIGN = C_FREQ + 1
C_QUARTER = C_SIGN + 1
C_QUARTER_ANGLE = C_QUARTER + 1
N_CONST = C_QUARTER_ANGLE + 1

V_MIXPRE, V_FFNPRE, V_QN, V_KVN, V_CONV = 0, 8, 16, 18, 19
V_GPREMIX2 = V_CONV + CONV_W * GDN_PANELS
V_GPREMLP2 = V_GPREMIX2 + KD
V_CONV2 = V_GPREMLP2 + KD
N_VEC = V_CONV2 + CONV2_TAPS * (CONV2 // P)
N_BADA = N_MOD * KD
N_VEC2 = N_BADA + KD


def constants():
    c = np.zeros((P, N_CONST), np.float32)
    r, k = np.arange(P)[:, None], np.arange(P)[None, :]
    same = r // CHUNK == k // CHUNK
    c[:, C_ID:C_ID + P] = r == k
    c[:, C_ONES:C_ONES + P] = 1.0
    c[:, C_CSUM:C_CSUM + P] = same & (r <= k)
    c[:, C_STRICT:C_STRICT + P] = same & (k < r)
    c[:, C_CHUNK:C_CHUNK + P] = same
    for n, s in enumerate(LEVELS):
        c[:, C_LEVEL + n * P:C_LEVEL + (n + 1) * P] = ((k // s) % 2 == 1) & (r // s == k // s - 1)
    c[:, C_KEYCAP:C_KEYCAP + P] = np.where(k < r, 3e38, -1e30)
    j = np.arange(ROPE // 2)
    freq = (ROPE_THETA ** (-2.0 * j / ROPE)).astype(np.float32)
    c[NOPE:P, C_FREQ] = np.tile(freq, 4)
    c[NOPE:DQK, C_SIGN] = 1.0
    c[DQK:P, C_SIGN] = np.repeat([-1.0, 1.0], ROPE // 2)
    c[NOPE:DQK, C_QUARTER] = 0.25
    c[NOPE:DQK, C_QUARTER_ANGLE] = 0.25 * TWO_PI
    return c


class Ring:

    SLOTS = 4

    def __init__(self, sem, total, raws, his, los, after=None):
        self.raw, self.hi, self.lo = raws, his, los
        self.nraw, self.nslab, self.total = len(raws), len(his), total
        self.raw_full = [sem(f"w_raw_full{r}") for r in range(self.SLOTS)]
        self.carrier = sem("wait_carrier")
        self.hi_done, self.split_done, self.used = sem("w_hi_done"), sem("w_split_done"), sem("w_slab_used")
        self.base = after.base + after.total if after else 0
        self.fills = after.fills_after if after else [0] * self.SLOTS
        self.fills_after = [self.fills[r] + (len(range(r, total, self.nraw)) if r < self.nraw else 0)
                            for r in range(self.SLOTS)]

    def credit(self, eng):
        eng.sem_inc(self.split_done, self.SLOTS)
        eng.sem_inc(self.used, self.SLOTS)

    def start(self, sp):
        sp.wait_ge(self.split_done, self.SLOTS + self.base)

    def start_split(self, pool):
        pool.wait_ge(self.used, self.SLOTS + self.base)

    def load(self, sp, n0, j, view, src):
        r = j % self.nraw
        sp.wait_ge(self.split_done, n0 + (self.SLOTS + self.base + j - self.nraw + 1))
        sp.sem_inc(self.carrier, 1)
        sp.dma_start(view(self.raw[r]), src).then_inc(self.raw_full[r], 16)

    def split(self, pool, n0, trips, j, width=1024):
        r, s = j % self.nraw, j % self.nslab
        pool.wait_ge(self.raw_full[r], trips * 16 + (self.fills[r] * 16 + 16))
        pool.wait_ge(self.used, n0 + (self.SLOTS + self.base + j - self.nslab + 1))
        pool.sem_inc(self.carrier, 1)
        pool.tensor_scalar(self.hi[s][:, 0:width], self.raw[r][:, 0:width], 1.0, 0.0, ALU.mult, ALU.add)\
            .then_inc(self.hi_done, 1)
        pool.wait_ge(self.hi_done, n0 + (self.base + j + 1))
        pool.tensor_tensor(self.lo[s][:, 0:width], self.raw[r][:, 0:width], self.hi[s][:, 0:width].bitcast(F32),
                           ALU.subtract).then_inc(self.split_done, 1)

    def ready(self, pe, n0, j):
        pe.wait_ge(self.split_done, n0 + (self.SLOTS + self.base + j + 1))

    def panel_done(self, eng, n0, j):
        eng.wait_ge(self.used, n0 + (self.SLOTS + self.base + j + 1))


class Chain:

    def __init__(self, eng, s):
        self.eng, self.s, self.base, self.n = eng, s, 0, 0

    def link(self, ins):
        ins.then_inc(self.s, 1)
        self.n += 1
        self.eng.wait_ge(self.s, self.base + self.n)

    def loop(self, i, per):
        self.start = self.base + self.n
        self.base, self.n, self.per = self.start + i * per, 0, per

    def end(self, trips):
        assert self.n == self.per, (self.n, self.per)
        self.base, self.n = self.start + trips * self.per, 0


def two_blocks(nc, d, out):
    ctx = ExitStack()
    with ctx:
        sems = {}

        def sem(name):
            if name not in sems:
                sems[name] = ctx.enter_context(nc.semaphore(name))
            return sems[name]

        SB0 = 16512

        def sb(name, kb, shape, dt=F32):
            t = nc.alloc_sbuf_tensor_at(name, list(shape), dt, offset=SB0 + int(kb * 1024))
            return t

        consts = sb("consts", 0, [P, N_CONST])
        vec = sb("vec_cols", 6.75, [P, N_VEC])
        vec2 = sb("vec2_cols", 7.25, [P, N_VEC2])
        mod = sb("mod_cols", 7.53125, [P, N_BADA])
        ssq = sb("ssq", 7.75, [P, NT])
        rstd = sb("rstd", 7.78125, [P, NT])
        mean_sq = sb("mean_sq", 7.8125, [P, NT])
        scale2 = sb("scale2_cols", 7.84375, [P, 2 * KD])
        half_neg = sb("minus_half", 7.90625, [P, 64])
        ident = consts[:, C_ID:C_ID + P]
        ones = consts[:, C_ONES:C_ONES + P]

        raws = [sb(f"raw{r}", 9 + 4 * r, [P, 1024]) for r in range(4)]
        slab_hi = [sb(f"slab_hi{s}", 25 + 8 * s, [P, 1024], F32R) for s in range(4)]
        slab_lo = [sb(f"slab_lo{s}", 29 + 8 * s, [P, 1024], F32R) for s in range(4)]

        act_hi = sb("act_hi", 57, [P, KD, SEQ], F32R)
        act_lo = sb("act_lo", 89, [P, KD, SEQ], F32R)
        acc = sb("acc", 121, [P, NT, D])
        resid = sb("resid", 153, [P, NT, D])
        norm_tmp = [sb(f"norm_tmp{i}", 203 + 2 * i, [P, HALF]) for i in range(2)]
        qkv = sb("qkv_feat", 121, [P, GDN_PANELS, SEQ])
        gate = sb("gate_tok", 169, [P, NT, GDN_W])
        lat = sb("lat_tok", 185, [P, NT, TAIL_W + ROPE])
        gate_tanh = [sb(f"gate_tanh{i}", 203 + 2 * i, [P, HALF]) for i in range(2)]
        out_norm_row = sb("out_norm_row", 49, [P, P])
        xpad = sb("conv_in", 199.25, [P, SEQ + CONV_W - 1])
        conv_y = sb("conv_y", 49, [P, SEQ])
        conv_t = sb("conv_tanh", 53, [P, SEQ])
        ss_gdn = sb("ss_gdn", 203.5, [P, NT, GDN_PANELS])
        vec_rows = sb("vec_rows", 185, [P, P])
        vec2_rows = sb("vec2_rows", 185.5, [P, P])
        mix = sb("mix_tok", 57, [P, NT, D])
        cq_f = sb("cq_feat", 89, [P, 2, SEQ])
        ckv_f = sb("ckv_feat", 97, [P, SEQ])
        trig = sb("rope_trig", 21, [P, SEQ])
        v_t = sb("v_tok", 101, [P, NT, MLA_HEADS, V_DIM])
        rope_t = sb("rope_tmp", 117, [P, SEQ])
        q_f = [sb("q_feat0", 49, [P, SEQ]), sb("q_feat1", 29, [P, SEQ])]
        k_f = [sb("k_feat0", 53, [P, SEQ]), sb("k_feat1", 33, [P, SEQ])]
        probs = [sb(f"probs{i}", kb, [P, SEQ]) for i, kb in enumerate((9, 13, 17, 25))]
        probs_t = [sb(f"probs_t{i}", 41 + 2 * i, [P, HALF]) for i in range(2)]
        wq = [sb(f"wq_head{i}", 37 + 1.25 * i, [P, 2, P]) for i in range(2)]
        wk = [sb(f"wk_head{i}", 38 + 1.25 * i, [P, NOPE]) for i in range(2)]
        w_kv = sb("w_kv_all", 45, [P, 1024])
        sm_max = [sb(f"sm_max{i}", 40 + 0.125 * i, [P, NT]) for i in range(2)]
        sm_neg = [sb(f"sm_neg{i}", 40.03125 + 0.125 * i, [P, NT]) for i in range(2)]
        sm_sum = [sb(f"sm_sum{i}", 40.0625 + 0.125 * i, [P, NT]) for i in range(2)]
        sm_rec = [sb(f"sm_rec{i}", 40.09375 + 0.125 * i, [P, NT]) for i in range(2)]
        lat_junk = [sb(f"lat_junk{i}", 199.25 + 1.5 * i, [P, Q_RANK + KV_RANK]) for i in range(2)]
        lat_ss = sb("lat_ss", 204.25, [P, 2 * NT])
        lat_ms = sb("lat_ms", 204.3125, [P, 2 * NT])
        lat_rstd = sb("lat_rstd", 204.375, [P, 2 * NT])
        pos_i = sb("pos_i", 53, [P, SEQ], I32)
        ang = sb("rope_ang", 49, [P, SEQ])
        turns = sb("rope_turns", 53, [P, SEQ])

        def small(name, slot):
            return sb(name, 205.5 + 0.125 * slot, [P, NT, GDN_HEADS])

        g_arg, g_exp, g_sp, g_la, g_beta, g_cum, g_tot, g_eg, g_ekd, g_rk, g_rq, g_bk, g_cw, g_cd, g_cv = [
            small(n, i) for i, n in enumerate(
                ["g_arg", "g_exp", "g_softplus", "g_log_a", "g_beta", "g_cumsum", "g_total", "g_exp_cum",
                 "g_exp_tail", "g_rk", "g_rq", "g_beta_rk", "g_w_scale", "g_kdec_scale", "g_v_scale"])]
        g_u = sb("g_exp_plus_1", 204.5, [P, NT, GDN_HEADS])
        a_log_b = sb("a_log_bc", 207.375, [P, GDN_HEADS])
        dt_b = sb("dt_bias_bc", 207.40625, [P, GDN_HEADS])
        ea_b = sb("exp_a_log", 207.4375, [P, GDN_HEADS])

        def head_tile(name, kb):
            return sb(name, kb, [P, GDN_HEADS, P])

        def tile_pair(name, kb):
            return [head_tile(f"{name}{a}", kb + 2 * a) for a in range(2)]

        k_s, v_s, e_d, e_g = (tile_pair(n, 9 + 4 * x) for x, n in enumerate(("k_tile", "v_tile", "decay", "exp_g_row")))
        k_w, v_b = k_s, v_s
        a_t, y_s = tile_pair("a_T", 25), tile_pair("level_y", 29)
        m_s = [tile_pair(f"a_level{n}_", 33 + 4 * n) for n in range(2)]
        t_f = [tile_pair(f"t_inv{n}_", 41 + 4 * n) for n in range(2)]
        t_r = [tile_pair(f"t_inv_T{n}_", 49 + 4 * n) for n in range(2)]
        w_t, u_s, q_d, k_d, p_t = (tile_pair(n, 89 + 4 * x) for x, n in enumerate(("w_T", "u", "q_dec", "k_dec", "p_T")))
        state = tile_pair("state", 109)
        v_n, s_dec, o_s, o_sq = (head_tile(n, 113 + 2 * x) for x, n in enumerate(("v_new", "state_dec", "o_tok", "o_sq")))
        u_g, i_b = head_tile("cumsum_la", 185), head_tile("ident_bk", 187)
        e_last = [sb(f"exp_g_last{a}", 189.125 + 0.0625 * a, [P, GDN_HEADS, 2]) for a in range(2)]
        o_ss = sb("o_ss", 189, [P, GDN_HEADS])
        o_ms = sb("o_ms", 189.03125, [P, GDN_HEADS])
        o_rstd = sb("o_rstd", 189.0625, [P, GDN_HEADS])

        act_hi_junk = sb("squares_junk_hi", 57, [P, NT, D])
        act_lo_junk = sb("squares_junk_lo", 89, [P, NT, D])
        hid_hi = sb("hid_hi", 185, [P, 2, SEQ], F32R)
        hid_lo = sb("hid_lo", 193, [P, 2, SEQ], F32R)
        relu_t = [sb(f"relu{i}", 201 + 2 * i, [P, HALF]) for i in range(2)]
        relu_sq = sb("relu_sq", 205, [P, HALF])
        mixt_hi = sb("mixt_hi", 89, [P, KD, SEQ], F32R)
        mixt_lo = sb("mixt_lo", 121, [P, KD, SEQ], F32R)
        mixed = sb("mixed", 57, [P, NT, D])
        post_row = sb("post_norm_row", 185, [P, D])
        post_tmp = [sb(f"post_tmp{i}", 189 + 4 * i, [P, D]) for i in range(2)]

        ada = [sb(f"w_ada{i}", 17 + 4 * i, [P, KD, P]) for i in range(2)]
        cg_t = sb("c_gate", 21, [P, SEQ])
        conv2_y = sb("conv2_y", 49, [P, SEQ])
        vpad = sb("conv2_in", 203, [P, SEQ + CONV2_TAPS - 1])
        y_hi = sb("conv2_out_hi", 121, [P, CONV2_PANELS, SEQ], F32R)
        y_lo = sb("conv2_out_lo", 137, [P, CONV2_PANELS, SEQ], F32R)
        merged = sb("merged_feat", 153, [P, KD, SEQ])
        conv_gate = [sb(f"conv_gate{i}", 185 + 4 * i, [P, SEQ]) for i in range(2)]
        v2 = sb("v2_tok", 185, [P, NT, SB_HEADS, SB_DIM])
        q2, k2 = sb("q2_feat", 17, [P, SEQ]), sb("k2_feat", 21, [P, SEQ])
        sb_z = [sb(f"sb_z{i}", 41 + 4 * i, [P, SEQ]) for i in range(2)]
        sb_sp = [sb(f"sb_softplus{i}", 49 + 4 * i, [P, SEQ]) for i in range(2)]
        sb_a = [sb(f"sb_weights{i}", 137 + 4 * i, [P, SEQ]) for i in range(3)]
        sb_at = [sb(f"sb_weights_t{i}", 201 + 2 * i, [P, HALF]) for i in range(2)]
        o2 = sb("o2_tok", 121, [P, NT, CONV2])
        o2_hi = sb("o2_feat_hi", 137, [P, CONV2_PANELS, SEQ], F32R)
        o2_lo = sb("o2_feat_lo", 185, [P, CONV2_PANELS, SEQ], F32R)
        attn_gate = [sb(f"attn_gate{i}", 121 + 4 * i, [P, SEQ]) for i in range(2)]
        attn_part = [sb(f"attn_part{i}", 129 + 4 * i, [P, SEQ]) for i in range(2)]
        gain_row = sb("post_gain_row", 199, [P, D])
        diag = sb("gate_diag", 189, [P, KD, P])

        ps = ctx.enter_context(nc.psum_tensor("ps", [P, 8, HALF], F32))

        R1 = Ring(sem, 8, raws[:3], slab_hi[:3], slab_lo[:3])
        R2 = Ring(sem, GDN_PANELS, raws[:3], slab_hi[:3], slab_lo[:3], R1)
        R3 = Ring(sem, 8, raws, slab_hi, slab_lo, R2)
        R4 = Ring(sem, 4 * FFN_STEPS, raws[:2], slab_hi, slab_lo, R3)
        R5 = Ring(sem, 3 * CONV2_PANELS, raws[:3], slab_hi[:3], slab_lo[:3], R4)
        R6 = Ring(sem, 2 * KD, raws, slab_hi, slab_lo, R5)
        R7 = Ring(sem, 4, raws, slab_hi, slab_lo, R6)
        R8 = Ring(sem, SB_HEADS, raws[:2], slab_hi[:2], slab_lo[:2], R7)
        R9 = Ring(sem, 2 * KD, raws, slab_hi, slab_lo, R8)
        R10 = Ring(sem, 8, raws, slab_hi, slab_lo, R9)
        R11 = Ring(sem, 4 * FFN_STEPS, raws, slab_hi, slab_lo, R10)

        NORMS = ["n1", "mix_post", "n2", "ffn_post", "n3", "mix_post2", "n4", "ffn_post2"]
        TURNS = {"n1": 0, "mixt": 16, "n2": 32, "n3": 48, "sb_o": 64, "n4": 72}
        SCALES = ["n1", "n2", "n3", "n4"]
        FFNS = ["ffn", "ffn2"]

        x1_spill = nc.dram_tensor("x1_spill", [NT, P, D], F32, kind="Internal").ap()
        w_in2 = d["w_in_2"][0].rearrange("(k p) n -> p k n", p=P)
        w_pc = d["w_proj_conv_2"][0].rearrange("(k p) n -> p k n", p=P)
        w_pa = d["w_proj_attn_2"][0].rearrange("(k p) n -> p k n", p=P)
        w_out2 = d["w_out_2"][0].rearrange("(k p) n -> p k n", p=P)
        w_up2 = d["w_mlp_in_2"][0].rearrange("(k p) n -> p k n", p=P)
        w_ada = d["w_ada_2"][0].rearrange("(k p) n -> p k n", p=P)
        w_in = d["w_in"][0].rearrange("(k p) n -> p k n", p=P)
        w_out = d["w_out"][0].rearrange("(k p) n -> p k n", p=P)
        w_up = d["w_up"][0].rearrange("(k p) n -> p k n", p=P)
        w_down = d["w_down"][0].rearrange("(s p) n -> s p n", p=P)
        w_down2 = d["w_mlp_out_2"][0].rearrange("(s p) n -> s p n", p=P)
        x_tiles = d["x"][0].rearrange("(t p) d -> t p d", p=P)
        T_COLS = [(GATE_COL, HALF), (TAIL_COL, TAIL_W)]

        def half_view(n):
            return lambda raw: raw[:, 0:2 * n].rearrange("p (j n) -> p j n", j=2)

        def panel_view(raw):
            return raw[:, :].rearrange("p (k n) -> p k n", n=P)

        block = ctx.enter_context(nc.Block())

        @block.sync
        def _(sp):
            for t in range(NT):
                sp.dma_start(acc[:, t, :], x_tiles[t]).then_inc(sem(f"x_in{t}"), 16)
            for name, row, n in (("mix_pre_norm", V_MIXPRE, KD), ("ffn_pre_norm", V_FFNPRE, KD), ("q_norm", V_QN, 2),
                                 ("kv_norm", V_KVN, 1), ("g_pre_mix_2", V_GPREMIX2, KD),
                                 ("g_pre_mlp_2", V_GPREMLP2, KD)):
                sp.dma_start(vec_rows[row:row + n, :], d[name][0].rearrange("(k p) -> k p", p=P))\
                    .then_inc(sem("vec_in"), 16)
            sp.dma_start(vec_rows[V_CONV:V_CONV + CONV_W * GDN_PANELS, :],
                         d["conv_w"][0].rearrange("w (k p) -> (w k) p", p=P)).then_inc(sem("vec_in"), 16)
            sp.dma_start(vec_rows[V_CONV2:N_VEC, :],
                         d["conv_w_2"][0].rearrange("w (k p) -> (w k) p", p=P)).then_inc(sem("vec_in"), 16)
            sp.dma_start(vec2_rows[0:N_BADA, :], d["b_ada_2"][0].rearrange("(k p) -> k p", p=P))\
                .then_inc(sem("vec_in"), 16)
            sp.dma_start(vec2_rows[N_BADA:N_VEC2, :], d["c_2"][0].rearrange("(k p) -> k p", p=P))\
                .then_inc(sem("vec_in"), 16)
            sp.dma_start(a_log_b[:], d["a_log"][0].partition_broadcast(P)).then_inc(sem("gdn_vec_in"), 16)
            sp.dma_start(dt_b[:], d["dt_bias"][0].partition_broadcast(P)).then_inc(sem("gdn_vec_in"), 16)
            sp.dma_start(out_norm_row[:], d["gdn_out_norm"][0].partition_broadcast(P)).then_inc(sem("gdn_vec_in"), 16)

            sp.dma_start(pos_i[NOPE:P, :], d["positions"][0].partition_broadcast(P - NOPE)).then_inc(sem("pos_in"), 16)

            for c, (col, n) in enumerate(T_COLS):
                for j in range(4):
                    R1.load(sp, 0, 4 * c + j, half_view(n), w_in[:, 2 * j:2 * j + 2, col:col + n])
            R2.start(sp)
            with sp.Fori(0, GDN_PANELS // 3) as i:
                for j in range(3):
                    R2.load(sp, 3 * i, j, panel_view, w_in[:, :, bass.ds((3 * i + j) * P, P)])
            R2.panel_done(sp, 0, GDN_PANELS - 1)
            w_q_up = d["w_q_up"][0].rearrange("(k p) n -> p k n", p=P)
            sp.dma_start(w_kv[:], d["w_kv_up"][0]).then_inc(sem("w_kv_in"), 16)
            with sp.Fori(0, MLA_PAIRS) as i:
                for a in range(2):
                    c, half = (2 * i + a) * DQK, ROPE // 2
                    parts = ((wq[a][:, :, 0:DQK], w_q_up[:, :, bass.ds(c, DQK)]),
                             (wq[a][:, :, DQK:DQK + half], w_q_up[:, :, bass.ds(c + NOPE + half, half)]),
                             (wq[a][:, :, DQK + half:P], w_q_up[:, :, bass.ds(c + NOPE, half)]),
                             (wk[a][:], d["w_kv_up"][0][:, bass.ds((2 * i + a) * P, NOPE)]))
                    sp.wait_ge(sem("mla_proj"), 8 * i + (4 * a + 1))
                    for dst, src in parts:
                        sp.dma_start(dst, src).then_inc(sem(f"mla_w_in{a}"), 16)

            sp.wait_ge(sem("gdn_out_done"), NT)
            for t in range(NT):
                sp.dma_start(resid[:, t, :], x_tiles[t]).then_inc(sem(f"x_in{t}"), 16)
            sp.dma_start(post_row[:], d["mix_post_norm"][0].partition_broadcast(P)).then_inc(sem("post_gain_in"), 16)
            R3.start(sp)
            for c in range(2):
                for j in range(4):
                    R3.load(sp, 0, 4 * c + j, half_view(HALF), w_out[:, 2 * j:2 * j + 2, c * HALF:(c + 1) * HALF])

            def ffn_loads(ring, up, down):
                with sp.Fori(0, FFN_STEPS) as i:
                    for j in range(2):
                        ring.load(sp, 4 * i, j, panel_view, up[:, :, bass.ds((2 * i + j) * P, P)])
                    for j in range(2):
                        ring.load(sp, 4 * i, 2 + j, lambda raw: raw[:, :], down[2 * i + j])

            R4.start(sp)
            ffn_loads(R4, w_up, w_down)
            def w2_panel(col, j):
                return w_in2[:, :, bass.ds(col + j * P, P)]

            R5.start(sp)
            sp.wait_ge(sem("ada_used"), N_MOD * KD + 2)
            with sp.Fori(0, CONV2_PANELS) as i:
                for j in range(3):
                    R5.load(sp, 3 * i, j, panel_view, w2_panel(j * CONV2, i))

            def merge_loads(ring, gate_col, proj):
                with sp.Fori(0, KD // 2) as i:
                    for j in range(2):
                        ring.load(sp, 4 * i, 2 * j, panel_view, w2_panel(gate_col, 2 * i + j))
                        ring.load(sp, 4 * i, 2 * j + 1, lambda raw: raw[:, 0:HALF].rearrange("p (k n) -> p k n", n=P),
                                  proj[:, :, bass.ds((2 * i + j) * P, P)])

            R6.start(sp)
            sp.wait_ge(sem("c2_y_done"), CONV2_PANELS + 1)
            merge_loads(R6, IN2_GA, w_pc)
            for j in range(4):
                R7.load(sp, 0, j, half_view(HALF), w_in2[:, 2 * j:2 * j + 2, IN2_V:IN2_V + HALF])
            R8.start(sp)
            with sp.Fori(0, SB_HEADS // 2) as i:
                R8.load(sp, 2 * i, 0, panel_view, w2_panel(IN2_Q, i))
                R8.load(sp, 2 * i, 1, panel_view, w2_panel(IN2_K, i))
            R9.start(sp)
            sp.wait_ge(sem("sb_o_done"), SB_HEADS + 2)
            merge_loads(R9, IN2_GB, w_pa)
            for c in range(2):
                for j in range(4):
                    R10.load(sp, 0, 4 * c + j, half_view(HALF), w_out2[:, 2 * j:2 * j + 2, c * HALF:(c + 1) * HALF])
            ffn_loads(R11, w_up2, w_down2)

            out_tiles = out[0].rearrange("(t p) d -> t p d", p=P)
            for t in range(NT):
                sp.wait_ge(sem("resid_done"), 3 * NT + t + 1)
                sp.dma_start(out_tiles[t], resid[:, t, :]).then_inc(sem("out_stored"), 16)
            sp.wait_ge(sem("out_stored"), NT * 16)

        @block.gpsimd
        def _(pool):
            R1.credit(pool)
            pool.sem_inc(sem("conv_done"), 1)
            pool.sem_inc(sem("conv_in_done"), 2)
            pool.sem_inc(sem("ss_gdn_done"), 2)
            for name, credit in (("mla_proj", 5), ("mla_proj_read", 1), ("mla_o_done", 1), ("mla_pv", 2),
                                 ("mla_exp_done", 2)):
                pool.sem_inc(sem(name), credit)
            pool.sem_inc(sem("ffn_hid"), FFN_CREDIT)
            for name, credit in (("kk_prod", 1), ("o_taken", 1), ("o_ss_done", 1), ("ada_used", 2), ("ada_read", 1), ("c2_cg_read", 1), ("c2_v_done", 1), ("c2_y_done", 1),
                                 ("m_gate_read", 2), ("m_done", 2), ("sb_z_done", 2), ("sb_o_done", 2), ("sb_pv", 2)):
                pool.sem_inc(sem(name), credit)
            pch = Chain(pool, sem("pool_chain"))
            pch.link(pool.memset(half_neg[:], -0.5))

            def norm_rstd(tag):
                b = NORMS.index(tag)
                for h in range(2):
                    pool.wait_ge(sem("norm_sq_done"), NT * b + 4 * h + 4)
                    pool.tensor_scalar(mean_sq[:, 4 * h:4 * h + 4], ssq[:, 4 * h:4 * h + 4], 1.0 / D, EPS,
                                       ALU.mult, ALU.add).then_inc(sem("norm_mean_done"), 1)
                    pool.wait_ge(sem("norm_mean_done"), 2 * b + h + 1)
                    pool.tensor_tensor(rstd[:, 4 * h:4 * h + 4], mean_sq[:, 4 * h:4 * h + 4], half_neg[:, 0:4],
                                       ALU.pow).then_inc(sem("norm_rstd_done"), 1)

            norm_rstd("n1")
            for c, (col, n) in enumerate(T_COLS):
                for j in range(4):
                    R1.split(pool, 0, (4 * c + j) // R1.nraw, 4 * c + j, 2 * n)
            R2.start_split(pool)
            for j in range(3):
                R2.split(pool, 0, 0, j)
            pool.wait_ge(sem("lat_sq_done"), 2 * NT)
            pool.tensor_scalar(lat_ms[:, 0:NT], lat_ss[:, 0:NT], 1.0 / Q_RANK, EPS, ALU.mult, ALU.add)
            pch.link(pool.tensor_scalar(lat_ms[:, NT:], lat_ss[:, NT:], 1.0 / KV_RANK, EPS, ALU.mult, ALU.add))
            pool.tensor_tensor(lat_rstd[:], lat_ms[:], half_neg[:, 0:2 * NT], ALU.pow).then_inc(sem("lat_rstd_done"), 1)
            with pool.Fori(0, GDN_PANELS // 3 - 1) as i:
                for j in range(3):
                    R2.split(pool, 3 * i + 3, i + 1, j)
            pool.wait_ge(sem("ss_gdn_done"), GDN_PANELS + 2)
            pool.tensor_scalar(g_rq[:], ss_gdn[:, :, 1:1 + GDN_HEADS], float(P), 4 * EPS * P, ALU.mult, ALU.add)
            pch.link(pool.tensor_scalar(g_rk[:], ss_gdn[:, :, 1 + GDN_HEADS:1 + 2 * GDN_HEADS], 1.0, 4 * EPS,
                                        ALU.mult, ALU.add))
            expo = half_neg[:, 0:NT * GDN_HEADS].rearrange("p (t h) -> p t h", h=GDN_HEADS)
            pool.tensor_tensor(g_rk[:], g_rk[:], expo, ALU.pow).then_inc(sem("qk_norm_done"), 1)
            pool.tensor_tensor(g_rq[:], g_rq[:], expo, ALU.pow).then_inc(sem("qk_norm_done"), 1)

            def each_head(mask):
                return consts[:, mask:mask + P].unsqueeze(1).broadcast_to([P, GDN_HEADS, P])

            def by_head(cols):
                return cols.unsqueeze(2).broadcast_to([P, GDN_HEADS, P])

            def gdn_rows(i):
                for a in range(2):
                    la, bk = g_la[:, 2 * i + a, :], g_bk[:, 2 * i + a, :]
                    pool.wait_ge(sem("kk_prod"), 2 * i + a + 1)
                    pool.sem_inc(sem("wait_carrier"), 1)
                    pool.tensor_tensor(u_g[:], each_head(C_CSUM), by_head(la), ALU.mult)
                    pool.tensor_tensor(i_b[:], each_head(C_ID), by_head(bk), ALU.mult).then_inc(sem("gdn_rows_in"), 1)

            def gdn_levels(i, n):
                for a in range(2):
                    if n >= 3:
                        pool.wait_ge(sem("y_prod"), 10 * i + (2 * (n - 3) + a + 1))
                    pool.wait_ge(sem("a_t_done"), 2 * i + a + 1)
                    pool.tensor_tensor(m_s[n % 2][a][:], a_t[a][:], each_head(C_LEVEL + n * P), ALU.mult)\
                        .then_inc(sem("level_done"), 1)

            def gdn_decayed_state(i, k):
                a, c = k // 2, k % 2
                pool.wait_ge(sem("e_last_done"), 2 * i + 2)
                pool.wait_ge(sem("state_done"), 4 * i + k + 1)
                pool.tensor_tensor(s_dec[:], state[c][:], e_last[a][:, :, c:c + 1].broadcast_to([P, GDN_HEADS, P]),
                                   ALU.mult).then_inc(sem("s_dec_done"), 1)

            def gdn_out_rstd(i, a):
                pool.wait_ge(sem("o_ss_done"), 2 * i + a + 2)
                pool.sem_inc(sem("wait_carrier"), 1)
                pool.tensor_scalar(o_ms[:], o_ss[:], 1.0 / P, EPS, ALU.mult, ALU.add).then_inc(sem("o_ms_done"), 1)
                pool.wait_ge(sem("o_ms_done"), 2 * i + a + 1)
                pool.tensor_tensor(o_rstd[:], o_ms[:], half_neg[:, 0:GDN_HEADS], ALU.pow).then_inc(sem("o_rstd_done"), 1)

            def gdn_pair(i, before):
                gdn_rows(i)
                for n in range(1, 3):
                    gdn_levels(i, n)
                for a in range(2):
                    pool.wait_ge(sem("a_t_done"), 2 * i + a + 1)
                    pool.tensor_tensor(e_d[a][:], e_d[a][:], each_head(C_CSUM), ALU.mult).then_inc(sem("p_decay_done"), 1)
                for n in range(1, 5):
                    if before is not None:
                        gdn_decayed_state(before, n - 1)
                    if n >= 2:
                        gdn_levels(i, n + 1)
                    if before is not None and n == 4:
                        gdn_out_rstd(before, 0)
                if before is not None:
                    gdn_out_rstd(before, 1)

            pool.wait_ge(sem("g_scales_done"), 1)
            gdn_pair(0, None)
            with pool.Fori(0, GDN_PAIRS - 1) as i:
                gdn_pair(i + 1, i)
            for k in range(4):
                gdn_decayed_state(GDN_PAIRS - 1, k)
                if k % 2:
                    gdn_out_rstd(GDN_PAIRS - 1, k // 2)

            R3.start_split(pool)
            for j in range(8):
                R3.split(pool, 0, j // 4, j)
            norm_rstd("mix_post")
            norm_rstd("n2")

            def ffn_splits(ring):
                with pool.Fori(0, FFN_STEPS) as i:
                    for j in range(4):
                        ring.split(pool, 4 * i, (4 // ring.nraw) * i + j // ring.nraw, j)

            R4.start_split(pool)
            ffn_splits(R4)
            norm_rstd("ffn_post")
            norm_rstd("n3")
            R5.start_split(pool)
            with pool.Fori(0, CONV2_PANELS) as i:
                for j in range(3):
                    R5.split(pool, 3 * i, i, j)

            def merge_splits(ring):
                with pool.Fori(0, KD // 2) as i:
                    for j in range(4):
                        ring.split(pool, 4 * i, i, j, 1024 if j % 2 == 0 else HALF)

            R6.start_split(pool)
            pool.wait_ge(sem("c2_split"), CONV2_PANELS)
            merge_splits(R6)
            for j in range(4):
                R7.split(pool, 0, 0, j)
            R8.start_split(pool)
            with pool.Fori(0, SB_HEADS // 2) as i:
                for j in range(2):
                    R8.split(pool, 2 * i, i, j)
            R9.start_split(pool)
            pool.wait_ge(sem("sb_o_done"), SB_HEADS + 2)
            merge_splits(R9)
            for j in range(8):
                R10.split(pool, 0, j // 4, j)
            norm_rstd("mix_post2")
            norm_rstd("n4")
            ffn_splits(R11)
            norm_rstd("ffn_post2")

        @block.tensor
        def _(pe):
            def turn(tag, src, ready, nk=KD):
                base = TURNS[tag]
                for h in range(2):
                    for k in range(nk):
                        n = h * nk + k
                        ready(h)
                        if n >= 4:
                            pe.wait_ge(sem("turn_read"), base + n - 3)
                        for j in range(4):
                            mm = pe.transpose(ps[:, n % 4, j * P:(j + 1) * P],
                                              src[:, 4 * h + j, k * P:(k + 1) * P], ident)
                        mm.then_inc(sem("turned"), 1)

            def scaled(tag, t):
                pe.wait_ge(sem("norm_scaled"), NT * SCALES.index(tag) + t + 1)

            def turn_done(tag, nk=KD):
                base = TURNS[tag]
                pe.wait_ge(sem("turn_read"), base + 2 * nk)
                pe.wait_ge(sem("turn_split"), base + 2 * nk)

            def panel(hi, lo, a_hi, a_lo, banks, nk, done, halves=(0, 1)):
                for h in halves:
                    o = ps[:, banks[h], :]
                    cols = slice(h * HALF, (h + 1) * HALF)
                    for k in range(nk):
                        w = slice(k * P, (k + 1) * P)
                        pe.matmul(o, hi[:, w], a_hi[:, k, cols], start=(k == 0), stop=False)
                        pe.matmul(o, hi[:, w], a_lo[:, k, cols], start=False, stop=False)
                        mm = pe.matmul(o, lo[:, w], a_hi[:, k, cols], start=False, stop=(k == nk - 1))
                    if done[h]:
                        mm.then_inc(done[h], 1)

            def token_chunk(ring, n0, width, a_hi, a_lo, bank_free, done):
                for j in range(4):
                    ring.ready(pe, 0, n0 + j)
                    hi, lo = ring.hi[(n0 + j) % ring.nslab], ring.lo[(n0 + j) % ring.nslab]
                    for t in range(NT):
                        o = ps[:, t, 0:width]
                        if j == 0:
                            bank_free(t)
                        for m in range(2):
                            k = 2 * j + m
                            w = slice(m * width, (m + 1) * width)
                            a = slice(t * P, (t + 1) * P)
                            pe.matmul(o, a_hi[:, k, a], hi[:, w], start=(k == 0), stop=False)
                            pe.matmul(o, a_lo[:, k, a], hi[:, w], start=False, stop=False)
                            mm = pe.matmul(o, a_hi[:, k, a], lo[:, w], start=False, stop=(k == KD - 1))
                        if t == NT - 1:
                            mm.then_inc(ring.used, 1)
                        elif j == 3:
                            mm.then_inc(done, 1)

            pe.wait_ge(sem("consts_in"), 16)
            pe.wait_ge(sem("vec_in"), 160)
            pe.transpose(ps[:, 4, 0:N_VEC], vec_rows[0:N_VEC, :], consts[0:N_VEC, C_ID:C_ID + N_VEC])
            pe.transpose(ps[:, 4, 256:256 + N_VEC2], vec2_rows[0:N_VEC2, :], consts[0:N_VEC2, C_ID:C_ID + N_VEC2])\
                .then_inc(sem("vec_turned"), 1)
            turn("n1", acc, lambda h: scaled("n1", 4 * h + 3))
            turn_done("n1")
            pe.wait_ge(sem("vec_cols_done"), 2)
            token_chunk(R1, 0, HALF, act_hi, act_lo, lambda t: None, sem("gate_prod"))
            token_chunk(R1, 4, TAIL_W, act_hi, act_lo, lambda t: pe.wait_ge(sem("gate_silu"), t + 1), sem("tail_prod"))
            pe.wait_ge(sem("lat_done"), NT)
            with pe.Fori(0, GDN_PANELS // 3) as i:
                for j in range(3):
                    p = 3 * i + j
                    R2.ready(pe, 3 * i, j)
                    pe.wait_ge(sem("conv_in_done"), p + 1)
                    b = 2 * j
                    panel(R2.hi[j], R2.lo[j], act_hi, act_lo, (b, b + 1), KD, (sem("qkv_half"), R2.used))
                    pe.wait_ge(sem("conv_sq_done"), p + 1)
                    pe.wait_ge(sem("ss_gdn_done"), p + 2)
                    for t in range(NT):
                        mm = pe.matmul(ps[:, 6, t:t + 1], conv_t[:, t * P:(t + 1) * P], ones[:, 0:1],
                                       start=True, stop=True)
                    mm.then_inc(sem("ss_prod"), 1)
            pe.wait_ge(sem("lat_norm_done"), 1)
            for n, b in enumerate(LAT_BANKS):
                kind, h = n // 2, n % 2
                c0 = (LAT_CQ, LAT_CQ + P, LAT_CKV, TAIL_W + ROPE - P)[kind]
                if b == 6:
                    pe.wait_ge(sem("ss_gdn_done"), GDN_PANELS + 2)
                elif b < 6:
                    pe.wait_ge(sem("conv_in_done"), GDN_PANELS + b // 2)
                for j in range(4):
                    mm = pe.transpose(ps[:, b, j * P:(j + 1) * P], lat[:, 4 * h + j, c0:c0 + P], ident)
                mm.then_inc(sem("lat_turned"), 1)
            pe.wait_ge(sem("w_kv_in"), 16)
            pe.wait_ge(sem("lat_feat_done"), 6)
            pe.wait_ge(sem("mla_k_rope_done"), 1)
            w_v = w_kv[:].rearrange("p (h c) -> p h c", c=P)[:, :, NOPE:P]
            for t in range(NT):
                pe.matmul(ps[:, t, :].rearrange("p (h e) -> p h e", e=V_DIM), ckv_f[:, t * P:(t + 1) * P], w_v,
                          start=True, stop=True).then_inc(sem("v_prod"), 1)
            pe.wait_ge(sem("log_a_done"), 1)
            pe.wait_ge(sem("v_done"), NT)
            n_gh = NT * GDN_HEADS
            la = g_la[:].rearrange("p t h -> p (t h)")
            pe.matmul(ps[:, 0, 0:n_gh], consts[:, C_CSUM:C_CSUM + P], la, start=True, stop=True)
            pe.matmul(ps[:, 0, n_gh:2 * n_gh], consts[:, C_CHUNK:C_CHUNK + P], la, start=True, stop=True)\
                .then_inc(sem("cumsum_prod"), 1)
            pe.wait_ge(sem("cumsum_done"), 2)

            def mla_project(i, h, n):
                a, cols = h % 2, slice(n % 2 * HALF, (n % 2 + 1) * HALF)
                if n == 0:
                    pe.wait_ge(sem(f"mla_w_in{a}"), 64 * i + (64 * (h // 2) + 64))
                pe.wait_ge(sem("mla_proj_read"), 8 * i + (4 * h + n + 1))
                if n == 1 or n == 2:
                    pe.wait_ge(sem("mla_rope_done"), 4 * i + (2 * h + n))
                if n < 2:
                    for k in range(2):
                        mm = pe.matmul(ps[:, 7, :], wq[a][:, k, :], cq_f[:, k, cols], start=(k == 0), stop=(k == 1))
                else:
                    mm = pe.matmul(ps[0:NOPE, 7, :], wk[a][:], ckv_f[:, cols], start=True, stop=True)
                mm.then_inc(sem("mla_proj"), 1)

            def mla_scores(i, s):
                t, a = s % NT, s // NT
                n = (t + 1) * P
                if t == 0:
                    pe.wait_ge(sem("mla_proj_read"), 8 * i + (4 * a + 5))
                    pe.wait_ge(sem("mla_rope_done"), 4 * i + (2 * a + 2))
                pe.wait_ge(sem("mla_exp_done"), MLA_ITEMS * i + s + 1)
                for f in range((n + HALF - 1) // HALF):
                    w = min(HALF, n - f * HALF)
                    mm = pe.matmul(ps[:, 2 * (s % 2) + f, 0:w], q_f[a][0:DQK, t * P:(t + 1) * P],
                                   k_f[a][0:DQK, f * HALF:f * HALF + w], start=True, stop=True)
                mm.then_inc(sem("mla_scores"), 1)

            def mla_turn(i, s):
                pe.wait_ge(sem("mla_exp_done"), MLA_ITEMS * i + (s + 3))
                for n, g in enumerate(mla_groups(s)):
                    for b in range(4 * n, min(4 * n + 4, s % NT + 1)):
                        mm = pe.transpose(ps[:, 4 + g % 2, (b % 4) * P:(b % 4 + 1) * P],
                                          probs[s % PROBS][:, b * P:(b + 1) * P], ident)
                    mm.then_inc(sem("mla_turned"), 1)

            def mla_outputs(i, s):
                t, a = s % NT, s // NT
                if t == 0:
                    pe.wait_ge(sem("mla_o_done"), 2 * i + (a + 1))
                for n, g in enumerate(mla_groups(s)):
                    pe.wait_ge(sem("mla_pt_done"), MLA_GROUPS * i + (g + 1))
                    for b in range(4 * n, min(4 * n + 4, t + 1)):
                        mm = pe.matmul(ps[:, 6, t * V_DIM:(t + 1) * V_DIM], probs_t[g % 2][:, (b % 4) * P:(b % 4 + 1) * P],
                                       v_t[:, b, 2 * i + a, :], start=(b == 0), stop=(b == t))
                    mm.then_inc(sem("mla_pv"), 1)

            def mla_pair(i, before, last):
                for s in range(MLA_ITEMS):
                    if s + 1 < MLA_ITEMS:
                        mla_scores(i, s + 1)
                    elif not last:
                        mla_scores(i + 1, 0)
                    if late := lagged(i, before, s, MLA_LAG_PV, MLA_ITEMS):
                        mla_outputs(*late)
                    if late := lagged(i, before, s, MLA_LAG_TURN, MLA_ITEMS):
                        mla_turn(*late)
                    if 1 <= s <= 4:
                        mla_project(i, 1, s - 1)
                    elif 8 <= s <= 11 and not last:
                        mla_project(i, 2, s - 8)

            pe.wait_ge(sem("mla_k_rope_done"), 2)
            for n in range(4):
                mla_project(0, 0, n)
            mla_scores(0, 0)
            mla_pair(0, None, False)
            with pe.Fori(0, MLA_PAIRS - 2) as i:
                mla_pair(i + 1, i, False)
            mla_pair(MLA_PAIRS - 1, MLA_PAIRS - 2, True)
            for s in range(MLA_ITEMS, MLA_ITEMS + MLA_LAG_PV):
                mla_outputs(MLA_PAIRS - 1, s - MLA_LAG_PV)
                if s < MLA_ITEMS + MLA_LAG_TURN:
                    mla_turn(MLA_PAIRS - 1, s - MLA_LAG_TURN)

            def heads(bank, lhs, rhs, signal=None):
                for h in range(GDN_HEADS):
                    mm = pe.matmul(ps[:, bank, h * P:(h + 1) * P], lhs(h), rhs(h), start=True, stop=True)
                if signal:
                    mm.then_inc(sem(signal), 1)

            def turn_heads(bank, src, signal):
                for h in range(GDN_HEADS):
                    mm = pe.transpose(ps[:, bank, h * P:(h + 1) * P], src[:, h, :], ident)
                mm.then_inc(sem(signal), 1)

            def gdn_grams(i):
                for a, (b_g, b_b, b_k) in enumerate(((0, 1, 2), (3, 4, 0))):
                    pe.wait_ge(sem("gdn_rows_in"), 2 * i + a + 1)
                    pe.matmul(ps[:, b_g, :], ones, u_g[:].rearrange("p h t -> p (h t)"), start=True, stop=True)\
                        .then_inc(sem("g_row_prod"), 1)
                    pe.matmul(ps[:, b_b, :], consts[:, C_STRICT:C_STRICT + P], i_b[:].rearrange("p h t -> p (h t)"),
                              start=True, stop=True)
                    pe.wait_ge(sem("gdn_k_in"), 2 * i + a + 1)
                    if a:
                        pe.wait_ge(sem("decay_arg_done"), 2 * i + 1)
                    heads(b_k, lambda h: k_s[a][:, h, :], lambda h: k_s[a][:, h, :], "kk_prod")

            def gdn_state_products(i, k):
                a, rows = k // 2, slice(k % 2 * CHUNK, (k % 2 + 1) * CHUNK)
                pe.wait_ge(sem("state_done"), 4 * i + k + 1)
                pe.wait_ge(sem("wu_done"), 4 * i + 2 * a + 2)
                for h in range(GDN_HEADS):
                    mm = pe.matmul(ps[rows, 5, h * P:(h + 1) * P], w_t[a][:, h, rows], state[k % 2][:, h, :],
                                   start=True, stop=True)
                mm.then_inc(sem("ws_prod"), 1)

            def gdn_state_update(i, k):
                a, c, rows = k // 2, k % 2, slice(k % 2 * CHUNK, (k % 2 + 1) * CHUNK)
                pe.wait_ge(sem("v_new_done"), 4 * i + k + 1)
                for h in range(GDN_HEADS):
                    mm = pe.matmul(ps[:, 5, h * P:(h + 1) * P], k_d[a][rows, h, :], v_n[rows, h, :], start=True, stop=True)
                mm.then_inc(sem("ds_prod"), 1)
                if c == 0:
                    pe.wait_ge(sem("o_taken"), 2 * i + a + 1)
                for h in range(GDN_HEADS):
                    o = ps[rows, 6, h * P:(h + 1) * P]
                    pe.matmul(o, q_d[a][:, h, rows], state[c][:, h, :], start=True, stop=False)
                    mm = pe.matmul(o, p_t[a][rows, h, rows], v_n[rows, h, :], start=False, stop=True)
                if c:
                    mm.then_inc(sem("o_prod"), 1)

            def gdn_turns(i, a):
                for bank, n in ((3, 1), (7, 2), (5, 3)):
                    if a:
                        pe.wait_ge(sem("gdn_turn_read"), 6 * i + n)
                    if bank == 3:
                        turn_heads(bank, k_s[a], "gdn_turned")
                    elif bank == 7:
                        turn_heads(bank, v_s[a], "gdn_turned")
                    else:
                        cols = bass.ds((2 * i + a) * P, P)
                        heads(bank, lambda h: k_s[a][:, h, :], lambda h: qkv[:, h, cols], "gdn_turned")

            def gdn_pair(i, before):
                if before is not None:
                    pe.wait_ge(sem("wu_done"), 4 * i)
                    pe.wait_ge(sem("gdn_turn_read"), 6 * i)
                gdn_grams(i)
                for a in range(2):
                    pe.wait_ge(sem("tr0_done"), 2 * i + a + 1)
                    turn_heads(1 + a, t_r[0][a], "t0_turned")
                for n in range(1, len(LEVELS)):
                    old, last = (n - 1) % 2, n == len(LEVELS) - 1
                    if before is not None and not last:
                        gdn_state_products(before, n - 1)
                    for a in range(2):
                        pe.wait_ge(sem("level_done"), 10 * i + (2 * (n - 1) + a + 1))
                        if n == 1:
                            pe.wait_ge(sem("t0_done"), 2 * i + a + 1)
                        else:
                            pe.wait_ge(sem("t_done"), 8 * i + (2 * (n - 2) + a + 1))
                        heads(a, lambda h: m_s[n % 2][a][:, h, :], lambda h: t_f[old][a][:, h, :], "y_prod")
                    if before is not None and not last:
                        gdn_state_update(before, n - 1)
                    if last:
                        if before is not None:
                            pe.wait_ge(sem("state_done"), 4 * i + 1)
                        gdn_turns(i, 0)
                    for a in range(2):
                        pe.wait_ge(sem("y_done"), 10 * i + (2 * (n - 1) + a + 1))
                        heads(2 + 2 * a, lambda h: y_s[a][:, h, :], lambda h: t_r[old][a][:, h, :], "zt_prod")
                        if not last:
                            heads(3 + 4 * a, lambda h: t_r[old][a][:, h, :], lambda h: y_s[a][:, h, :], "z_prod")
                gdn_turns(i, 1)
                for a in range(2):
                    pe.wait_ge(sem("t_last_done"), 2 * i + a + 1)
                    pe.wait_ge(sem("gdn_turn_read"), 6 * i + 3 * a + 3)
                    heads(2 * a, lambda h: k_w[a][:, h, :], lambda h: t_r[1][a][:, h, :], "wu_prod")
                    heads(1 + 3 * a, lambda h: t_r[1][a][:, h, :], lambda h: v_b[a][:, h, :], "wu_prod")

            gdn_pair(0, None)
            with pe.Fori(0, GDN_PAIRS - 1) as i:
                gdn_pair(i + 1, i)
            for k in range(4):
                gdn_state_products(GDN_PAIRS - 1, k)
                gdn_state_update(GDN_PAIRS - 1, k)

            turn("mixt", mix, lambda h: pe.wait_ge(sem("gdn_out_done"), NT))
            turn_done("mixt")
            token_chunk(R3, 0, HALF, mixt_hi, mixt_lo, lambda t: None, sem("mixed_prod"))
            token_chunk(R3, 4, HALF, mixt_hi, mixt_lo, lambda t: pe.wait_ge(sem("mixed_done"), t + 1), sem("mixed_prod"))

            def ffn(ring, run):
                with pe.Fori(0, FFN_STEPS) as i:
                    for j in range(2):
                        ring.ready(pe, 4 * i, j)
                        if j == 0 and run == 0:
                            pe.wait_ge(sem("ada_read"), i + 1)
                        panel(ring.hi[j], ring.lo[j], act_hi, act_lo, (2 * j, 2 * j + 1), KD,
                              (sem("ffn_half"), ring.used))

                    def down(g, j, stop):
                        t, f = g // 2, g % 2
                        o, a, c = ps[:, 4 + g % 4, :], slice(t * P, (t + 1) * P), slice(f * HALF, (f + 1) * HALF)
                        pe.matmul(o, hid_hi[:, j, a], ring.hi[2 + j][:, c], start=(j == 0), stop=False)
                        pe.matmul(o, hid_lo[:, j, a], ring.hi[2 + j][:, c], start=False, stop=False)
                        return pe.matmul(o, hid_hi[:, j, a], ring.lo[2 + j][:, c], start=False, stop=stop)

                    ring.ready(pe, 4 * i, 2)
                    pe.wait_ge(sem("ffn_hid"), 4 * i + (4 * FFN_STEPS * run + 2 + FFN_CREDIT))
                    for g in range(4):
                        pe.wait_ge(sem("ffn_acc"), 16 * i + ((16 * FFN_STEPS + 4) * run + g + 1))
                        down(g, 0, False)
                    ring.ready(pe, 4 * i, 3)
                    pe.wait_ge(sem("ffn_hid"), 4 * i + (4 * FFN_STEPS * run + 4 + FFN_CREDIT))
                    def modulation(j):
                        pe.wait_ge(sem(f"ada_in{j % 2}"), (32 if j % 2 == 0 else 16) * i + (j // 2 + 1) * 16)
                        for k in range(KD):
                            mm = pe.matmul(ps[:, 0, j:j + 1], ada[j % 2][:, k, :], vec2[:, N_BADA + k:N_BADA + k + 1],
                                           start=(k == 0), stop=(k == KD - 1))
                        mm.then_inc(sem("ada_used"), 1)

                    if run == 0:
                        modulation(0)
                        modulation(1)
                    for g in range(16):
                        if g == 12 and run == 0:
                            modulation(2)
                        if g >= 4:
                            pe.wait_ge(sem("ffn_acc"), 16 * i + ((16 * FFN_STEPS + 4) * run + g + 1))
                            mm = down(g, 0, False)
                            if g == 15:
                                mm.then_inc(ring.used, 1)
                        mm = down(g, 1, True)
                        mm.then_inc(ring.used if g == 15 else sem("ffn_down"), 1)

            turn("n2", acc, lambda h: scaled("n2", 4 * h + 3))
            turn_done("n2")
            ffn(R4, 0)
            turn("n3", acc, lambda h: scaled("n3", 4 * h + 3))
            turn_done("n3")
            with pe.Fori(0, CONV2_PANELS) as i:
                for j, free in enumerate(("c2_y_done", "c2_cg_read", "c2_v_done")):
                    R5.ready(pe, 3 * i, j)
                    pe.wait_ge(sem(free), i + 1)
                    panel(R5.hi[j], R5.lo[j], act_hi, act_lo, (2 * j, 2 * j + 1), KD, (None, R5.used))

            def merge(ring, run, a_hi, a_lo, ready):
                with pe.Fori(0, KD // 2) as i:
                    for j in range(2):
                        b = 4 * j
                        ring.ready(pe, 4 * i, 2 * j)
                        pe.wait_ge(sem("m_gate_read"), 2 * i + (KD * run + j + 1))
                        panel(ring.hi[2 * j], ring.lo[2 * j], act_hi, act_lo, (b, b + 1), KD, (None, ring.used))
                        ring.ready(pe, 4 * i, 2 * j + 1)
                        if j == 0:
                            ready()
                        pe.wait_ge(sem("m_done"), 2 * i + (KD * run + j + 1))
                        panel(ring.hi[2 * j + 1], ring.lo[2 * j + 1], a_hi, a_lo, (b + 2, b + 3), CONV2_PANELS,
                              (None, ring.used))

            merge(R6, 0, y_hi, y_lo, lambda: pe.wait_ge(sem("c2_split"), CONV2_PANELS))
            pe.wait_ge(sem("m_done"), KD + 2)
            token_chunk(R7, 0, HALF, act_hi, act_lo, lambda t: None, sem("v2_prod"))
            pe.wait_ge(sem("v2_done"), NT)

            def sb_project(i, j, halves=(0, 1)):
                if halves[0] == 0:
                    R8.ready(pe, 2 * i, j)
                panel(R8.hi[j], R8.lo[j], act_hi, act_lo, (2 * j, 2 * j + 1), KD, (None, R8.used), halves)

            def sb_scores(i, s):
                t, rows = s // 2, slice(s % 2 * SB_DIM, (s % 2 + 1) * SB_DIM)
                n = (t + 1) * P
                pe.wait_ge(sem("sb_z_done"), SB_ITEMS * i + s + 1)
                for f in range((n + HALF - 1) // HALF):
                    w = min(HALF, n - f * HALF)
                    mm = pe.matmul(ps[:, 2 * (s % 2) + f, 0:w], q2[rows, t * P:(t + 1) * P],
                                   k2[rows, f * HALF:f * HALF + w], start=True, stop=True)
                mm.then_inc(sem("sb_scores"), 1)

            def sb_turn(i, s):
                pe.wait_ge(sem("sb_weights_done"), SB_ITEMS * i + s + 1)
                for n, g in enumerate(sb_groups(s)):
                    for b in range(4 * n, min(4 * n + 4, s // 2 + 1)):
                        mm = pe.transpose(ps[:, 4 + g % 2, (b % 4) * P:(b % 4 + 1) * P],
                                          sb_a[s % 3][:, b * P:(b + 1) * P], ident)
                    mm.then_inc(sem("sb_turned"), 1)

            def sb_outputs(i, s):
                t, half = s // 2, s // NT
                if s % NT == 0:
                    pe.wait_ge(sem("sb_o_done"), 2 * i + half + 1)
                for n, g in enumerate(sb_groups(s)):
                    pe.wait_ge(sem("sb_at_done"), SB_GROUPS * i + g + 1)
                    for b in range(4 * n, min(4 * n + 4, t + 1)):
                        mm = pe.matmul(ps[:, 6 + half, s % NT * SB_DIM:(s % NT + 1) * SB_DIM],
                                       sb_at[g % 2][:, (b % 4) * P:(b % 4 + 1) * P], v2[:, b, 2 * i + s % 2, :],
                                       start=(b == 0), stop=(b == t))
                    mm.then_inc(sem("sb_pv"), 1)

            def sb_pair(i, last):
                pe.wait_ge(sem("sb_qk_done"), 2 * i + 2)
                sb_scores(i, 0)
                for s in range(SB_ITEMS + SB_LAG_PV):
                    if s + 1 < SB_ITEMS:
                        sb_scores(i, s + 1)
                    if s >= SB_ITEMS and not last:
                        if s == SB_ITEMS:
                            pe.wait_ge(sem("sb_z_done"), SB_ITEMS * i + SB_ITEMS + 2)
                        sb_project(i + 1, (s - SB_ITEMS) // 2, ((s - SB_ITEMS) % 2,))
                    if s >= SB_LAG_PV:
                        sb_outputs(i, s - SB_LAG_PV)
                    if SB_LAG_TURN <= s < SB_ITEMS + SB_LAG_TURN:
                        sb_turn(i, s - SB_LAG_TURN)

            sb_project(0, 0)
            sb_project(0, 1)
            with pe.Fori(0, SB_PAIRS - 1) as i:
                sb_pair(i, False)
            sb_pair(SB_PAIRS - 1, True)

            turn("sb_o", o2, lambda h: pe.wait_ge(sem("sb_o_done"), SB_HEADS + 2), CONV2_PANELS)
            turn_done("sb_o", CONV2_PANELS)
            merge(R9, 1, o2_hi, o2_lo, lambda: None)

            pe.wait_ge(sem("merged_split"), KD)
            token_chunk(R10, 0, HALF, act_hi, act_lo, lambda t: None, sem("mixed_prod"))
            token_chunk(R10, 4, HALF, act_hi, act_lo, lambda t: pe.wait_ge(sem("mixed_done"), 2 * NT + t + 1),
                        sem("mixed_prod"))

            def gate_row(run):
                pe.wait_ge(sem("gate_diag_done"), run + 1)
                for f in range(2):
                    mm = pe.matmul(ps[:, f, :], ones, diag[:, 4 * f:4 * f + 4, :].rearrange("p k n -> p (k n)"),
                                   start=True, stop=True)
                mm.then_inc(sem("gate_row_prod"), 1)

            pe.wait_ge(sem("mixed_done"), 4 * NT)
            gate_row(0)
            turn("n4", acc, lambda h: scaled("n4", 4 * h + 3))
            turn_done("n4")
            ffn(R11, 1)
            gate_row(1)

        @block.scalar
        def _(act):
            act.dma_start(consts[:], d["consts"]).then_inc(sem("consts_in"), 16)

            def norm_square(src, junk, ready):
                for t in range(NT):
                    ready(t)
                    act.activation(junk[:, t, :], src[:, t, :], ACT.Square, accum_out=ssq[:, t:t + 1])\
                        .then_inc(sem("norm_sq_done"), 1)

            def norm_scale(tag, src, dst):
                for t in range(NT):
                    act.wait_ge(sem("norm_rstd_done"), 2 * NORMS.index(tag) + t // 4 + 1)
                    act.activation(dst[:, t, :], src[:, t, :], ACT.Copy, scale=rstd[:, t:t + 1])\
                        .then_inc(sem("norm_scaled"), 1)

            def norm_full(tag, scale=None, bias=None, nk=KD):
                base = TURNS[tag]
                for n in range(2 * nk):
                    k = n % nk
                    act.wait_ge(sem("turned"), base + n + 1)
                    if base + n >= 2:
                        act.wait_ge(sem("turn_split"), base + n - 1)
                    if bias:
                        ins = act.activation(norm_tmp[n % 2][:], ps[:, n % 4, :], ACT.Identity, bias=bias(k),
                                             scale=scale(k))
                    elif scale:
                        ins = act.activation(norm_tmp[n % 2][:], ps[:, n % 4, :], ACT.Copy, scale=scale(k))
                    else:
                        ins = act.copy(norm_tmp[n % 2][:], ps[:, n % 4, :])
                    ins.then_inc(sem("turn_read"), 1)

            norm_square(acc, resid, lambda t: act.wait_ge(sem(f"x_in{t}"), 16))
            act.wait_ge(sem("vec_turned"), 1)
            act.copy(vec[:], ps[:, 4, 0:N_VEC]).then_inc(sem("vec_cols_done"), 1)
            act.copy(vec2[:], ps[:, 4, 256:256 + N_VEC2]).then_inc(sem("vec_cols_done"), 1)
            norm_scale("n1", acc, acc)
            act.wait_ge(sem("vec_cols_done"), 2)
            norm_full("n1", lambda k: vec[:, V_MIXPRE + k:V_MIXPRE + k + 1])

            for t in range(NT):
                if t < NT - 1:
                    act.wait_ge(sem("gate_prod"), t + 1)
                else:
                    R1.panel_done(act, 0, 3)
                if t >= 2:
                    act.wait_ge(sem("gate_silu"), t - 1)
                act.activation(gate_tanh[t % 2][:], ps[:, t, :], ACT.Tanh, scale=0.5).then_inc(sem("gate_tanh_done"), 1)
            for t in range(NT):
                if t < NT - 1:
                    act.wait_ge(sem("tail_prod"), t + 1)
                else:
                    R1.panel_done(act, 0, 7)
                act.copy(lat[:, t, 0:TAIL_W], ps[:, t, 0:TAIL_W]).then_inc(sem("lat_done"), 1)

            for t in range(NT):
                act.wait_ge(sem("lat_done"), t + 1)
                if t >= 2:
                    act.wait_ge(sem("lat_sq_done"), 2 * t - 2)
                act.activation(lat_junk[t % 2][:, 0:Q_RANK], lat[:, t, LAT_CQ:LAT_CKV], ACT.Square,
                               accum_out=lat_ss[:, t:t + 1]).then_inc(sem("lat_sq_done"), 1)
                act.activation(lat_junk[t % 2][:, Q_RANK:], lat[:, t, LAT_CKV:LAT_KR], ACT.Square,
                               accum_out=lat_ss[:, NT + t:NT + t + 1]).then_inc(sem("lat_sq_done"), 1)
            act.wait_ge(sem("rope_arg_done"), 1)
            act.activation(trig[NOPE:P, :], trig[NOPE:P, :], ACT.Sin).then_inc(sem("rope_sin_done"), 1)
            act.wait_ge(sem("g_min_done"), 1)
            act.activation(g_exp[:], g_la[:], ACT.Exp).then_inc(sem("g_exp_done"), 1)
            act.activation(ea_b[:], a_log_b[:], ACT.Exp).then_inc(sem("g_exp_done"), 1)
            act.wait_ge(sem("g_exp1_done"), 1)
            act.activation(g_sp[:], g_u[:], ACT.Ln).then_inc(sem("g_exp_done"), 1)
            act.activation(g_beta[:], lat[:, :, GDN_HEADS:2 * GDN_HEADS], ACT.Tanh, scale=0.5)\
                .then_inc(sem("g_exp_done"), 1)

            with act.Fori(0, GDN_PANELS // 3) as i:
                for j in range(3):
                    p = 3 * i + j
                    b = 2 * j
                    act.wait_ge(sem("qkv_half"), p + 1)
                    act.wait_ge(sem("conv_done"), p + 1)
                    act.copy(xpad[:, CONV_W - 1:CONV_W - 1 + HALF], ps[:, b, :])
                    R2.panel_done(act, 3 * i, j)
                    act.copy(xpad[:, CONV_W - 1 + HALF:], ps[:, b + 1, :]).then_inc(sem("conv_in_done"), 1)
                    act.wait_ge(sem("conv_done"), p + 2)
                    act.wait_ge(sem("ss_prod"), p + 1)
                    act.activation(conv_t[:], conv_y[:], ACT.Tanh, scale=0.5).then_inc(sem("conv_tanh_done"), 1)
                    act.wait_ge(sem("conv_silu_done"), p + 1)
                    act.activation(conv_t[:], qkv[:, p, :], ACT.Square)\
                        .then_inc(sem("conv_sq_done"), 1)
            for n in range(6):
                kind, h = n // 2, n % 2
                dst = (cq_f[:, 0, :], cq_f[:, 1, :], ckv_f[:])[kind][:, h * HALF:(h + 1) * HALF]
                gain = V_QN + kind if kind < 2 else V_KVN
                act.wait_ge(sem("lat_turned"), n + 1)
                act.activation(dst, ps[:, LAT_BANKS[n], :], ACT.Copy, scale=vec[:, gain:gain + 1]).then_inc(sem("lat_feat_done"), 1)
            for t in range(NT):
                act.wait_ge(sem("v_prod"), t + 1)
                act.copy(v_t[:, t, :, :].rearrange("p h e -> p (h e)"), ps[:, t, :]).then_inc(sem("v_done"), 1)
            act.wait_ge(sem("cumsum_prod"), 1)
            n_gh = NT * GDN_HEADS
            act.copy(g_cum[:].rearrange("p t h -> p (t h)"), ps[:, 0, 0:n_gh]).then_inc(sem("cumsum_done"), 1)
            act.copy(g_tot[:].rearrange("p t h -> p (t h)"), ps[:, 0, n_gh:2 * n_gh]).then_inc(sem("cumsum_done"), 1)
            act.wait_ge(sem("cumsum_done"), 2)
            act.activation(g_eg[:], g_cum[:], ACT.Exp).then_inc(sem("g_exps_done"), 1)
            act.wait_ge(sem("g_tail_done"), 1)
            act.activation(g_ekd[:], g_ekd[:], ACT.Exp).then_inc(sem("g_exps_done"), 1)

            scale = float(DQK) ** -0.5
            def mla_take(i, h, n):
                a = h % 2
                act.wait_ge(sem("mla_proj"), 8 * i + (4 * h + n + 6))
                act.copy((q_f if n < 2 else k_f)[a][0:NOPE, n % 2 * HALF:(n % 2 + 1) * HALF], ps[0:NOPE, 7, :])\
                    .then_inc(sem("mla_proj_read"), 1)

            def mla_exp(i, s, before):
                t, a = s % NT, s // NT
                n = (t + 1) * P
                act.wait_ge(sem("mla_max_done"), MLA_ITEMS * i + s + 1)
                if slot := lagged(i, before, s, PROBS, MLA_ITEMS):
                    act.wait_ge(sem("mla_turned"), MLA_GROUPS * slot[0] + (mla_groups(slot[1])[-1] + 1))
                act.activation(probs[s % PROBS][:, 0:n], ps[:, 2 * (s % 2):2 * (s % 2) + 2, :].rearrange("p b n -> p (b n)")[:, 0:n],
                               ACT.Exp, bias=sm_neg[a][:, t:t + 1], scale=scale, accum_out=sm_sum[a][:, t:t + 1])\
                    .then_inc(sem("mla_exp_done"), 1)

            def mla_probs_out(i, s):
                for n, g in enumerate(mla_groups(s)):
                    w = min(4, s % NT + 1 - 4 * n) * P
                    act.wait_ge(sem("mla_turned"), MLA_GROUPS * i + (g + 1))
                    act.wait_ge(sem("mla_pv"), MLA_GROUPS * i + (g + 1))
                    act.copy(probs_t[g % 2][:, 0:w], ps[:, 4 + g % 2, 0:w]).then_inc(sem("mla_pt_done"), 1)

            def mla_pair(i, before, last):
                for s in range(MLA_ITEMS):
                    mla_exp(i, s, before)
                    if late := lagged(i, before, s, MLA_LAG_TURN, MLA_ITEMS):
                        mla_probs_out(*late)
                    if 2 <= s <= 5:
                        mla_take(i, 1, s - 2)
                    elif 9 <= s <= 12 and not last:
                        mla_take(i, 2, s - 9)

            for n in range(4):
                mla_take(0, 0, n)
            mla_pair(0, None, False)
            with act.Fori(0, MLA_PAIRS - 2) as i:
                mla_pair(i + 1, i, False)
            mla_pair(MLA_PAIRS - 1, MLA_PAIRS - 2, True)
            for s in range(MLA_ITEMS - MLA_LAG_TURN, MLA_ITEMS):
                mla_probs_out(MLA_PAIRS - 1, s)

            def gdn_flat(tile):
                return tile[:].rearrange("p h t -> p (h t)")

            def gdn_squares(i, a):
                act.wait_ge(sem("o_taken"), 2 * i + a + 2)
                act.wait_ge(sem("o_ss_done"), 2 * i + a + 1)
                for h in range(GDN_HEADS):
                    ins = act.activation(o_sq[:, h, :], o_s[:, h, :], ACT.Square, accum_out=o_ss[:, h:h + 1])
                ins.then_inc(sem("o_ss_done"), 1)

            def gdn_pair(i, before):
                for a in range(2):
                    act.wait_ge(sem("g_row_prod"), 2 * i + a + 1)
                    act.activation(gdn_flat(e_g[a]), ps[:, 3 * a, :], ACT.Exp).then_inc(sem("e_g_done"), 1)
                for a in range(2):
                    act.wait_ge(sem("decay_arg_done"), 2 * i + a + 1)
                    act.activation(e_d[a][:], e_d[a][:], ACT.Exp).then_inc(sem("decay_done"), 1)
                for a in range(2):
                    act.wait_ge(sem("t0_turned"), 2 * i + a + 1)
                    act.copy(gdn_flat(t_f[0][a]), ps[:, 1 + a, :]).then_inc(sem("t0_done"), 1)
                for n in range(1, len(LEVELS)):
                    for a in range(2):
                        act.wait_ge(sem("y_prod"), 10 * i + (2 * (n - 1) + a + 1))
                        act.copy(gdn_flat(y_s[a]), ps[:, a, :]).then_inc(sem("y_done"), 1)
                    if before is not None and n == 3:
                        gdn_squares(before, 0)
                if before is not None:
                    gdn_squares(before, 1)
                    act.wait_ge(sem("state_done"), 4 * i + 1)
                for a in range(2):
                    act.copy(e_last[a][:], e_g[a][:, :, CHUNK - 1::CHUNK]).then_inc(sem("e_last_done"), 1)
                for a in range(2):
                    for n, dst in enumerate((w_t, u_s)):
                        act.wait_ge(sem("wu_prod"), 4 * i + 2 * a + n + 1)
                        act.copy(gdn_flat(dst[a]), ps[:, (0, 1, 2, 4)[2 * a + n], :]).then_inc(sem("wu_done"), 1)

            gdn_pair(0, None)
            with act.Fori(0, GDN_PAIRS - 1) as i:
                gdn_pair(i + 1, i)
            for a in range(2):
                gdn_squares(GDN_PAIRS - 1, a)

            norm_full("mixt")
            for c in range(2):
                for t in range(NT):
                    if t < NT - 1:
                        act.wait_ge(sem("mixed_prod"), 7 * c + t + 1)
                    else:
                        R3.panel_done(act, 0, 4 * c + 3)
                    act.copy(mixed[:, t, c * HALF:(c + 1) * HALF], ps[:, t, :]).then_inc(sem("mixed_done"), 1)
            act.wait_ge(sem("mixed_done"), 2 * NT)
            norm_square(mixed, act_lo_junk, lambda t: None)
            norm_square(resid, acc, lambda t: act.wait_ge(sem("resid_done"), t + 1))
            norm_scale("n2", resid, acc)
            norm_full("n2", lambda k: vec[:, V_FFNPRE + k:V_FFNPRE + k + 1])

            def ffn_relu(ring, run):
                def ada_load(i, j):
                    slab = w_ada[:, :, bass.ds((ADA_STEP * i + j) * P, P)]
                    act.wait_ge(sem("ada_used"), ADA_STEP * i + (2, 1, 3)[j])
                    act.dma_start(ada[j % 2][:], slab).then_inc(sem(f"ada_in{j % 2}"), 16)

                with act.Fori(0, FFN_STEPS) as i:
                    if run == 0:
                        ada_load(i, 0)
                        ada_load(i, 1)
                    for q in range(4):
                        j, f = q // 2, q % 2
                        if f == 0:
                            act.wait_ge(sem("ffn_half"), 2 * i + (2 * FFN_STEPS * run + j + 1))
                        else:
                            ring.panel_done(act, 4 * i, j)
                        act.wait_ge(sem("ffn_hid"), 4 * i + (4 * FFN_STEPS * run + q - 1 + FFN_CREDIT))
                        act.activation(relu_t[q % 2][:], ps[:, q, :], ACT.Relu).then_inc(sem("ffn_relu"), 1)
                        act.wait_ge(sem("ffn_relu"), 4 * i + (4 * FFN_STEPS * run + q + 1))
                        act.activation(hid_hi[:, j, f * HALF:(f + 1) * HALF], relu_t[q % 2][:], ACT.Square)\
                            .then_inc(sem("ffn_hid_hi"), 1)
                    if run == 0:
                        ada_load(i, 2)
                        act.wait_ge(sem("ada_used"), ADA_STEP * i + ADA_STEP + 2)
                        act.copy(mod[:, bass.ds(ADA_STEP * i, ADA_STEP)], ps[:, 0, 0:ADA_STEP]).then_inc(sem("ada_read"), 1)

            ffn_relu(R4, 0)
            act.wait_ge(sem("ffn_acc"), 16 * FFN_STEPS + 4)
            act.dma_start(post_row[:], d["ffn_post_norm"][0].partition_broadcast(P)).then_inc(sem("post_gain_in"), 16)
            norm_square(acc, act_hi_junk, lambda t: None)
            def spill(t):
                act.wait_ge(sem("resid_done"), NT + t + 1)
                act.dma_start(x1_spill[t], resid[:, t, :]).then_inc(sem("x1_stored"), 16)

            norm_square(resid, acc, spill)
            norm_scale("n3", resid, acc)
            act.wait_ge(sem("mod_scales_done"), 1)
            norm_full("n3", lambda k: scale2[:, k:k + 1], lambda k: mod[:, k:k + 1])

            with act.Fori(0, CONV2_PANELS) as i:
                R5.panel_done(act, 3 * i, 1)
                act.wait_ge(sem("c2_v_done"), i + 1)
                act.copy(cg_t[:], ps[:, 2:4, :].rearrange("p b n -> p (b n)")).then_inc(sem("c2_cg_read"), 1)
                act.wait_ge(sem("c2_y_done"), i + 2)
                act.copy(y_hi[:, i, :], conv2_y[:]).then_inc(sem("c2_hi_done"), 1)

            def merge_gates(ring, run, gates):
                with act.Fori(0, KD // 2) as i:
                    for j in range(2):
                        ring.panel_done(act, 4 * i, 2 * j)
                        act.wait_ge(sem("m_done"), 2 * i + (KD * run + j + 1))
                        act.activation(gates[j][:], ps[:, 4 * j:4 * j + 2, :].rearrange("p b n -> p (b n)"), ACT.Tanh,
                                       scale=0.5).then_inc(sem("m_gate_read"), 1)

            merge_gates(R6, 0, conv_gate)
            for t in range(NT):
                if t < NT - 1:
                    act.wait_ge(sem("v2_prod"), t + 1)
                else:
                    R7.panel_done(act, 0, 3)
                act.copy(v2[:, t, :, :].rearrange("p h e -> p (h e)"), ps[:, t, :]).then_inc(sem("v2_done"), 1)

            act.preload_act_table_set("natural_log_exp_and_others")

            def sb_copy_qk(i):
                for j, dst in enumerate((q2, k2)):
                    R8.panel_done(act, 2 * i, j)
                    act.copy(dst[:], ps[:, 2 * j:2 * j + 2, :].rearrange("p b n -> p (b n)")).then_inc(sem("sb_qk_done"), 1)

            ach = Chain(act, sem("act_chain"))

            def sb_pair(i):
                for s in range(SB_ITEMS + SB_LAG_EXP):
                    if s >= SB_LAG_EXP:
                        u = s - SB_LAG_EXP
                        a = sb_a[u % 3][:, 0:(u // 2 + 1) * P]
                        act.wait_ge(sem("sb_arg_done"), SB_ITEMS * i + u + 1)
                        act.activation(a, a, ACT.Exp).then_inc(sem("sb_weights_done"), 1)
                    if s < SB_ITEMS:
                        n = (s // 2 + 1) * P
                        l = sb_sp[s % 2][:, 0:n]
                        act.wait_ge(sem("sb_z_done"), SB_ITEMS * i + s + 3)
                        ach.link(act.activation(l, sb_z[s % 2][:, 0:n], ACT.Abs))
                        ach.link(act.activation(l, l, ACT.Exp, scale=-1.0))
                        act.activation(l, l, ACT.Ln, bias=1.0).then_inc(sem("sb_ln_done"), 1)

            sb_copy_qk(0)
            with act.Fori(0, SB_PAIRS - 1) as i:
                ach.loop(i, 2 * SB_ITEMS)
                sb_pair(i)
                sb_copy_qk(i + 1)
            ach.end(SB_PAIRS - 1)
            sb_pair(SB_PAIRS - 1)

            norm_full("sb_o", nk=CONV2_PANELS)
            merge_gates(R9, 1, attn_gate)
            R9.panel_done(act, 0, 2 * KD - 1)
            for k in range(KD):
                act.wait_ge(sem("m_done"), KD + 2 + k + 1)
                act.activation(act_hi[:, k, :], merged[:, k, :], ACT.Copy, scale=0.5).then_inc(sem("merged_hi_done"), 1)
            for c in range(2):
                for t in range(NT):
                    if t < NT - 1:
                        act.wait_ge(sem("mixed_prod"), 14 + 7 * c + t + 1)
                    else:
                        R10.panel_done(act, 0, 4 * c + 3)
                    act.copy(acc[:, t, c * HALF:(c + 1) * HALF], ps[:, t, :]).then_inc(sem("mixed_done"), 1)
                if c == 0:
                    act.wait_ge(sem("merged_split"), KD)
                    act.wait_ge(sem("x1_stored"), 16 * NT)
                    for t in range(NT):
                        act.dma_start(resid[:, t, :], x1_spill[t]).then_inc(sem(f"x_in{t}"), 16)
                    act.dma_start(gain_row[:], d["g_post_mix_2"][0].partition_broadcast(P)).then_inc(sem("post_gain_in"), 16)
            act.wait_ge(sem("mixed_done"), 4 * NT)
            norm_square(acc, act_lo_junk, lambda t: None)
            norm_square(resid, acc, lambda t: act.wait_ge(sem("resid_done"), 2 * NT + t + 1))
            norm_scale("n4", resid, acc)
            norm_full("n4", lambda k: scale2[:, KD + k:KD + k + 1], lambda k: mod[:, 3 * KD + k:3 * KD + k + 1])
            ffn_relu(R11, 1)
            act.wait_ge(sem("ffn_acc"), 2 * (16 * FFN_STEPS + 4))
            act.dma_start(gain_row[:], d["g_post_mlp_2"][0].partition_broadcast(P)).then_inc(sem("post_gain_in"), 16)
            norm_square(acc, act_hi_junk, lambda t: None)

        @block.vector
        def _(dve):
            ch = Chain(dve, sem("dve_chain"))

            def norm_split(tag, hi, lo, nk=KD):
                base = TURNS[tag]
                for n in range(2 * nk):
                    h, k = n // nk, n % nk
                    cols = slice(h * HALF, (h + 1) * HALF)
                    dve.wait_ge(sem("turn_read"), base + n + 1)
                    dve.tensor_copy(hi[:, k, cols], norm_tmp[n % 2][:]).then_inc(sem("turn_hi_done"), 1)
                    dve.wait_ge(sem("turn_hi_done"), base + n + 1)
                    dve.tensor_tensor(lo[:, k, cols], norm_tmp[n % 2][:], hi[:, k, cols].bitcast(F32), ALU.subtract)\
                        .then_inc(sem("turn_split"), 1)

            norm_split("n1", act_hi, act_lo)

            dve.wait_ge(sem("gdn_vec_in"), 48)
            ch.link(dve.tensor_scalar(out_norm_row[:], out_norm_row[:], 0.5, None, ALU.mult))
            for t in range(NT):
                dve.wait_ge(sem("gate_tanh_done"), t + 1)
                dve.scalar_tensor_tensor(gate[:, t, :], gate_tanh[t % 2][:], 1.0, ps[:, t, :], ALU.add, ALU.mult)\
                    .then_inc(sem("gate_silu"), 1)
                dve.wait_ge(sem("gate_silu"), t + 1)
                gh = gate[:, t, :].rearrange("p (h e) -> p h e", h=GDN_HEADS)
                ch.link(dve.tensor_tensor(gh, gh, out_norm_row[:].unsqueeze(1).broadcast_to([P, GDN_HEADS, P]), ALU.mult))

            rot = slice(NOPE, P)
            dve.wait_ge(sem("pos_in"), 16)
            ch.link(dve.tensor_copy(ang[rot, :], pos_i[rot, :]))
            ch.link(dve.tensor_scalar(ang[rot, :], ang[rot, :], consts[rot, C_FREQ:C_FREQ + 1], None, ALU.mult))
            ch.link(dve.tensor_scalar(turns[rot, :], ang[rot, :], 1.0 / TWO_PI, consts[rot, C_QUARTER:C_QUARTER + 1],
                                      ALU.mult, ALU.add))
            ch.link(dve.tensor_scalar(turns[rot, :], turns[rot, :], ROUND, ROUND, ALU.add, ALU.subtract))
            src = ang
            for part in TWO_PI_PARTS:
                ch.link(dve.scalar_tensor_tensor(trig[rot, :], turns[rot, :], -part, src[rot, :], ALU.mult, ALU.add))
                src = trig
            ch.link(dve.tensor_scalar(trig[rot, :], trig[rot, :], consts[rot, C_QUARTER_ANGLE:C_QUARTER_ANGLE + 1],
                                      PI_BELOW, ALU.add, ALU.min))
            dve.tensor_scalar(trig[rot, :], trig[rot, :], -PI_BELOW, None, ALU.max).then_inc(sem("rope_arg_done"), 1)
            dve.memset(conv_t[:], 0.0).then_inc(sem("conv_sq_done"), 1)

            dve.wait_ge(sem("lat_done"), NT)
            dtb = dt_b[:].unsqueeze(1).broadcast_to([P, NT, GDN_HEADS])
            ch.link(dve.tensor_tensor(g_arg[:], lat[:, :, 0:GDN_HEADS], dtb, ALU.add))
            dve.tensor_scalar(g_la[:], g_arg[:], 40.0, None, ALU.min).then_inc(sem("g_min_done"), 1)
            dve.wait_ge(sem("g_exp_done"), 1)
            dve.tensor_scalar(g_u[:], g_exp[:], 1.0, None, ALU.add).then_inc(sem("g_exp1_done"), 1)
            dve.wait_ge(sem("g_exp1_done"), 1)
            ch.link(dve.scalar_tensor_tensor(g_exp[:], g_u[:], -1.0, g_exp[:], ALU.add, ALU.subtract))
            dve.wait_ge(sem("g_exp_done"), 3)
            ch.link(dve.reciprocal(g_u[:], g_u[:]))
            ch.link(dve.tensor_tensor(g_exp[:], g_exp[:], g_u[:], ALU.mult))
            ch.link(dve.tensor_tensor(g_sp[:], g_sp[:], g_exp[:], ALU.subtract))
            ch.link(dve.tensor_tensor(g_sp[:], g_sp[:], g_arg[:], ALU.max))
            eab = ea_b[:].unsqueeze(1).broadcast_to([P, NT, GDN_HEADS])
            dve.scalar_tensor_tensor(g_la[:], g_sp[:], -1.0, eab, ALU.mult, ALU.mult).then_inc(sem("log_a_done"), 1)
            dve.wait_ge(sem("g_exp_done"), 4)
            ch.link(dve.tensor_scalar(g_beta[:], g_beta[:], 0.5, 0.5, ALU.mult, ALU.add))

            dve.wait_ge(sem("lat_rstd_done"), 1)

            def by_tile(col, n):
                return lat_rstd[:, col:col + NT].unsqueeze(2).broadcast_to([P, NT, n])

            half = ROPE // 2
            dve.tensor_tensor(lat[:, :, LAT_CQ:LAT_CKV], lat[:, :, LAT_CQ:LAT_CKV], by_tile(0, Q_RANK), ALU.mult)
            dve.tensor_tensor(lat[:, :, LAT_CKV:LAT_KR], lat[:, :, LAT_CKV:LAT_KR], by_tile(NT, KV_RANK), ALU.mult)
            dve.tensor_copy(lat[:, :, TAIL_W:TAIL_W + half], lat[:, :, LAT_KR + half:LAT_KR + ROPE])
            dve.tensor_copy(lat[:, :, TAIL_W + half:TAIL_W + ROPE], lat[:, :, LAT_KR:LAT_KR + half])\
                .then_inc(sem("lat_norm_done"), 1)
            dve.wait_ge(sem("rope_sin_done"), 1)
            ch.link(dve.tensor_scalar(trig[rot, :], trig[rot, :], consts[rot, C_SIGN:C_SIGN + 1], None, ALU.mult))
            dve.wait_ge(sem("lat_sq_done"), 2 * NT)
            ch.link(dve.memset(xpad[:, 0:CONV_W - 1], 0.0))

            with dve.Fori(0, GDN_PANELS // 3) as i:
                ch.loop(i, 9)
                for j in range(3):
                    p = 3 * i + j
                    dve.wait_ge(sem("conv_in_done"), p + 3)

                    def tap(w):
                        return vec[:, bass.ds(V_CONV + w * GDN_PANELS + p, 1)]

                    ch.link(dve.tensor_scalar(conv_y[:], xpad[:, 0:SEQ], tap(0), None, ALU.mult))
                    for w in range(1, CONV_W):
                        ins = dve.scalar_tensor_tensor(conv_y[:], xpad[:, w:w + SEQ], tap(w), conv_y[:],
                                                       ALU.mult, ALU.add)
                        if w < CONV_W - 1:
                            ch.link(ins)
                        else:
                            ins.then_inc(sem("conv_done"), 1)
                    dve.wait_ge(sem("conv_tanh_done"), p + 1)
                    dve.scalar_tensor_tensor(qkv[:, p, :], conv_t[:], 1.0, conv_y[:], ALU.add, ALU.mult)\
                        .then_inc(sem("conv_silu_done"), 1)
                    dve.wait_ge(sem("ss_prod"), p + 1)
                    dve.tensor_copy(ss_gdn[:, :, p], ps[:, 6, 0:NT]).then_inc(sem("ss_gdn_done"), 1)
                ch.end(GDN_PANELS // 3)
            rr, swap = slice(NOPE, DQK), slice(DQK, P)
            dve.wait_ge(sem("conv_sq_done"), GDN_PANELS + 1)
            for h in range(2):
                cols = slice(h * HALF, (h + 1) * HALF)
                dve.wait_ge(sem("lat_turned"), 7 + h)
                b = LAT_BANKS[6 + h]
                dve.tensor_tensor(rope_t[rr, cols], ps[swap, b, :], trig[swap, cols], ALU.mult)
                ch.link(dve.tensor_tensor(k_f[0][rr, cols], ps[rr, b, :], trig[rr, cols], ALU.mult))
            dve.tensor_tensor(k_f[0][rr, :], k_f[0][rr, :], rope_t[rr, :], ALU.add).then_inc(sem("mla_k_rope_done"), 1)
            dve.wait_ge(sem("mla_k_rope_done"), 1)
            dve.tensor_copy(k_f[1][rr, :], k_f[0][rr, :]).then_inc(sem("mla_k_rope_done"), 1)
            dve.wait_ge(sem("cumsum_done"), 2)
            dve.tensor_tensor(g_ekd[:], g_tot[:], g_cum[:], ALU.subtract).then_inc(sem("g_tail_done"), 1)

            scale = float(DQK) ** -0.5

            def mla_rotate(i, h, n):
                a, cols = h % 2, slice(n * HALF, (n + 1) * HALF)
                dve.wait_ge(sem("mla_proj"), 8 * i + (4 * h + n + 6))
                dve.tensor_tensor(rope_t[rr, cols], ps[swap, 7, :], trig[swap, cols], ALU.mult)
                ch.link(dve.tensor_tensor(q_f[a][rr, cols], ps[rr, 7, :], trig[rr, cols], ALU.mult))
                dve.tensor_tensor(q_f[a][rr, cols], q_f[a][rr, cols], rope_t[rr, cols], ALU.add)\
                    .then_inc(sem("mla_rope_done"), 1)
                dve.wait_ge(sem("mla_rope_done"), 4 * i + (2 * h + n + 1))

            def mla_max(i, s):
                t, a = s % NT, s // NT
                n = (t + 1) * P
                z = ps[:, 2 * (s % 2):2 * (s % 2) + 2, :].rearrange("p b n -> p (b n)")
                dve.wait_ge(sem("mla_scores"), MLA_ITEMS * i + s + 1)
                ch.link(dve.memset(z[0:CHUNK, n - CHUNK:n], -1e30))
                ch.link(dve.tensor_reduce(sm_max[a][:, t:t + 1], z[:, 0:n], AX_X, ALU.max))
                dve.tensor_scalar(sm_neg[a][:, t:t + 1], sm_max[a][:, t:t + 1], -scale, None, ALU.mult)\
                    .then_inc(sem("mla_max_done"), 1)

            def mla_out(i, a):
                dve.wait_ge(sem("mla_pv"), MLA_GROUPS * i + (mla_groups(a * NT + NT - 1)[-1] + 3))
                ch.link(dve.reciprocal(sm_rec[a][:], sm_sum[a][:]))
                dve.tensor_tensor(mix[:, :, bass.ds(2 * V_DIM * i + (GDN_W + a * V_DIM), V_DIM)],
                                  ps[:, 6, :].rearrange("p (t e) -> p t e", e=V_DIM),
                                  sm_rec[a][:].unsqueeze(2).broadcast_to([P, NT, V_DIM]), ALU.mult)\
                    .then_inc(sem("mla_o_done"), 1)

            def mla_pair(i, before, last):
                for s in range(MLA_ITEMS):
                    mla_max(i, s)
                    if before is not None and s == MLA_LAG_PV:
                        mla_out(before, 1)
                    if s == NT + MLA_LAG_PV:
                        mla_out(i, 0)
                    if 2 <= s <= 3:
                        mla_rotate(i, 1, s - 2)
                    elif 9 <= s <= 10 and not last:
                        mla_rotate(i, 2, s - 9)

            for n in range(2):
                mla_rotate(0, 0, n)
            mla_pair(0, None, False)
            with dve.Fori(0, MLA_PAIRS - 2) as i:
                ch.loop(i, 2 * MLA_ITEMS + 2 + 4)
                mla_pair(i + 1, i, False)
            ch.end(MLA_PAIRS - 2)
            mla_pair(MLA_PAIRS - 1, MLA_PAIRS - 2, True)
            mla_out(MLA_PAIRS - 1, 1)

            dve.wait_ge(sem("qk_norm_done"), 2)
            ch.link(dve.tensor_tensor(g_bk[:], g_beta[:], g_rk[:], ALU.mult))
            dve.wait_ge(sem("g_exps_done"), 2)
            dve.tensor_scalar(g_cv[:], g_beta[:], 0.5, None, ALU.mult)
            dve.tensor_tensor(g_cd[:], g_rk[:], g_ekd[:], ALU.mult)
            dve.tensor_tensor(g_cw[:], g_bk[:], g_eg[:], ALU.mult).then_inc(sem("g_scales_done"), 1)

            def by_head(cols):
                return cols.unsqueeze(2).broadcast_to([P, GDN_HEADS, P])

            def each_head(mask):
                return consts[:, mask:mask + P].unsqueeze(1).broadcast_to([P, GDN_HEADS, P])

            def bank(n):
                return ps[:, n, :].rearrange("p (h t) -> p h t", h=GDN_HEADS)

            def gdn_decay(i):
                for a in range(2):
                    cols = bass.ds((2 * i + a) * P, P)
                    dve.tensor_copy(k_s[a][:], qkv[:, GDN_HEADS:2 * GDN_HEADS, cols])
                    dve.tensor_copy(v_s[a][:], qkv[:, 2 * GDN_HEADS:3 * GDN_HEADS, cols]).then_inc(sem("gdn_k_in"), 1)
                for a in range(2):
                    dve.wait_ge(sem("e_g_done"), 2 * i + a + 1)
                    ch.link(dve.tensor_tensor(e_d[a][:], bank(3 * a), by_head(g_cum[:, 2 * i + a, :]), ALU.subtract))
                    dve.tensor_scalar(e_d[a][:], e_d[a][:], 0.0, None, ALU.min).then_inc(sem("decay_arg_done"), 1)
                for a, (b_b, b_k) in enumerate(((1, 2), (4, 0))):
                    dve.wait_ge(sem("decay_done"), 2 * i + a + 1)
                    rk = g_rk[:, 2 * i + a, :]
                    ch.link(dve.tensor_tensor(e_d[a][:], e_d[a][:], by_head(rk), ALU.mult))
                    dve.wait_ge(sem("kk_prod"), 2 * i + a + 2)
                    ch.link(dve.tensor_tensor(a_t[a][:], bank(b_b), e_d[a][:], ALU.mult))
                    dve.tensor_tensor(a_t[a][:], bank(b_k), a_t[a][:], ALU.mult).then_inc(sem("a_t_done"), 1)
                    dve.wait_ge(sem("a_t_done"), 2 * i + a + 1)
                    ch.link(dve.tensor_tensor(t_r[0][a][:], a_t[a][:], each_head(C_LEVEL), ALU.mult))
                    dve.tensor_tensor(t_r[0][a][:], each_head(C_ID), t_r[0][a][:], ALU.subtract).then_inc(sem("tr0_done"), 1)

            def gdn_new_values(i, k):
                a, rows = k // 2, slice(k % 2 * CHUNK, (k % 2 + 1) * CHUNK)
                dve.wait_ge(sem("ws_prod"), 4 * i + k + 1)
                dve.tensor_tensor(v_n[rows, :, :], u_s[a][rows, :, :], bank(5)[rows], ALU.subtract)\
                    .then_inc(sem("v_new_done"), 1)

            def gdn_new_state(i, k):
                dve.wait_ge(sem("ds_prod"), 4 * i + k + 1)
                dve.wait_ge(sem("s_dec_done"), 4 * i + k + 1)
                dve.tensor_tensor(state[1 - k % 2][:], s_dec[:], bank(5), ALU.add).then_inc(sem("state_done"), 1)

            def gdn_take_out(i, a):
                dve.wait_ge(sem("o_prod"), 2 * i + a + 1)
                dve.tensor_tensor(o_s[:], bank(6), by_head(g_rq[:, 2 * i + a, :]), ALU.mult).then_inc(sem("o_taken"), 1)

            def gdn_out(i, a):
                t = 2 * i + a
                dve.wait_ge(sem("o_rstd_done"), t + 1)
                ch.link(dve.tensor_tensor(o_s[:], o_s[:], by_head(o_rstd[:]), ALU.mult))
                dve.tensor_tensor(mix[:, t, 0:GDN_W].rearrange("p (h e) -> p h e", h=GDN_HEADS), o_s[:],
                                  gate[:, t, :].rearrange("p (h e) -> p h e", h=GDN_HEADS), ALU.mult)\
                    .then_inc(sem("gdn_out_done"), 1)
                dve.wait_ge(sem("gdn_out_done"), t + 1)

            def gdn_scaled(i, a):
                t = 2 * i + a
                dve.wait_ge(sem("gdn_turned"), 6 * i + 3 * a + 3)
                dve.tensor_tensor(q_d[a][:], qkv[:, 0:GDN_HEADS, bass.ds(t * P, P)], e_g[a][:], ALU.mult)
                dve.tensor_tensor(k_w[a][:], bank(3), by_head(g_cw[:, t, :]), ALU.mult)
                dve.tensor_tensor(k_d[a][:], bank(3), by_head(g_cd[:, t, :]), ALU.mult).then_inc(sem("gdn_turn_read"), 1)
                dve.tensor_tensor(v_b[a][:], bank(7), by_head(g_cv[:, t, :]), ALU.mult).then_inc(sem("gdn_turn_read"), 1)
                dve.wait_ge(sem("p_decay_done"), t + 1)
                dve.tensor_tensor(p_t[a][:], bank(5), e_d[a][:], ALU.mult).then_inc(sem("gdn_turn_read"), 1)

            def gdn_pair(i, before):
                if before is not None:
                    dve.wait_ge(sem("wu_prod"), 4 * i)
                gdn_decay(i)
                for n in range(1, len(LEVELS)):
                    old, new, last = (n - 1) % 2, n % 2, n == len(LEVELS) - 1
                    if before is not None and not last:
                        gdn_new_values(before, n - 1)
                    if last:
                        gdn_scaled(i, 0)
                    for a in range(2):
                        dve.wait_ge(sem("zt_prod"), 10 * i + (2 * (n - 1) + a + 1))
                        ins = dve.tensor_tensor(t_r[new][a][:], t_r[old][a][:], bank(2 + 2 * a), ALU.subtract)
                        if last:
                            ins.then_inc(sem("t_last_done"), 1)
                        else:
                            dve.wait_ge(sem("z_prod"), 8 * i + (2 * (n - 1) + a + 1))
                            dve.tensor_tensor(t_f[new][a][:], t_f[old][a][:], bank(3 + 4 * a), ALU.subtract)\
                                .then_inc(sem("t_done"), 1)
                            if a == 0 and before is not None:
                                gdn_new_state(before, n - 1)
                    if before is not None and n == 2:
                        gdn_take_out(before, 0)
                    if before is not None and n == 4:
                        gdn_out(before, 0)
                        gdn_take_out(before, 1)
                gdn_scaled(i, 1)
                if before is not None:
                    gdn_out(before, 1)

            dve.memset(state[0][:], 0.0).then_inc(sem("state_done"), 1)
            gdn_pair(0, None)
            with dve.Fori(0, GDN_PAIRS - 1) as i:
                ch.loop(i, 8 + 2)
                gdn_pair(i + 1, i)
            ch.end(GDN_PAIRS - 1)
            for k in range(4):
                gdn_new_values(GDN_PAIRS - 1, k)
                gdn_new_state(GDN_PAIRS - 1, k)
                if k % 2:
                    gdn_take_out(GDN_PAIRS - 1, k // 2)
                    gdn_out(GDN_PAIRS - 1, k // 2)

            norm_split("mixt", mixt_hi, mixt_lo)

            def post_norm(tag, src, row, ready):
                dve.wait_ge(sem("post_gain_in"), 16 * row)
                for t in range(NT):
                    ready(t)
                    dve.wait_ge(sem("norm_rstd_done"), 2 * NORMS.index(tag) + t // 4 + 1)
                    ch.link(dve.scalar_tensor_tensor(post_tmp[t % 2][:], src[:, t, :], rstd[:, t:t + 1], post_row[:],
                                                     ALU.mult, ALU.mult))
                    dve.tensor_tensor(resid[:, t, :], resid[:, t, :], post_tmp[t % 2][:], ALU.add)\
                        .then_inc(sem("resid_done"), 1)

            post_norm("mix_post", mixed, 1, lambda t: dve.wait_ge(sem(f"x_in{t}"), 32))
            norm_split("n2", act_hi, act_lo)

            def ffn_sums(ring, run):
                for t in range(NT):
                    ins = dve.memset(acc[:, t, :], 0.0)
                ins.then_inc(sem("ffn_acc"), 4)
                with dve.Fori(0, FFN_STEPS) as i:
                    ch.loop(i, 4)
                    for q in range(4):
                        j, cols = q // 2, slice((q % 2) * HALF, (q % 2 + 1) * HALF)
                        dve.wait_ge(sem("ffn_relu"), 4 * i + (4 * FFN_STEPS * run + q + 1))
                        dve.wait_ge(sem("ffn_hid"), 4 * i + (4 * FFN_STEPS * run + q + FFN_CREDIT))
                        ch.link(dve.tensor_tensor(relu_sq[:], relu_t[q % 2][:], relu_t[q % 2][:], ALU.mult))
                        dve.wait_ge(sem("ffn_hid_hi"), 4 * i + (4 * FFN_STEPS * run + q + 1))
                        dve.tensor_tensor(hid_lo[:, j, cols], relu_sq[:], hid_hi[:, j, cols].bitcast(F32), ALU.subtract)\
                            .then_inc(sem("ffn_hid"), 1)
                    for g in range(16):
                        t, cols = g // 2, slice((g % 2) * HALF, (g % 2 + 1) * HALF)
                        if g < 15:
                            dve.wait_ge(sem("ffn_down"), 15 * i + (15 * FFN_STEPS * run + g + 1))
                        else:
                            ring.panel_done(dve, 4 * i, 3)
                        dve.tensor_tensor(acc[:, t, cols], ps[:, 4 + g % 4, :], acc[:, t, cols], ALU.add)\
                            .then_inc(sem("ffn_acc"), 1)
                    dve.wait_ge(sem("ffn_acc"), 16 * i + ((16 * FFN_STEPS + 4) * run + 20))
                ch.end(FFN_STEPS)

            ffn_sums(R4, 0)
            post_norm("ffn_post", acc, 2, lambda t: None)
            dve.wait_ge(sem("ada_read"), FFN_STEPS + 1)
            ch.link(dve.tensor_tensor(mod[:], mod[:], vec2[:, 0:N_BADA], ALU.add))
            for n, (gain, col) in enumerate(((V_GPREMIX2, KD), (V_GPREMLP2, 4 * KD))):
                ch.link(dve.scalar_tensor_tensor(scale2[:, n * KD:(n + 1) * KD], mod[:, col:col + KD], 1.0,
                                                 vec[:, gain:gain + KD], ALU.add, ALU.mult))
            dve.sem_inc(sem("mod_scales_done"), 1)
            norm_split("n3", act_hi, act_lo)

            ch.link(dve.memset(vpad[:, 0:CONV2_TAPS - 1], 0.0))
            with dve.Fori(0, CONV2_PANELS) as i:
                ch.loop(i, 3)

                def tap(w):
                    return vec[:, bass.ds(V_CONV2 + w * CONV2_PANELS + i, 1)]

                R5.panel_done(dve, 3 * i, 2)
                dve.wait_ge(sem("c2_cg_read"), i + 2)
                dve.tensor_tensor(vpad[:, CONV2_TAPS - 1:], ps[:, 4:6, :].rearrange("p b n -> p (b n)"), cg_t[:], ALU.mult)\
                    .then_inc(sem("c2_v_done"), 1)
                dve.wait_ge(sem("c2_v_done"), i + 2)
                ch.link(dve.tensor_scalar(conv2_y[:], vpad[:, 0:SEQ], tap(0), None, ALU.mult))
                for w in range(1, CONV2_TAPS):
                    ch.link(dve.scalar_tensor_tensor(conv2_y[:], vpad[:, w:w + SEQ], tap(w), conv2_y[:], ALU.mult, ALU.add))
                dve.tensor_tensor(conv2_y[:], ps[:, 0:2, :].rearrange("p b n -> p (b n)"), conv2_y[:], ALU.mult)\
                    .then_inc(sem("c2_y_done"), 1)
                dve.wait_ge(sem("c2_hi_done"), i + 1)
                dve.wait_ge(sem("c2_y_done"), i + 2)
                dve.tensor_tensor(y_lo[:, i, :], conv2_y[:], y_hi[:, i, :].bitcast(F32), ALU.subtract)\
                    .then_inc(sem("c2_split"), 1)
                dve.wait_ge(sem("c2_split"), i + 1)
            ch.end(CONV2_PANELS)

            dve.wait_ge(sem("x1_stored"), 16 * NT)
            with dve.Fori(0, KD // 2) as i:
                for j in range(2):
                    R6.panel_done(dve, 4 * i, 2 * j + 1)
                    dve.wait_ge(sem("m_gate_read"), 2 * i + (j + 3))
                    dve.scalar_tensor_tensor(merged[:, 2 * i + j, :], conv_gate[j][:], 1.0,
                                             ps[:, 4 * j + 2:4 * j + 4, :].rearrange("p b n -> p (b n)"), ALU.add, ALU.mult)\
                        .then_inc(sem("m_done"), 1)

            z_scale = float(SB_DIM) ** -0.5

            def sb_take(i, s):
                t = s // 2
                n, z = (t + 1) * P, sb_z[s % 2]
                dve.wait_ge(sem("sb_scores"), SB_ITEMS * i + s + 1)
                ch.link(dve.tensor_scalar(z[:, 0:n], ps[:, 2 * (s % 2):2 * (s % 2) + 2, :].rearrange("p b n -> p (b n)")[:, 0:n],
                                          z_scale, None, ALU.mult))
                dve.tensor_tensor(z[:, t * P:n], z[:, t * P:n], consts[:, C_KEYCAP:C_KEYCAP + P], ALU.min)\
                    .then_inc(sem("sb_z_done"), 1)

            def sb_log_weights(i, s):
                n = (s // 2 + 1) * P
                z, l, a = (x[:, 0:n] for x in (sb_z[s % 2], sb_sp[s % 2], sb_a[s % 3]))
                dve.wait_ge(sem("sb_ln_done"), SB_ITEMS * i + s + 1)
                ch.link(dve.scalar_tensor_tensor(l, z, 0.0, l, ALU.max, ALU.add))
                ch.link(dve.tensor_tensor_scan(a[:, ::-1], l[:, ::-1], l[:, ::-1], 0.0, ALU.add, ALU.bypass))
                dve.tensor_tensor(a, z, a, ALU.subtract).then_inc(sem("sb_arg_done"), 1)
                dve.wait_ge(sem("sb_arg_done"), SB_ITEMS * i + s + 1)

            def sb_weights_out(i, s):
                for n, g in enumerate(sb_groups(s)):
                    w = min(4, s // 2 + 1 - 4 * n) * P
                    dve.wait_ge(sem("sb_turned"), SB_GROUPS * i + g + 1)
                    dve.wait_ge(sem("sb_pv"), SB_GROUPS * i + g + 1)
                    dve.tensor_copy(sb_at[g % 2][:, 0:w], ps[:, 4 + g % 2, 0:w]).then_inc(sem("sb_at_done"), 1)

            def sb_out(i, half):
                dve.wait_ge(sem("sb_pv"), SB_GROUPS * i + (sb_groups(half * NT + NT - 1)[-1] + 3))
                dve.tensor_copy(o2[:, 4 * half:4 * half + 4, bass.ds(P * i, P)],
                                ps[:, 6 + half, :].rearrange("p (t e) -> p t e", t=4)).then_inc(sem("sb_o_done"), 1)

            def sb_pair(i):
                for s in range(SB_ITEMS + SB_LAG_TURN):
                    if s < SB_ITEMS:
                        sb_take(i, s)
                    if SB_LAG_ARG <= s < SB_ITEMS + SB_LAG_ARG:
                        sb_log_weights(i, s - SB_LAG_ARG)
                    if s >= SB_LAG_TURN:
                        sb_weights_out(i, s - SB_LAG_TURN)
                    if s == NT + SB_LAG_PV:
                        sb_out(i, 0)
                sb_out(i, 1)

            with dve.Fori(0, SB_PAIRS - 1) as i:
                ch.loop(i, 3 * SB_ITEMS)
                sb_pair(i)
            ch.end(SB_PAIRS - 1)
            sb_pair(SB_PAIRS - 1)

            norm_split("sb_o", o2_hi, o2_lo, CONV2_PANELS)
            with dve.Fori(0, KD // 2) as i:
                ch.loop(i, 2)
                for j in range(2):
                    p = 2 * i + j
                    R9.panel_done(dve, 4 * i, 2 * j + 1)
                    dve.wait_ge(sem("m_gate_read"), p + KD + 3)
                    ch.link(dve.scalar_tensor_tensor(attn_part[j][:], attn_gate[j][:], 1.0,
                                                     ps[:, 4 * j + 2:4 * j + 4, :].rearrange("p b n -> p (b n)"),
                                                     ALU.add, ALU.mult))
                    dve.tensor_tensor(merged[:, p, :], merged[:, p, :], attn_part[j][:], ALU.add).then_inc(sem("m_done"), 1)
                    dve.wait_ge(sem("m_done"), p + KD + 3)
            ch.end(KD // 2)
            for k in range(KD):
                dve.wait_ge(sem("merged_hi_done"), k + 1)
                dve.scalar_tensor_tensor(act_lo[:, k, :], merged[:, k, :], 0.5, act_hi[:, k, :].bitcast(F32),
                                         ALU.mult, ALU.subtract).then_inc(sem("merged_split"), 1)

            def gate_row(run):
                col = mod[:, (2 + 3 * run) * KD:(3 + 3 * run) * KD]
                dve.tensor_tensor(diag[:], consts[:, C_ID:C_ID + P].unsqueeze(1).broadcast_to([P, KD, P]),
                                  col.unsqueeze(2).broadcast_to([P, KD, P]), ALU.mult).then_inc(sem("gate_diag_done"), 1)
                dve.wait_ge(sem("post_gain_in"), 16 * run + 48)
                dve.wait_ge(sem("gate_row_prod"), run + 1)
                ch.link(dve.tensor_tensor(post_row[:], ps[:, 0:2, :].rearrange("p b n -> p (b n)"), gain_row[:], ALU.mult))

            R10.panel_done(dve, 0, 7)
            gate_row(0)
            post_norm("mix_post2", acc, 3, lambda t: dve.wait_ge(sem(f"x_in{t}"), 48))
            norm_split("n4", act_hi, act_lo)
            ffn_sums(R11, 1)
            gate_row(1)
            post_norm("ffn_post2", acc, 4, lambda t: None)


def kernel(**inputs):
    from concourse import bacc
    from concourse.bass_utils import run_bass_kernel_spmd

    nc = bacc.Bacc("TRN2", target_bir_lowering=False, num_devices=1)
    arrays, d = {}, {}
    for name, value in list(inputs.items()) + [("consts", constants())]:
        a = np.ascontiguousarray(value)
        arrays[f"in_{name}"] = a
        d[name] = nc.dram_tensor(f"in_{name}", a.shape, mybir.dt.from_np(a.dtype), kind="ExternalInput").ap()
    out = nc.dram_tensor("out_0", [1, SEQ, D], F32, kind="ExternalOutput").ap()
    two_blocks(nc, d, out)
    r = run_bass_kernel_spmd(nc, [arrays], core_ids=[0])
    return r.results[0]["out_0"]
```

```python
import math
from contextlib import ExitStack

import concourse.bass as bass
import numpy as np
from concourse import mybir

F32 = mybir.dt.float32
F32R = mybir.dt.float32r
I32 = mybir.dt.int32
ALU = mybir.AluOpType
ACT = mybir.ActivationFunctionType
AX_X = mybir.AxisListType.X

P = 128
D = 1024
SEQ = 1024
NT = SEQ // P
KD = D // P
HALF = 512
EPS = 1e-6
D_FF = 4 * D

GDN_HEADS = 4
CHUNK = 64
GDN_W = GDN_HEADS * P
CONV_W = 4
MLA_HEADS = 8
NOPE = 64
ROPE = 32
DQK = NOPE + ROPE
V_DIM = 64
Q_RANK = 256
KV_RANK = 128
ROPE_THETA = 10000.0
GATE_COL = 3 * GDN_W
TAIL_COL = 4 * GDN_W
TAIL_W = 2 * GDN_HEADS + Q_RANK + KV_RANK + ROPE
LAT_CQ = 2 * GDN_HEADS
LAT_CKV = LAT_CQ + Q_RANK
LAT_KR = LAT_CKV + KV_RANK
GDN_PANELS = 3 * GDN_HEADS

CONV2 = 512
CONV2_TAPS = 3
CONV2_PANELS = CONV2 // P
CONV2_ORDER = (1, 2, 0)
SB_HEADS = 8
SB_DIM = 64
IN2_Q = 3 * CONV2
IN2_K = IN2_Q + 512
IN2_V = IN2_K + 512
IN2_GA = IN2_V + 512
IN2_GB = IN2_GA + D
N_MOD = 6

FFN_STEPS = D_FF // 256
FFN_CREDIT = 2
ADA_STEP = N_MOD * KD // FFN_STEPS
MLA_GROUPS = sum(2 * (t // 4 + 1) for t in range(NT))

SB_PAIRS = SB_HEADS // 2
SB_ITEMS = 2 * NT
SB_PROJECT = (3, 6, 9, 12)
SB_SLOTS = 4
SB_LAG_ARG, SB_LAG_EXP, SB_LAG_TURN, SB_LAG_PV = 1, 2, 3, 4


def sb_groups(s):
    first = sum(u // 2 // 4 + 1 for u in range(s))
    return range(first, first + s // 2 // 4 + 1)


SB_GROUPS = sb_groups(SB_ITEMS - 1)[-1] + 1

GDN_PAIRS = NT // 2

MLA_PAIRS = MLA_HEADS // 2
MLA_ITEMS = 2 * NT
MLA_LAG_TURN, MLA_LAG_PV = 2, 3
PROBS = 4
LAT_BANKS = (7, 0, 1, 2, 3, 6, 4, 5)


def mla_tile(s):
    return NT - 1 - s % NT


def mla_groups(s):
    first = sum(mla_tile(u) // 4 + 1 for u in range(s))
    return range(first, first + mla_tile(s) // 4 + 1)


def lagged(i, before, s, lag, items):
    if s >= lag:
        return i, s - lag
    return None if before is None else (before, items + s - lag)


TWO_PI = 2 * math.pi
TWO_PI_MID = math.floor((TWO_PI - 6.28125) * 2 ** 21) / 2 ** 21
TWO_PI_PARTS = (6.28125, TWO_PI_MID, TWO_PI - 6.28125 - TWO_PI_MID)
ROUND = 1.5 * 2.0 ** 23
PI_BELOW = 3.1415925

C_ID, C_ONES, C_CSUM, C_STRICT, C_CHUNK = 0, 128, 256, 384, 512
LEVELS = (1, 2, 4, 8, 16, 32)
C_LEVEL = 640
C_KEYCAP = C_LEVEL + P * len(LEVELS)
C_FREQ = C_KEYCAP + P
C_SIGN = C_FREQ + 1
C_QUARTER = C_SIGN + 1
C_QUARTER_ANGLE = C_QUARTER + 1
N_CONST = C_QUARTER_ANGLE + 1

V_MIXPRE, V_FFNPRE, V_QN, V_KVN, V_CONV = 0, 8, 16, 18, 19
V_GPREMIX2 = V_CONV + CONV_W * GDN_PANELS
V_GPREMLP2 = V_GPREMIX2 + KD
V_CONV2 = V_GPREMLP2 + KD
N_VEC = V_CONV2 + CONV2_TAPS * (CONV2 // P)
N_BADA = N_MOD * KD
N_VEC2 = N_BADA + KD


def constants():
    c = np.zeros((P, N_CONST), np.float32)
    r, k = np.arange(P)[:, None], np.arange(P)[None, :]
    same = r // CHUNK == k // CHUNK
    c[:, C_ID:C_ID + P] = r == k
    c[:, C_ONES:C_ONES + P] = 1.0
    c[:, C_CSUM:C_CSUM + P] = same & (r <= k)
    c[:, C_STRICT:C_STRICT + P] = same & (k < r)
    c[:, C_CHUNK:C_CHUNK + P] = same
    for n, s in enumerate(LEVELS):
        c[:, C_LEVEL + n * P:C_LEVEL + (n + 1) * P] = ((k // s) % 2 == 1) & (r // s == k // s - 1)
    c[:, C_KEYCAP:C_KEYCAP + P] = np.where(k < r, 3e38, -1e30)
    j = np.arange(ROPE // 2)
    freq = (ROPE_THETA ** (-2.0 * j / ROPE)).astype(np.float32)
    c[NOPE:P, C_FREQ] = np.tile(freq, 4)
    c[NOPE:DQK, C_SIGN] = 1.0
    c[DQK:P, C_SIGN] = np.repeat([-1.0, 1.0], ROPE // 2)
    c[NOPE:DQK, C_QUARTER] = 0.25
    c[NOPE:DQK, C_QUARTER_ANGLE] = 0.25 * TWO_PI
    return c


class Ring:

    SLOTS = 4

    def __init__(self, sem, total, raws, his, los, after=None):
        self.raw, self.hi, self.lo = raws, his, los
        self.nraw, self.nslab, self.total = len(raws), len(his), total
        self.raw_full = [sem(f"w_raw_full{r}") for r in range(self.SLOTS)]
        self.carrier = sem("wait_carrier")
        self.hi_done, self.split_done, self.used = sem("w_hi_done"), sem("w_split_done"), sem("w_slab_used")
        self.base = after.base + after.total if after else 0
        self.first_raw = min(self.nraw, after.nraw) if after else self.nraw
        self.first_slab = min(self.nslab, after.nslab) if after else self.nslab
        self.fills = after.fills_after if after else [0] * self.SLOTS
        self.fills_after = [self.fills[r] + (len(range(r, total, self.nraw)) if r < self.nraw else 0)
                            for r in range(self.SLOTS)]

    def credit(self, eng):
        eng.sem_inc(self.split_done, self.SLOTS)
        eng.sem_inc(self.used, self.SLOTS)

    def start(self, sp):
        sp.wait_ge(self.split_done, self.SLOTS + self.base)

    def start_split(self, pool):
        pool.wait_ge(self.used, self.SLOTS + self.base)

    def behind(self, n0, j, first, slots):
        return first if isinstance(n0, int) and n0 + j < slots else slots

    def load(self, sp, n0, j, view, src):
        r = j % self.nraw
        sp.wait_ge(self.split_done, n0 + (self.SLOTS + self.base + j - self.behind(n0, j, self.first_raw, self.nraw) + 1))
        sp.sem_inc(self.carrier, 1)
        sp.dma_start(view(self.raw[r]), src).then_inc(self.raw_full[r], 16)

    def split(self, pool, n0, trips, j, width=1024):
        r, s = j % self.nraw, j % self.nslab
        pool.wait_ge(self.raw_full[r], trips * 16 + (self.fills[r] * 16 + 16))
        pool.wait_ge(self.used, n0 + (self.SLOTS + self.base + j - self.behind(n0, j, self.first_slab, self.nslab) + 1))
        pool.sem_inc(self.carrier, 1)
        pool.tensor_scalar(self.hi[s][:, 0:width], self.raw[r][:, 0:width], 1.0, 0.0, ALU.mult, ALU.add)\
            .then_inc(self.hi_done, 1)
        pool.wait_ge(self.hi_done, n0 + (self.base + j + 1))
        pool.tensor_tensor(self.lo[s][:, 0:width], self.raw[r][:, 0:width], self.hi[s][:, 0:width].bitcast(F32),
                           ALU.subtract).then_inc(self.split_done, 1)

    def ready(self, pe, n0, j):
        pe.wait_ge(self.split_done, n0 + (self.SLOTS + self.base + j + 1))

    def panel_done(self, eng, n0, j):
        eng.wait_ge(self.used, n0 + (self.SLOTS + self.base + j + 1))


class Chain:

    def __init__(self, eng, s):
        self.eng, self.s, self.base, self.n = eng, s, 0, 0

    def link(self, ins):
        ins.then_inc(self.s, 1)
        self.n += 1
        self.eng.wait_ge(self.s, self.base + self.n)

    def loop(self, i, per):
        self.start = self.base + self.n
        self.base, self.n, self.per = self.start + i * per, 0, per

    def end(self, trips):
        assert self.n == self.per, (self.n, self.per)
        self.base, self.n = self.start + trips * self.per, 0


def two_blocks(nc, d, out):
    ctx = ExitStack()
    with ctx:
        sems = {}

        def sem(name):
            if name not in sems:
                sems[name] = ctx.enter_context(nc.semaphore(name))
            return sems[name]

        SB0 = 16512

        def sb(name, kb, shape, dt=F32):
            t = nc.alloc_sbuf_tensor_at(name, list(shape), dt, offset=SB0 + int(kb * 1024))
            return t

        consts = sb("consts", 0, [P, N_CONST])
        vec = sb("vec_cols", 6.75, [P, N_VEC])
        vec2 = sb("vec2_cols", 7.25, [P, N_VEC2])
        mod = sb("mod_cols", 7.53125, [P, N_BADA])
        ssq = sb("ssq", 7.75, [P, NT])
        rstd = sb("rstd", 7.78125, [P, NT])
        mean_sq = sb("mean_sq", 7.8125, [P, NT])
        scale2 = sb("scale2_cols", 7.84375, [P, 2 * KD])
        half_neg = sb("minus_half", 7.90625, [P, 64])
        ident = consts[:, C_ID:C_ID + P]
        ones = consts[:, C_ONES:C_ONES + P]

        raws = [sb(f"raw{r}", 9 + 4 * r, [P, 1024]) for r in range(4)]
        slab_hi = [sb(f"slab_hi{s}", 25 + 8 * s, [P, 1024], F32R) for s in range(4)]
        slab_lo = [sb(f"slab_lo{s}", 29 + 8 * s, [P, 1024], F32R) for s in range(4)]

        acc = sb("acc", 57, [P, NT, D])
        act_lo = sb("act_lo", 89, [P, KD, SEQ], F32R)
        act_hi = sb("act_hi", 121, [P, KD, SEQ], F32R)
        resid = sb("resid", 153, [P, NT, D])
        norm_tmp = [sb(f"norm_tmp{i}", 199 + 2 * i, [P, HALF]) for i in range(4)]
        junk = [sb(f"squares_junk{i}", 189 + 4 * i, [P, D]) for i in range(2)]
        junk_ffn = [sb(f"squares_junk_ffn{i}", 121 + 4 * i, [P, D]) for i in range(2)]
        x_tok = sb("x_tok", 121, [P, NT, D])
        in_hi = sb("in_hi", 57, [P, KD, SEQ], F32R)
        in_lo = sb("in_lo", 89, [P, KD, SEQ], F32R)
        qkv = sb("qkv_feat", 121, [P, GDN_PANELS, SEQ])
        gate = sb("gate_tok", 169, [P, NT, GDN_W])
        lat = sb("lat_tok", 185, [P, NT, TAIL_W + ROPE])
        gate_tanh = [sb(f"gate_tanh{i}", 203 + 2 * i, [P, HALF]) for i in range(2)]
        out_norm_row = sb("out_norm_row", 49, [P, P])
        xpad = sb("conv_in", 199.25, [P, SEQ + CONV_W - 1])
        conv_y = sb("conv_y", 49, [P, SEQ])
        conv_t = sb("conv_tanh", 53, [P, SEQ])
        ss_gdn = sb("ss_gdn", 203.5, [P, NT, GDN_PANELS])
        vec_rows = sb("vec_rows", 185, [P, P])
        vec2_rows = sb("vec2_rows", 185.5, [P, P])
        mix = sb("mix_tok", 57, [P, NT, D])
        cq_f = sb("cq_feat", 89, [P, 2, SEQ])
        ckv_f = sb("ckv_feat", 97, [P, SEQ])
        trig = sb("rope_trig", 21, [P, SEQ])
        v_t = sb("v_tok", 101, [P, NT, MLA_HEADS, V_DIM])
        rope_t = sb("rope_tmp", 117, [P, SEQ])
        q_f = [sb("q_feat0", 49, [P, SEQ]), sb("q_feat1", 29, [P, SEQ])]
        k_f = [sb("k_feat0", 53, [P, SEQ]), sb("k_feat1", 33, [P, SEQ])]
        probs = [sb(f"probs{i}", kb, [P, SEQ]) for i, kb in enumerate((9, 13, 17, 25))]
        probs_t = [sb(f"probs_t{i}", 41 + 2 * i, [P, HALF]) for i in range(2)]
        wq = [sb(f"wq_head{i}", 37 + 1.25 * i, [P, 2, P]) for i in range(2)]
        wk = [sb(f"wk_head{i}", 38 + 1.25 * i, [P, NOPE]) for i in range(2)]
        w_kv = sb("w_kv_all", 45, [P, 1024])
        sm_max = [sb(f"sm_max{i}", 40 + 0.125 * i, [P, NT]) for i in range(2)]
        sm_neg = [sb(f"sm_neg{i}", 40.03125 + 0.125 * i, [P, NT]) for i in range(2)]
        sm_sum = [sb(f"sm_sum{i}", 40.0625 + 0.125 * i, [P, NT]) for i in range(2)]
        sm_rec = [sb(f"sm_rec{i}", 40.09375 + 0.125 * i, [P, NT]) for i in range(2)]
        lat_junk = [sb(f"lat_junk{i}", 199.25 + 1.5 * i, [P, Q_RANK + KV_RANK]) for i in range(2)]
        lat_ss = sb("lat_ss", 204.25, [P, 2 * NT])
        lat_ms = sb("lat_ms", 204.3125, [P, 2 * NT])
        lat_rstd = sb("lat_rstd", 204.375, [P, 2 * NT])
        pos_i = sb("pos_i", 53, [P, SEQ], I32)
        ang = sb("rope_ang", 49, [P, SEQ])
        turns = sb("rope_turns", 53, [P, SEQ])

        def small(name, slot):
            return sb(name, 205.5 + 0.125 * slot, [P, NT, GDN_HEADS])

        g_arg, g_exp, g_sp, g_la, g_beta, g_cum, g_tot, g_eg, g_ekd, g_rk, g_rq, g_bk, g_cw, g_cd, g_cv = [
            small(n, i) for i, n in enumerate(
                ["g_arg", "g_exp", "g_softplus", "g_log_a", "g_beta", "g_cumsum", "g_total", "g_exp_cum",
                 "g_exp_tail", "g_rk", "g_rq", "g_beta_rk", "g_w_scale", "g_kdec_scale", "g_v_scale"])]
        g_u = sb("g_exp_plus_1", 204.5, [P, NT, GDN_HEADS])
        a_log_b = sb("a_log_bc", 207.375, [P, GDN_HEADS])
        dt_b = sb("dt_bias_bc", 207.40625, [P, GDN_HEADS])
        ea_b = sb("exp_a_log", 207.4375, [P, GDN_HEADS])

        def head_tile(name, kb):
            return sb(name, kb, [P, GDN_HEADS, P])

        def tile_pair(name, kb):
            return [head_tile(f"{name}{a}", kb + 2 * a) for a in range(2)]

        k_s, v_s, e_d, e_g = (tile_pair(n, 9 + 4 * x) for x, n in enumerate(("k_tile", "v_tile", "decay", "exp_g_row")))
        k_w, v_b = k_s, v_s
        a_t, y_s = tile_pair("a_T", 25), tile_pair("level_y", 29)
        m_s = [tile_pair(f"a_level{n}_", 33 + 4 * n) for n in range(2)]
        t_f = [tile_pair(f"t_inv{n}_", 41 + 4 * n) for n in range(2)]
        t_r = [tile_pair(f"t_inv_T{n}_", 49 + 4 * n) for n in range(2)]
        w_t, u_s, q_d, k_d, p_t = (tile_pair(n, 89 + 4 * x) for x, n in enumerate(("w_T", "u", "q_dec", "k_dec", "p_T")))
        state = tile_pair("state", 109)
        v_n, s_dec, o_s, o_sq = (head_tile(n, 113 + 2 * x) for x, n in enumerate(("v_new", "state_dec", "o_tok", "o_sq")))
        u_g, i_b = tile_pair("cumsum_la", 185), tile_pair("ident_bk", 190)
        e_last = [sb(f"exp_g_last{a}", 189.125 + 0.0625 * a, [P, GDN_HEADS, 2]) for a in range(2)]
        o_ss = sb("o_ss", 189, [P, GDN_HEADS])
        o_ms = sb("o_ms", 189.03125, [P, GDN_HEADS])
        o_rstd = sb("o_rstd", 189.0625, [P, GDN_HEADS])

        hid_hi = sb("hid_hi", 185, [P, 2, SEQ], F32R)
        hid_lo = sb("hid_lo", 193, [P, 2, SEQ], F32R)
        relu_t = [sb(f"relu{i}", 201 + 2 * i, [P, HALF]) for i in range(2)]
        relu_sq = sb("relu_sq", 205, [P, HALF])
        mixt_hi = sb("mixt_hi", 89, [P, KD, SEQ], F32R)
        mixt_lo = sb("mixt_lo", 121, [P, KD, SEQ], F32R)
        mix_post_row = sb("mix_post_row", 185, [P, D])
        ffn_post_row = sb("ffn_post_row", 21, [P, D])
        gate_rows = [sb(f"gate_row{i}", 17 + 4 * i, [P, D]) for i in range(2)]

        ada = [sb(f"w_ada{i}", 17 + 4 * i, [P, KD, P]) for i in range(2)]
        cg_t = sb("c_gate", 193, [P, SEQ])
        conv2_y = sb("conv2_y", 197, [P, SEQ])
        vpad = sb("conv2_in", 203, [P, SEQ + CONV2_TAPS - 1])
        y_hi = sb("conv2_out_hi", 57, [P, CONV2_PANELS, SEQ], F32R)
        y_lo = sb("conv2_out_lo", 73, [P, CONV2_PANELS, SEQ], F32R)
        merged = sb("merged_feat", 153, [P, KD, SEQ])
        conv_gate = [sb(f"conv_gate{i}", 185 + 4 * i, [P, SEQ]) for i in range(2)]
        v2 = sb("v2_tok", 185, [P, NT, SB_HEADS, SB_DIM])
        q2, k2 = sb("q2_feat", 17, [P, SEQ]), sb("k2_feat", 21, [P, SEQ])
        sb_z = [sb(f"sb_z{i}", 41 + 4 * i, [P, SEQ]) for i in range(2)]
        sb_w = [sb(f"sb_weights{i}", kb, [P, SEQ]) for i, kb in enumerate((49, 53, 73, 77))]
        q2_next, k2_next = sb("q2_next", 81, [P, SEQ]), sb("k2_next", 85, [P, SEQ])
        sb_at = [sb(f"sb_weights_t{i}", 201 + 2 * i, [P, HALF]) for i in range(2)]
        o2 = sb("o2_tok", 57, [P, NT, CONV2])
        o2_hi = sb("o2_feat_hi", 73, [P, CONV2_PANELS, SEQ], F32R)
        o2_lo = sb("o2_feat_lo", 185, [P, CONV2_PANELS, SEQ], F32R)
        attn_gate = [sb(f"attn_gate{i}", 57 + 4 * i, [P, SEQ]) for i in range(2)]
        attn_part = [sb(f"attn_part{i}", 65 + 4 * i, [P, SEQ]) for i in range(2)]
        diag = sb("gate_diag", 203, [P, KD, P])

        ps = ctx.enter_context(nc.psum_tensor("ps", [P, 8, HALF], F32))

        R1 = Ring(sem, 8, raws[:3], slab_hi[:3], slab_lo[:3])
        R2 = Ring(sem, GDN_PANELS, raws[:3], slab_hi[:3], slab_lo[:3], R1)
        R3 = Ring(sem, 16, raws, slab_hi, slab_lo, R2)
        R4 = Ring(sem, 4 * FFN_STEPS, raws[:2], slab_hi, slab_lo, R3)
        R5 = Ring(sem, 3 * CONV2_PANELS, raws[:3], slab_hi[:3], slab_lo[:3], R4)
        R6 = Ring(sem, 2 * KD, raws, slab_hi, slab_lo, R5)
        R7 = Ring(sem, 4, raws, slab_hi, slab_lo, R6)
        R8 = Ring(sem, SB_HEADS, raws[:2], slab_hi[:2], slab_lo[:2], R7)
        R9 = Ring(sem, 2 * KD, raws, slab_hi, slab_lo, R8)
        R10 = Ring(sem, 16, raws[:2], slab_hi, slab_lo, R9)
        R11 = Ring(sem, 4 * FFN_STEPS, raws[:2], slab_hi, slab_lo, R10)

        MERGE_GATES = ((6, 0), (0, 2))
        MERGE_PROJS = ((2, 4), (4, 6))

        EARLY, LATE = range(NT // 2), range(NT // 2, NT)
        FFN_NORMS = []
        for t in range(NT + 3):
            FFN_NORMS += [("ffn_post", t)] * (t < NT) + [("n3", t - 3)] * (t >= 3)
        NORM_ORDER = [("n1", t) for t in range(NT)]
        for halves in (("mix_post", "n2"), None, ("mix_post2", "n4")):
            NORM_ORDER += [(tag, t) for part in (EARLY, LATE) for tag in halves for t in part] if halves else FFN_NORMS
        NORM_ORDER += [("ffn_post2", t) for t in range(NT)]
        NORM_AT = {key: n for n, key in enumerate(NORM_ORDER)}
        TURNS = {"n1": 0, "mixt": 16, "n2": 32, "n3": 48, "sb_o": 64, "n4": 72}
        SCALES = ["n1", "n2", "n3", "n4"]

        def turn_bank(tag, h, k):
            return 4 + k if tag == "sb_o" else 4 * h + k % 4

        SHIFTED = ["n3", "n4"]

        x1_spill = nc.dram_tensor("x1_spill", [NT, P, D], F32, kind="Internal").ap()
        w_in2 = d["w_in_2"][0].rearrange("(k p) n -> p k n", p=P)
        w_pc = d["w_proj_conv_2"][0].rearrange("(k p) n -> p k n", p=P)
        w_pa = d["w_proj_attn_2"][0].rearrange("(k p) n -> p k n", p=P)
        w_out2 = d["w_out_2"][0].rearrange("(k p) n -> p k n", p=P)
        w_up2 = d["w_mlp_in_2"][0].rearrange("(k p) n -> p k n", p=P)
        w_ada = d["w_ada_2"][0].rearrange("(k p) n -> p k n", p=P)
        w_in = d["w_in"][0].rearrange("(k p) n -> p k n", p=P)
        w_out = d["w_out"][0].rearrange("(k p) n -> p k n", p=P)
        w_up = d["w_up"][0].rearrange("(k p) n -> p k n", p=P)
        w_down = d["w_down"][0].rearrange("(s p) n -> s p n", p=P)
        w_down2 = d["w_mlp_out_2"][0].rearrange("(s p) n -> s p n", p=P)
        x_tiles = d["x"][0].rearrange("(t p) d -> t p d", p=P)
        T_COLS = [(GATE_COL, HALF), (TAIL_COL, TAIL_W)]

        def mix_pre_gain(k):
            return vec[:, V_MIXPRE + k:V_MIXPRE + k + 1]

        def half_view(n):
            return lambda raw: raw[:, 0:2 * n].rearrange("p (j n) -> p j n", j=2)

        def panel_view(raw):
            return raw[:, :].rearrange("p (k n) -> p k n", n=P)

        block = ctx.enter_context(nc.Block())

        @block.sync
        def _(sp):
            def x_load(t):
                sp.dma_start(x_tok[:, t, :], x_tiles[t]).then_inc(sem(f"x_in{t}"), 16)

            def token_slab(m):
                (col, n), j = T_COLS[m // 4], m % 4
                R1.load(sp, 0, m, half_view(n), w_in[:, 2 * j:2 * j + 2, col:col + n])

            for t in EARLY:
                x_load(t)
            sp.dma_start(consts[:], d["consts"]).then_inc(sem("consts_in"), 16)
            for name, row, n in (("mix_pre_norm", V_MIXPRE, KD), ("ffn_pre_norm", V_FFNPRE, KD), ("q_norm", V_QN, 2),
                                 ("kv_norm", V_KVN, 1), ("g_pre_mix_2", V_GPREMIX2, KD),
                                 ("g_pre_mlp_2", V_GPREMLP2, KD)):
                sp.dma_start(vec_rows[row:row + n, :], d[name][0].rearrange("(k p) -> k p", p=P))\
                    .then_inc(sem("vec_in"), 16)
            sp.dma_start(vec_rows[V_CONV:V_CONV + CONV_W * GDN_PANELS, :],
                         d["conv_w"][0].rearrange("w (k p) -> (w k) p", p=P)).then_inc(sem("vec_in"), 16)
            sp.dma_start(vec_rows[V_CONV2:N_VEC, :],
                         d["conv_w_2"][0].rearrange("w (k p) -> (w k) p", p=P)).then_inc(sem("vec_in"), 16)
            sp.dma_start(vec2_rows[0:N_BADA, :], d["b_ada_2"][0].rearrange("(k p) -> k p", p=P))\
                .then_inc(sem("vec_in"), 16)
            sp.dma_start(vec2_rows[N_BADA:N_VEC2, :], d["c_2"][0].rearrange("(k p) -> k p", p=P))\
                .then_inc(sem("vec_in"), 16)
            token_slab(0)
            for t in LATE:
                x_load(t)
            for m in range(1, 4):
                token_slab(m)
            sp.dma_start(a_log_b[:], d["a_log"][0].partition_broadcast(P)).then_inc(sem("gdn_vec_in"), 16)
            sp.dma_start(dt_b[:], d["dt_bias"][0].partition_broadcast(P)).then_inc(sem("gdn_vec_in"), 16)
            sp.dma_start(out_norm_row[:], d["gdn_out_norm"][0].partition_broadcast(P)).then_inc(sem("gdn_vec_in"), 16)
            sp.dma_start(pos_i[NOPE:P, :], d["positions"][0].partition_broadcast(P - NOPE)).then_inc(sem("pos_in"), 16)
            for m in range(4, 8):
                token_slab(m)
            R2.start(sp)
            with sp.Fori(0, GDN_PANELS // 3) as i:
                for j in range(3):
                    R2.load(sp, 3 * i, j, panel_view, w_in[:, :, bass.ds((3 * i + j) * P, P)])
            R2.panel_done(sp, 0, GDN_PANELS - 1)
            w_q_up = d["w_q_up"][0].rearrange("(k p) n -> p k n", p=P)
            sp.dma_start(w_kv[:], d["w_kv_up"][0]).then_inc(sem("w_kv_in"), 16)
            with sp.Fori(0, MLA_PAIRS) as i:
                for a in range(2):
                    c, half = (2 * i + a) * DQK, ROPE // 2
                    parts = ((wq[a][:, :, 0:DQK], w_q_up[:, :, bass.ds(c, DQK)]),
                             (wq[a][:, :, DQK:DQK + half], w_q_up[:, :, bass.ds(c + NOPE + half, half)]),
                             (wq[a][:, :, DQK + half:P], w_q_up[:, :, bass.ds(c + NOPE, half)]),
                             (wk[a][:], d["w_kv_up"][0][:, bass.ds((2 * i + a) * P, NOPE)]))
                    sp.wait_ge(sem("mla_proj"), 8 * i + (4 * a + 1))
                    for dst, src in parts:
                        sp.dma_start(dst, src).then_inc(sem(f"mla_w_in{a}"), 16)

            def projection_load(ring, w, m):
                c, j = m // 4 % 2, m % 4
                ring.load(sp, 0, m, half_view(HALF), w[:, 2 * j:2 * j + 2, c * HALF:(c + 1) * HALF])

            sp.wait_ge(sem("gdn_out_done"), NT)
            for m in range(16):
                projection_load(R3, w_out, m)
                if m == 3:
                    for t in range(NT):
                        sp.dma_start(resid[:, t, :], x_tiles[t]).then_inc(sem(f"x_in{t}"), 16)
                    sp.dma_start(mix_post_row[:], d["mix_post_norm"][0].partition_broadcast(P)).then_inc(sem("post_gain_in"), 16)

            def ffn_loads(ring, up, down):
                with sp.Fori(0, FFN_STEPS) as i:
                    for j in range(2):
                        ring.load(sp, 4 * i, j, panel_view, up[:, :, bass.ds((2 * i + j) * P, P)])
                    for j in range(2):
                        ring.load(sp, 4 * i, 2 + j, lambda raw: raw[:, :], down[2 * i + j])

            ffn_loads(R4, w_up, w_down)
            def w2_panel(col, j):
                return w_in2[:, :, bass.ds(col + j * P, P)]

            def conv_loads(i, slabs=range(3)):
                for j in slabs:
                    R5.load(sp, 3 * i, j, panel_view, w2_panel(CONV2_ORDER[j] * CONV2, i))

            conv_loads(0, range(2))
            sp.wait_ge(sem("ada_used"), N_MOD * KD + 2)
            conv_loads(0, range(2, 3))
            with sp.Fori(0, CONV2_PANELS - 1) as i:
                conv_loads(i + 1)

            def merge_loads(ring, gate_col, proj, i, slabs=range(4)):
                for j in slabs:
                    if j < 2:
                        ring.load(sp, 4 * i, j, panel_view, w2_panel(gate_col, 2 * i + j))
                    else:
                        ring.load(sp, 4 * i, j, lambda raw: raw[:, 0:HALF].rearrange("p (k n) -> p k n", n=P),
                                  proj[:, :, bass.ds((2 * i + j - 2) * P, P)])

            sp.wait_ge(sem("resid_done"), 2 * NT)
            merge_loads(R6, IN2_GA, w_pc, 0)
            with sp.Fori(0, KD // 2 - 1) as i:
                merge_loads(R6, IN2_GA, w_pc, i + 1)
            for j in range(4):
                R7.load(sp, 0, j, half_view(HALF), w_in2[:, 2 * j:2 * j + 2, IN2_V:IN2_V + HALF])
            with sp.Fori(0, SB_HEADS // 2) as i:
                R8.load(sp, 2 * i, 0, panel_view, w2_panel(IN2_Q, i))
                R8.load(sp, 2 * i, 1, panel_view, w2_panel(IN2_K, i))
            merge_loads(R9, IN2_GB, w_pa, 0, range(2))
            sp.wait_ge(sem("sb_o_done"), SB_HEADS + 2)
            merge_loads(R9, IN2_GB, w_pa, 0, range(2, 4))
            with sp.Fori(0, KD // 2 - 1) as i:
                merge_loads(R9, IN2_GB, w_pa, i + 1)
            for m in range(16):
                projection_load(R10, w_out2, m)
            ffn_loads(R11, w_up2, w_down2)

            out_tiles = out[0].rearrange("(t p) d -> t p d", p=P)
            for t in range(NT):
                sp.wait_ge(sem("resid_done"), 3 * NT + t + 1)
                sp.dma_start(out_tiles[t], resid[:, t, :]).then_inc(sem("out_stored"), 16)
            sp.wait_ge(sem("out_stored"), NT * 16)

        @block.gpsimd
        def _(pool):
            R1.credit(pool)
            pool.sem_inc(sem("conv_done"), 1)
            pool.sem_inc(sem("conv_in_done"), 2)
            pool.sem_inc(sem("ss_gdn_done"), 2)
            for name, credit in (("mla_proj", 5), ("proj_read", 1), ("mla_o_done", 1), ("mla_pv", 2),
                                 ("mla_exp_done", 2)):
                pool.sem_inc(sem(name), credit)
            pool.sem_inc(sem("ffn_hid"), FFN_CREDIT)
            for name, credit in (("kk_prod", 1), ("o_taken", 1), ("o_ss_done", 1), ("ada_used", 2), ("ada_read", 1), ("c2_cg_read", 1), ("c2_v_done", 1), ("c2_y_done", 1),
                                 ("m_gate_read", 2), ("m_done", 2), ("sb_z_done", 2), ("sb_o_done", 2), ("sb_pv", 2)):
                pool.sem_inc(sem(name), credit)
            pch = Chain(pool, sem("pool_chain"))
            pch.link(pool.memset(half_neg[:], -0.5))

            def norm_rstd(tag, tiles):
                for t in tiles:
                    n, col = NORM_AT[tag, t], slice(t, t + 1)
                    pool.wait_ge(sem("norm_sq_done"), n + 1)
                    pool.tensor_scalar(mean_sq[:, col], ssq[:, col], 1.0 / D, EPS, ALU.mult, ALU.add)\
                        .then_inc(sem("norm_mean_done"), 1)
                    pool.wait_ge(sem("norm_mean_done"), n + 1)
                    pool.tensor_tensor(rstd[:, col], mean_sq[:, col], half_neg[:, 0:1], ALU.pow)\
                        .then_inc(sem("norm_rstd_done"), 1)

            def post_add(run, t):
                pool.wait_ge(sem("post_scaled"), NT * run + t + 1)
                pool.tensor_tensor(resid[:, t, :], resid[:, t, :], acc[:, t, :], ALU.add).then_inc(sem("resid_done"), 1)

            def norm_hi(tag, h, ks=range(KD)):
                for k in ks:
                    n = h * KD + k
                    pool.wait_ge(sem("turn_read"), TURNS[tag] + n + 1)
                    pool.tensor_scalar(act_hi[:, k, h * HALF:(h + 1) * HALF], norm_tmp[n % 4][:], 1.0, 0.0, ALU.mult, ALU.add)\
                        .then_inc(sem("turn_hi_done"), 1)

            norm_rstd("n1", EARLY)
            for m in range(8):
                R1.split(pool, 0, m // R1.nraw, m, 2 * T_COLS[m // 4][1])
                if m == 0:
                    norm_rstd("n1", LATE)
            R2.start_split(pool)
            for j in range(3):
                R2.split(pool, 0, 0, j)
            pool.wait_ge(sem("lat_sq_done"), 2 * NT)
            pool.tensor_scalar(lat_ms[:, 0:NT], lat_ss[:, 0:NT], 1.0 / Q_RANK, EPS, ALU.mult, ALU.add)
            pch.link(pool.tensor_scalar(lat_ms[:, NT:], lat_ss[:, NT:], 1.0 / KV_RANK, EPS, ALU.mult, ALU.add))
            pool.tensor_tensor(lat_rstd[:], lat_ms[:], half_neg[:, 0:2 * NT], ALU.pow).then_inc(sem("lat_rstd_done"), 1)
            with pool.Fori(0, GDN_PANELS // 3 - 1) as i:
                for j in range(3):
                    R2.split(pool, 3 * i + 3, i + 1, j)
            pool.wait_ge(sem("ss_gdn_done"), GDN_PANELS + 2)
            pool.tensor_scalar(g_rq[:], ss_gdn[:, :, 1:1 + GDN_HEADS], float(P), 4 * EPS * P, ALU.mult, ALU.add)
            pch.link(pool.tensor_scalar(g_rk[:], ss_gdn[:, :, 1 + GDN_HEADS:1 + 2 * GDN_HEADS], 1.0, 4 * EPS,
                                        ALU.mult, ALU.add))
            expo = half_neg[:, 0:NT * GDN_HEADS].rearrange("p (t h) -> p t h", h=GDN_HEADS)
            pool.tensor_tensor(g_rk[:], g_rk[:], expo, ALU.pow).then_inc(sem("qk_norm_done"), 1)
            pool.tensor_tensor(g_rq[:], g_rq[:], expo, ALU.pow).then_inc(sem("qk_norm_done"), 1)

            def each_head(mask):
                return consts[:, mask:mask + P].unsqueeze(1).broadcast_to([P, GDN_HEADS, P])

            def by_head(cols):
                return cols.unsqueeze(2).broadcast_to([P, GDN_HEADS, P])

            def gdn_rows(i):
                for a in range(2):
                    la, bk = g_la[:, 2 * i + a, :], g_bk[:, 2 * i + a, :]
                    if not isinstance(i, int):
                        pool.wait_ge(sem("kk_prod"), 2 * i + a)
                        pool.sem_inc(sem("wait_carrier"), 1)
                    pool.tensor_tensor(u_g[a][:], each_head(C_CSUM), by_head(la), ALU.mult)
                    pool.tensor_tensor(i_b[a][:], each_head(C_ID), by_head(bk), ALU.mult).then_inc(sem("gdn_rows_in"), 1)

            def gdn_levels(i, n):
                for a in range(2):
                    if n >= 3:
                        pool.wait_ge(sem("y_prod"), 10 * i + (2 * (n - 3) + a + 1))
                    pool.wait_ge(sem("a_t_done"), 2 * i + a + 1)
                    pool.tensor_tensor(m_s[n % 2][a][:], a_t[a][:], each_head(C_LEVEL + n * P), ALU.mult)\
                        .then_inc(sem("level_done"), 1)

            def gdn_decayed_state(i, k):
                a, c = k // 2, k % 2
                pool.wait_ge(sem("e_last_done"), 2 * i + 2)
                pool.wait_ge(sem("state_done"), 4 * i + k + 1)
                pool.tensor_tensor(s_dec[:], state[c][:], e_last[a][:, :, c:c + 1].broadcast_to([P, GDN_HEADS, P]),
                                   ALU.mult).then_inc(sem("s_dec_done"), 1)

            def gdn_out_rstd(i, a):
                pool.wait_ge(sem("o_ss_done"), 2 * i + a + 2)
                pool.sem_inc(sem("wait_carrier"), 1)
                pool.tensor_scalar(o_ms[:], o_ss[:], 1.0 / P, EPS, ALU.mult, ALU.add).then_inc(sem("o_ms_done"), 1)
                pool.wait_ge(sem("o_ms_done"), 2 * i + a + 1)
                pool.tensor_tensor(o_rstd[:], o_ms[:], half_neg[:, 0:GDN_HEADS], ALU.pow).then_inc(sem("o_rstd_done"), 1)

            def gdn_pair(i, before):
                gdn_rows(i)
                for n in range(1, 3):
                    gdn_levels(i, n)
                for a in range(2):
                    pool.wait_ge(sem("a_t_done"), 2 * i + a + 1)
                    pool.tensor_tensor(e_d[a][:], e_d[a][:], each_head(C_CSUM), ALU.mult).then_inc(sem("p_decay_done"), 1)
                for n in range(1, 5):
                    if before is not None:
                        gdn_decayed_state(before, n - 1)
                    if n >= 2:
                        gdn_levels(i, n + 1)
                    if before is not None and n == 4:
                        gdn_out_rstd(before, 0)
                if before is not None:
                    gdn_out_rstd(before, 1)

            pool.wait_ge(sem("g_scales_done"), 1)
            gdn_pair(0, None)
            with pool.Fori(0, GDN_PAIRS - 1) as i:
                gdn_pair(i + 1, i)
            for k in range(4):
                gdn_decayed_state(GDN_PAIRS - 1, k)
                if k % 2:
                    gdn_out_rstd(GDN_PAIRS - 1, k // 2)

            R3.start_split(pool)
            def ffn_splits(ring, i, slabs):
                for j in slabs:
                    ring.split(pool, 4 * i, (4 // ring.nraw) * i + j // ring.nraw, j)

            def projection_splits(ring, following, post, pre):
                for m in range(12):
                    ring.split(pool, 0, m // ring.nraw, m)
                norm_rstd(post, EARLY)
                norm_rstd(pre, EARLY)
                for m in range(12, 16):
                    ring.split(pool, 0, m // ring.nraw, m)
                ffn_splits(following, 0, range(1))
                for j in range(2):
                    if pre in SHIFTED:
                        norm_hi(pre, 0, range(4 * j, 4 * j + 4))
                    ffn_splits(following, 0, range(1 + j, 2 + j))
                norm_rstd(post, LATE)
                norm_rstd(pre, LATE)
                if pre in SHIFTED:
                    norm_hi(pre, 1)
                ffn_splits(following, 0, range(3, 4))
                pool.wait_ge(sem("turn_split"), TURNS[pre] + 2 * KD)
                for t in range(NT):
                    ins = pool.memset(acc[:, t, :], 0.0)
                ins.then_inc(sem("ffn_acc"), 4)
                with pool.Fori(0, FFN_STEPS - 1) as i:
                    ffn_splits(following, i + 1, range(4))

            projection_splits(R3, R4, "mix_post", "n2")
            R5.split(pool, 0, 0, 0)
            for tag, t in FFN_NORMS:
                norm_rstd(tag, [t])
                if tag == "ffn_post" and t - 1 in EARLY:
                    post_add(0, t - 1)
                if (tag, t) == ("ffn_post", NT - 1):
                    norm_hi("n3", 0)
                    R5.split(pool, 0, 0, 1)
            norm_hi("n3", 1)
            R5.split(pool, 0, 0, 2)
            with pool.Fori(0, CONV2_PANELS - 1) as i:
                for j in range(3):
                    R5.split(pool, 3 * i + 3, i + 1, j)

            def merge_splits(ring, i, slabs=range(4)):
                for j in slabs:
                    ring.split(pool, 4 * i, i, j, 1024 if j < 2 else HALF)

            merge_splits(R6, 0)
            with pool.Fori(0, KD // 2 - 1) as i:
                merge_splits(R6, i + 1)
            for j in range(4):
                R7.split(pool, 0, 0, j)
            def sb_stage(i):
                if not isinstance(i, int):
                    pool.wait_ge(sem("sb_scores"), SB_ITEMS * i)
                for n in (0, 2, 1, 3):
                    j, cols = n // 2, slice(n % 2 * HALF, (n % 2 + 1) * HALF)
                    pool.wait_ge(sem("proj_read"), 4 * i + (4 * MLA_HEADS + n + 2))
                    pool.sem_inc(sem("wait_carrier"), 1)
                    pool.tensor_scalar((q2, k2)[j][:, cols], (q2_next, k2_next)[j][:, cols], 1.0, 0.0, ALU.mult, ALU.add)\
                        .then_inc(sem("sb_qk_done"), 1)

            for j in range(2):
                R8.split(pool, 0, 0, j)
            sb_stage(0)
            with pool.Fori(0, SB_PAIRS - 1) as i:
                for j in range(2):
                    R8.split(pool, 2 * i + 2, i + 1, j)
                sb_stage(i + 1)
            merge_splits(R9, 0, range(2))
            pool.wait_ge(sem("sb_o_done"), SB_HEADS + 2)
            merge_splits(R9, 0, range(2, 4))
            with pool.Fori(0, KD // 2 - 1) as i:
                merge_splits(R9, i + 1)
            projection_splits(R10, R11, "mix_post2", "n4")
            for t in range(NT):
                norm_rstd("ffn_post2", [t])
                if t - 1 in EARLY:
                    post_add(1, t - 1)

        @block.tensor
        def _(pe):
            def turn(tag, src, h, ready, nk=KD, ks=None):
                for k in ks or range(nk):
                    n = TURNS[tag] + h * nk + k
                    ready(k)
                    if k >= 4 or (h and tag == "sb_o"):
                        pe.wait_ge(sem("turn_split"), n - 3)
                    for j in range(4):
                        mm = pe.transpose(ps[:, turn_bank(tag, h, k), j * P:(j + 1) * P],
                                          src[:, 4 * h + j, k * P:(k + 1) * P], ident)
                    mm.then_inc(sem("turned"), 1)

            def scaled(tag, h):
                return lambda k: pe.wait_ge(sem("norm_scaled"), NT * SCALES.index(tag) + 4 * h + 4)

            def turn_done(tag, h, nk=KD):
                pe.wait_ge(sem("turn_split"), TURNS[tag] + (h + 1) * nk)

            def as_split(tag, h):
                return lambda k: pe.wait_ge(sem("turn_split"), TURNS[tag] + h * KD + max(k, 0 if h else 4) + 1)

            def panel(hi, lo, a_hi, a_lo, banks, nk, done, halves=(0, 1), ready=None):
                for h in halves:
                    o = ps[:, banks[h], :]
                    cols = slice(h * HALF, (h + 1) * HALF)
                    for k in range(nk):
                        w = slice(k * P, (k + 1) * P)
                        if ready:
                            ready(k)
                        pe.matmul(o, hi[:, w], a_hi[:, k, cols], start=(k == 0), stop=False)
                        pe.matmul(o, hi[:, w], a_lo[:, k, cols], start=False, stop=False)
                        mm = pe.matmul(o, lo[:, w], a_hi[:, k, cols], start=False, stop=(k == nk - 1))
                    if done[h]:
                        mm.then_inc(done[h], 1)

            def token_chunk(ring, n0, width, a_hi, a_lo, bank_free, done):
                for j in range(4):
                    ring.ready(pe, 0, n0 + j)
                    hi, lo = ring.hi[(n0 + j) % ring.nslab], ring.lo[(n0 + j) % ring.nslab]
                    for t in range(NT):
                        o = ps[:, t, 0:width]
                        if j == 0:
                            bank_free(t)
                        for m in range(2):
                            k = 2 * j + m
                            w = slice(m * width, (m + 1) * width)
                            a = slice(t * P, (t + 1) * P)
                            pe.matmul(o, a_hi[:, k, a], hi[:, w], start=(k == 0), stop=False)
                            pe.matmul(o, a_lo[:, k, a], hi[:, w], start=False, stop=False)
                            mm = pe.matmul(o, a_hi[:, k, a], lo[:, w], start=False, stop=(k == KD - 1))
                        if t == NT - 1:
                            mm.then_inc(ring.used, 1)
                        elif j == 3:
                            mm.then_inc(done, 1)

            pe.wait_ge(sem("consts_in"), 16)
            pe.wait_ge(sem("vec_in"), 160)
            pe.transpose(ps[:, 4, 0:N_VEC], vec_rows[0:N_VEC, :], consts[0:N_VEC, C_ID:C_ID + N_VEC])
            pe.transpose(ps[:, 4, 256:256 + N_VEC2], vec2_rows[0:N_VEC2, :], consts[0:N_VEC2, C_ID:C_ID + N_VEC2])\
                .then_inc(sem("vec_turned"), 1)
            turn("n1", x_tok, 0, scaled("n1", 0))
            turn_done("n1", 0)

            def late_half(t):
                if t == NT // 2:
                    pe.wait_ge(sem("vec_cols_done"), 2)
                    turn("n1", x_tok, 1, scaled("n1", 1))
                    turn_done("n1", 1)

            token_chunk(R1, 0, HALF, in_hi, in_lo, late_half, sem("gate_prod"))
            token_chunk(R1, 4, TAIL_W, in_hi, in_lo, lambda t: pe.wait_ge(sem("gate_silu"), t + 1), sem("tail_prod"))
            pe.wait_ge(sem("lat_done"), NT)
            with pe.Fori(0, GDN_PANELS // 3) as i:
                for j in range(3):
                    p = 3 * i + j
                    R2.ready(pe, 3 * i, j)
                    pe.wait_ge(sem("conv_in_done"), p + 1)
                    b = 2 * j
                    panel(R2.hi[j], R2.lo[j], in_hi, in_lo, (b, b + 1), KD, (sem("panel_half"), R2.used))
                    pe.wait_ge(sem("conv_sq_done"), p + 1)
                    pe.wait_ge(sem("ss_gdn_done"), p + 2)
                    for t in range(NT):
                        mm = pe.matmul(ps[:, 6, t:t + 1], conv_t[:, t * P:(t + 1) * P], ones[:, 0:1],
                                       start=True, stop=True)
                    mm.then_inc(sem("ss_prod"), 1)
            pe.wait_ge(sem("lat_norm_done"), 1)
            for n, b in enumerate(LAT_BANKS):
                kind, h = n // 2, n % 2
                c0 = (LAT_CQ, LAT_CQ + P, LAT_CKV, TAIL_W + ROPE - P)[kind]
                if b == 6:
                    pe.wait_ge(sem("ss_gdn_done"), GDN_PANELS + 2)
                elif b < 6:
                    pe.wait_ge(sem("conv_in_done"), GDN_PANELS + b // 2)
                for j in range(4):
                    mm = pe.transpose(ps[:, b, j * P:(j + 1) * P], lat[:, 4 * h + j, c0:c0 + P], ident)
                mm.then_inc(sem("lat_turned"), 1)
            pe.wait_ge(sem("w_kv_in"), 16)
            pe.wait_ge(sem("lat_feat_done"), 6)
            pe.wait_ge(sem("mla_k_rope_done"), 1)
            w_v = w_kv[:].rearrange("p (h c) -> p h c", c=P)[:, :, NOPE:P]
            for t in range(NT):
                pe.matmul(ps[:, t, :].rearrange("p (h e) -> p h e", e=V_DIM), ckv_f[:, t * P:(t + 1) * P], w_v,
                          start=True, stop=True).then_inc(sem("v_prod"), 1)
            pe.wait_ge(sem("log_a_done"), 1)
            pe.wait_ge(sem("v_done"), NT)
            n_gh = NT * GDN_HEADS
            la = g_la[:].rearrange("p t h -> p (t h)")
            pe.matmul(ps[:, 0, 0:n_gh], consts[:, C_CSUM:C_CSUM + P], la, start=True, stop=True)
            pe.matmul(ps[:, 0, n_gh:2 * n_gh], consts[:, C_CHUNK:C_CHUNK + P], la, start=True, stop=True)\
                .then_inc(sem("cumsum_prod"), 1)
            pe.wait_ge(sem("cumsum_done"), 2)

            def mla_project(i, h, n):
                a, cols = h % 2, slice(n % 2 * HALF, (n % 2 + 1) * HALF)
                if n == 0:
                    pe.wait_ge(sem(f"mla_w_in{a}"), 64 * i + (64 * (h // 2) + 64))
                pe.wait_ge(sem("proj_read"), 8 * i + (4 * h + n + 1))
                if n == 1 or n == 2:
                    pe.wait_ge(sem("mla_rope_done"), 4 * i + (2 * h + n))
                if n < 2:
                    for k in range(2):
                        mm = pe.matmul(ps[:, 7, :], wq[a][:, k, :], cq_f[:, k, cols], start=(k == 0), stop=(k == 1))
                else:
                    mm = pe.matmul(ps[0:NOPE, 7, :], wk[a][:], ckv_f[:, cols], start=True, stop=True)
                mm.then_inc(sem("mla_proj"), 1)

            def mla_scores(i, s):
                t, a = mla_tile(s), s // NT
                n = (t + 1) * P
                if s % NT == 0:
                    pe.wait_ge(sem("proj_read"), 8 * i + (4 * a + 5))
                    pe.wait_ge(sem("mla_rope_done"), 4 * i + (2 * a + 2))
                pe.wait_ge(sem("mla_exp_done"), MLA_ITEMS * i + s + 1)
                for f in range((n + HALF - 1) // HALF):
                    w = min(HALF, n - f * HALF)
                    mm = pe.matmul(ps[:, 2 * (s % 2) + f, 0:w], q_f[a][0:DQK, t * P:(t + 1) * P],
                                   k_f[a][0:DQK, f * HALF:f * HALF + w], start=True, stop=True)
                mm.then_inc(sem("mla_scores"), 1)

            def mla_turn(i, s):
                pe.wait_ge(sem("mla_exp_done"), MLA_ITEMS * i + (s + 3))
                for n, g in enumerate(mla_groups(s)):
                    for b in range(4 * n, min(4 * n + 4, mla_tile(s) + 1)):
                        mm = pe.transpose(ps[:, 4 + g % 2, (b % 4) * P:(b % 4 + 1) * P],
                                          probs[s % PROBS][:, b * P:(b + 1) * P], ident)
                    mm.then_inc(sem("mla_turned"), 1)

            def mla_outputs(i, s):
                t, a = mla_tile(s), s // NT
                if s % NT == 0:
                    pe.wait_ge(sem("mla_o_done"), 2 * i + (a + 1))
                for n, g in enumerate(mla_groups(s)):
                    pe.wait_ge(sem("mla_pt_done"), MLA_GROUPS * i + (g + 1))
                    for b in range(4 * n, min(4 * n + 4, t + 1)):
                        mm = pe.matmul(ps[:, 6, t * V_DIM:(t + 1) * V_DIM], probs_t[g % 2][:, (b % 4) * P:(b % 4 + 1) * P],
                                       v_t[:, b, 2 * i + a, :], start=(b == 0), stop=(b == t))
                    mm.then_inc(sem("mla_pv"), 1)

            def mla_pair(i, before, last):
                for s in range(MLA_ITEMS):
                    if s + 1 < MLA_ITEMS:
                        mla_scores(i, s + 1)
                    elif not last:
                        mla_scores(i + 1, 0)
                    if late := lagged(i, before, s, MLA_LAG_PV, MLA_ITEMS):
                        mla_outputs(*late)
                    if late := lagged(i, before, s, MLA_LAG_TURN, MLA_ITEMS):
                        mla_turn(*late)
                    if 1 <= s <= 4:
                        mla_project(i, 1, s - 1)
                    elif 8 <= s <= 11 and not last:
                        mla_project(i, 2, s - 8)

            pe.wait_ge(sem("mla_k_rope_done"), 2)
            for n in range(4):
                mla_project(0, 0, n)
            mla_scores(0, 0)
            mla_pair(0, None, False)
            with pe.Fori(0, MLA_PAIRS - 2) as i:
                mla_pair(i + 1, i, False)
            mla_pair(MLA_PAIRS - 1, MLA_PAIRS - 2, True)
            for s in range(MLA_ITEMS, MLA_ITEMS + MLA_LAG_PV):
                mla_outputs(MLA_PAIRS - 1, s - MLA_LAG_PV)
                if s < MLA_ITEMS + MLA_LAG_TURN:
                    mla_turn(MLA_PAIRS - 1, s - MLA_LAG_TURN)

            def heads(bank, lhs, rhs, signal=None):
                for h in range(GDN_HEADS):
                    mm = pe.matmul(ps[:, bank, h * P:(h + 1) * P], lhs(h), rhs(h), start=True, stop=True)
                if signal:
                    mm.then_inc(sem(signal), 1)

            def turn_heads(bank, src, signal):
                for h in range(GDN_HEADS):
                    mm = pe.transpose(ps[:, bank, h * P:(h + 1) * P], src[:, h, :], ident)
                mm.then_inc(sem(signal), 1)

            def gdn_grams(i):
                for a, (b_g, b_b, b_k) in enumerate(((0, 1, 2), (3, 4, 0))):
                    pe.wait_ge(sem("gdn_rows_in"), 2 * i + a + 1)
                    pe.matmul(ps[:, b_g, :], ones, u_g[a][:].rearrange("p h t -> p (h t)"), start=True, stop=True)\
                        .then_inc(sem("g_row_prod"), 1)
                    pe.matmul(ps[:, b_b, :], consts[:, C_STRICT:C_STRICT + P], i_b[a][:].rearrange("p h t -> p (h t)"),
                              start=True, stop=True)
                    pe.wait_ge(sem("gdn_k_in"), 2 * i + a + 1)
                    if a:
                        pe.wait_ge(sem("decay_arg_done"), 2 * i + 1)
                    heads(b_k, lambda h: k_s[a][:, h, :], lambda h: k_s[a][:, h, :], "kk_prod")

            def gdn_state_products(i, k):
                a, rows = k // 2, slice(k % 2 * CHUNK, (k % 2 + 1) * CHUNK)
                pe.wait_ge(sem("state_done"), 4 * i + k + 1)
                pe.wait_ge(sem("wu_done"), 4 * i + 2 * a + 2)
                for h in range(GDN_HEADS):
                    mm = pe.matmul(ps[rows, 5, h * P:(h + 1) * P], w_t[a][:, h, rows], state[k % 2][:, h, :],
                                   start=True, stop=True)
                mm.then_inc(sem("ws_prod"), 1)

            def gdn_state_update(i, k):
                a, c, rows = k // 2, k % 2, slice(k % 2 * CHUNK, (k % 2 + 1) * CHUNK)
                pe.wait_ge(sem("v_new_done"), 4 * i + k + 1)
                for h in range(GDN_HEADS):
                    mm = pe.matmul(ps[:, 5, h * P:(h + 1) * P], k_d[a][rows, h, :], v_n[rows, h, :], start=True, stop=True)
                mm.then_inc(sem("ds_prod"), 1)
                if c == 0:
                    pe.wait_ge(sem("o_taken"), 2 * i + a + 1)
                for h in range(GDN_HEADS):
                    o = ps[rows, 6, h * P:(h + 1) * P]
                    pe.matmul(o, q_d[a][:, h, rows], state[c][:, h, :], start=True, stop=False)
                    mm = pe.matmul(o, p_t[a][rows, h, rows], v_n[rows, h, :], start=False, stop=True)
                if c:
                    mm.then_inc(sem("o_prod"), 1)

            def gdn_turns(i, a):
                for bank, n in ((3, 1), (7, 2), (5, 3)):
                    if a:
                        pe.wait_ge(sem("gdn_turn_read"), 6 * i + n)
                    if bank == 3:
                        turn_heads(bank, k_s[a], "gdn_turned")
                    elif bank == 7:
                        turn_heads(bank, v_s[a], "gdn_turned")
                    else:
                        cols = bass.ds((2 * i + a) * P, P)
                        heads(bank, lambda h: k_s[a][:, h, :], lambda h: qkv[:, h, cols], "gdn_turned")

            def gdn_pair(i, before):
                if before is not None:
                    pe.wait_ge(sem("wu_done"), 4 * i)
                    pe.wait_ge(sem("gdn_turn_read"), 6 * i)
                gdn_grams(i)
                for a in range(2):
                    pe.wait_ge(sem("tr0_done"), 2 * i + a + 1)
                    turn_heads(1 + a, t_r[0][a], "t0_turned")
                for n in range(1, len(LEVELS)):
                    old, last = (n - 1) % 2, n == len(LEVELS) - 1
                    if before is not None and not last:
                        gdn_state_products(before, n - 1)
                    for a in range(2):
                        pe.wait_ge(sem("level_done"), 10 * i + (2 * (n - 1) + a + 1))
                        if n == 1:
                            pe.wait_ge(sem("t0_done"), 2 * i + a + 1)
                        else:
                            pe.wait_ge(sem("t_done"), 8 * i + (2 * (n - 2) + a + 1))
                        heads(a, lambda h: m_s[n % 2][a][:, h, :], lambda h: t_f[old][a][:, h, :], "y_prod")
                    if before is not None and not last:
                        gdn_state_update(before, n - 1)
                    if last:
                        if before is not None:
                            pe.wait_ge(sem("state_done"), 4 * i + 1)
                        gdn_turns(i, 0)
                    for a in range(2):
                        pe.wait_ge(sem("y_done"), 10 * i + (2 * (n - 1) + a + 1))
                        heads(2 + 2 * a, lambda h: y_s[a][:, h, :], lambda h: t_r[old][a][:, h, :], "zt_prod")
                        if not last:
                            heads(3 + 4 * a, lambda h: t_r[old][a][:, h, :], lambda h: y_s[a][:, h, :], "z_prod")
                gdn_turns(i, 1)
                for a in range(2):
                    pe.wait_ge(sem("t_last_done"), 2 * i + a + 1)
                    pe.wait_ge(sem("gdn_turn_read"), 6 * i + 3 * a + 3)
                    heads(2 * a, lambda h: k_w[a][:, h, :], lambda h: t_r[1][a][:, h, :], "wu_prod")
                    heads(1 + 3 * a, lambda h: t_r[1][a][:, h, :], lambda h: v_b[a][:, h, :], "wu_prod")

            gdn_pair(0, None)
            with pe.Fori(0, GDN_PAIRS - 1) as i:
                gdn_pair(i + 1, i)
            for k in range(4):
                gdn_state_products(GDN_PAIRS - 1, k)
                gdn_state_update(GDN_PAIRS - 1, k)

            for h in range(2):
                turn("mixt", mix, h, lambda k: pe.wait_ge(sem("gdn_out_done"), NT))

            def out_projection(ring, run, pre, a_hi, a_lo, ready):
                for m in range(16):
                    half, c, j = m // 8, m // 4 % 2, m % 4
                    ring.ready(pe, 0, m)
                    hi, lo = ring.hi[m % ring.nslab], ring.lo[m % ring.nslab]
                    ready(half, c, j)
                    for t in range(4):
                        if half and j == 0:
                            pe.wait_ge(sem("mixed_done"), 16 * run + 4 * c + t + 1)
                        for k in (2 * j, 2 * j + 1):
                            o, w = ps[:, 4 * c + t, :], slice(k % 2 * HALF, (k % 2 + 1) * HALF)
                            a = slice((4 * half + t) * P, (4 * half + t + 1) * P)
                            pe.matmul(o, a_hi[:, k, a], hi[:, w], start=(k == 0), stop=False)
                            pe.matmul(o, a_lo[:, k, a], hi[:, w], start=False, stop=False)
                            mm = pe.matmul(o, a_hi[:, k, a], lo[:, w], start=False, stop=(k == KD - 1))
                        if t == 3:
                            mm.then_inc(ring.used, 1)
                        elif j == 3:
                            mm.then_inc(sem("mixed_prod"), 1)
                    if m in (13, 14):
                        pe.wait_ge(sem("mixed_done"), 16 * run + 12)
                        turn(pre, acc, 0, scaled(pre, 0), ks=range(4 * (m - 13), 4 * (m - 13) + 4))

            def mixt_ready(half, c, j):
                if half == 0 and j == 0:
                    turn_done("mixt", c)

            out_projection(R3, 0, "n2", mixt_hi, mixt_lo, mixt_ready)

            def ffn(ring, run, pre):
                def up(i, q, ready=None):
                    j, f = q % 2, q // 2
                    if f == 0:
                        ring.ready(pe, 4 * i, j)
                    panel(ring.hi[j], ring.lo[j], act_hi, act_lo, (j, 2 + j), KD, (sem("ffn_half"), ring.used), (f,), ready)

                def down(i, g, j):
                    t, f = g // 2, g % 2
                    o, a, c = ps[:, 4 + g % 4, :], slice(t * P, (t + 1) * P), slice(f * HALF, (f + 1) * HALF)
                    pe.matmul(o, hid_hi[:, j, a], ring.hi[2 + j][:, c], start=(j == 0), stop=False)
                    pe.matmul(o, hid_lo[:, j, a], ring.hi[2 + j][:, c], start=False, stop=False)
                    return pe.matmul(o, hid_hi[:, j, a], ring.lo[2 + j][:, c], start=False, stop=(j == 1))

                def step(i, first):
                    if run == 0:
                        pe.wait_ge(sem("ada_read"), i + 1)
                    if first:
                        turn_done(pre, 0)
                    up(i, 0)
                    up(i, 1)
                    if first:
                        pe.wait_ge(sem("mixed_done"), 16 * run + 16)
                        turn(pre, acc, 1, scaled(pre, 1))
                    up(i, 2, as_split(pre, 1) if first else None)

                    def modulation(j):
                        pe.wait_ge(sem("ada_sum"), ADA_STEP * i + (j + 1))
                        pe.matmul(ps[:, 0, j:j + 1], ada[j % 2][:, 0, :], ones[:, 0:1], start=True, stop=True)\
                            .then_inc(sem("ada_used"), 1)

                    if first:
                        up(i, 3)
                    if run == 0:
                        pe.wait_ge(sem("ffn_hid"), 4 * i + (1 + FFN_CREDIT))
                        modulation(0)
                        modulation(1)
                    if not first:
                        up(i, 3)
                    ring.ready(pe, 4 * i, 2)
                    ring.ready(pe, 4 * i, 3)
                    for g in range(16):
                        t = g // 2
                        if t % 4 == 0 and g % 2 == 0:
                            pe.wait_ge(sem("ffn_hid"), 4 * i + (4 * FFN_STEPS * run + 2 * (t // 4) + 2 + FFN_CREDIT))
                        if run == 0 and g == 8:
                            modulation(2)
                        pe.wait_ge(sem("ffn_acc"), 16 * i + ((16 * FFN_STEPS + 4) * run + g + 1))
                        mm = down(i, g, 0)
                        if g == 15:
                            mm.then_inc(ring.used, 1)
                        mm = down(i, g, 1)
                        mm.then_inc(ring.used if g == 15 else sem("ffn_down"), 1)

                step(0, True)
                with pe.Fori(0, FFN_STEPS - 1) as i:
                    step(i + 1, False)

            ffn(R4, 0, "n2")
            turn("n3", acc, 0, scaled("n3", 0))

            def conv_step(i, first):
                for j, free in enumerate(("c2_cg_read", "c2_v_done", "c2_y_done")):
                    R5.ready(pe, 3 * i, j)
                    pe.wait_ge(sem(free), i + 1)
                    panel(R5.hi[j], R5.lo[j], act_hi, act_lo, (2 * j, 2 * j + 1), KD, (None, R5.used),
                          (0,) if j < 2 and first else (0, 1), as_split("n3", 0) if j == 0 and first else None)
                    if j == 1 and first:
                        turn("n3", acc, 1, scaled("n3", 1))
                        for n in range(2):
                            panel(R5.hi[n], R5.lo[n], act_hi, act_lo, (2 * n, 2 * n + 1), KD, (None, R5.used), (1,),
                                  None if n else as_split("n3", 1))

            conv_step(0, True)
            with pe.Fori(0, CONV2_PANELS - 1) as i:
                conv_step(i + 1, False)

            def merge_gate(ring, run, i, j):
                b = MERGE_GATES[run][j]
                ring.ready(pe, 4 * i, j)
                pe.wait_ge(sem("m_gate_read"), 2 * i + (KD * run + j + 1))
                panel(ring.hi[j], ring.lo[j], act_hi, act_lo, (b, b + 1), KD, (None, ring.used))

            def merge_projection(ring, run, i, j, a_hi, a_lo):
                b = MERGE_PROJS[run][j]
                ring.ready(pe, 4 * i, 2 + j)
                pe.wait_ge(sem("m_done"), 2 * i + (KD * run + j + 1))
                panel(ring.hi[2 + j], ring.lo[2 + j], a_hi, a_lo, (b, b + 1), CONV2_PANELS, (None, ring.used))

            def merge(ring, run, a_hi, a_lo):
                for j in range(2):
                    merge_projection(ring, run, 0, j, a_hi, a_lo)
                with pe.Fori(0, KD // 2 - 1) as i:
                    for j in range(2):
                        merge_gate(ring, run, i + 1, j)
                    for j in range(2):
                        merge_projection(ring, run, i + 1, j, a_hi, a_lo)

            pe.wait_ge(sem("c2_cg_read"), CONV2_PANELS + 1)
            pe.wait_ge(sem("c2_v_done"), CONV2_PANELS + 1)
            for j in range(2):
                merge_gate(R6, 0, 0, j)
            pe.wait_ge(sem("c2_split"), CONV2_PANELS)
            merge(R6, 0, y_hi, y_lo)
            pe.wait_ge(sem("m_done"), KD + 2)
            token_chunk(R7, 0, HALF, act_hi, act_lo, lambda t: None, sem("v2_prod"))
            pe.wait_ge(sem("v2_done"), NT)

            def sb_project(i, n):
                j, h = n // 2, n % 2
                if h == 0:
                    R8.ready(pe, 2 * i, j)
                pe.wait_ge(sem("proj_read"), 4 * i + (4 * MLA_HEADS + n + 1))
                panel(R8.hi[j], R8.lo[j], act_hi, act_lo, (7, 7), KD, (sem("panel_half"), R8.used), (h,))

            def sb_scores(i, s):
                t, rows = s // 2, slice(s % 2 * SB_DIM, (s % 2 + 1) * SB_DIM)
                n = (t + 1) * P
                if s % NT == 0:
                    pe.wait_ge(sem("sb_qk_done"), 4 * i + 2 * (s // NT) + 2)
                pe.wait_ge(sem("sb_z_done"), SB_ITEMS * i + s + 1)
                for f in range((n + HALF - 1) // HALF):
                    w = min(HALF, n - f * HALF)
                    mm = pe.matmul(ps[:, 2 * (s % 2) + f, 0:w], q2[rows, t * P:(t + 1) * P],
                                   k2[rows, f * HALF:f * HALF + w], start=True, stop=True)
                mm.then_inc(sem("sb_scores"), 1)

            def sb_turn(i, s):
                pe.wait_ge(sem("sb_weights_done"), SB_ITEMS * i + s + 1)
                for n, g in enumerate(sb_groups(s)):
                    for b in range(4 * n, min(4 * n + 4, s // 2 + 1)):
                        mm = pe.transpose(ps[:, 4 + g % 2, (b % 4) * P:(b % 4 + 1) * P],
                                          sb_w[s % SB_SLOTS][:, b * P:(b + 1) * P], ident)
                    mm.then_inc(sem("sb_turned"), 1)

            def sb_outputs(i, s):
                t, half = s // 2, s // NT
                if s % NT == 0:
                    pe.wait_ge(sem("sb_o_done"), 2 * i + half + 2)
                for n, g in enumerate(sb_groups(s)):
                    pe.wait_ge(sem("sb_at_done"), SB_GROUPS * i + g + 1)
                    for b in range(4 * n, min(4 * n + 4, t + 1)):
                        mm = pe.matmul(ps[:, 6, s % NT * SB_DIM:(s % NT + 1) * SB_DIM],
                                       sb_at[g % 2][:, (b % 4) * P:(b % 4 + 1) * P], v2[:, b, 2 * i + s % 2, :],
                                       start=(b == 0), stop=(b == t))
                    mm.then_inc(sem("sb_pv"), 1)

            def sb_pair(i, before, last):
                for s in range(SB_ITEMS):
                    if s + 1 < SB_ITEMS:
                        sb_scores(i, s + 1)
                    if late := lagged(i, before, s, SB_LAG_PV, SB_ITEMS):
                        sb_outputs(*late)
                    if late := lagged(i, before, s, SB_LAG_TURN, SB_ITEMS):
                        sb_turn(*late)
                    if s in SB_PROJECT and not last:
                        sb_project(i + 1, SB_PROJECT.index(s))
                    if s + 1 == SB_ITEMS and not last:
                        sb_scores(i + 1, 0)

            for n in range(4):
                sb_project(0, n)
            sb_scores(0, 0)
            sb_pair(0, None, False)
            with pe.Fori(0, SB_PAIRS - 2) as i:
                sb_pair(i + 1, i, False)
            sb_pair(SB_PAIRS - 1, SB_PAIRS - 2, True)
            pe.wait_ge(sem("sb_z_done"), SB_ITEMS * SB_PAIRS + 2)
            merge_gate(R9, 1, 0, 0)
            for s in range(SB_ITEMS, SB_ITEMS + SB_LAG_PV):
                sb_outputs(SB_PAIRS - 1, s - SB_LAG_PV)
                if s < SB_ITEMS + SB_LAG_TURN:
                    sb_turn(SB_PAIRS - 1, s - SB_LAG_TURN)

            for h in range(2):
                turn("sb_o", o2, h, lambda k: pe.wait_ge(sem("sb_o_done"), SB_HEADS + 2), CONV2_PANELS)
            turn_done("sb_o", 1, CONV2_PANELS)
            merge_gate(R9, 1, 0, 1)
            merge(R9, 1, o2_hi, o2_lo)

            pe.wait_ge(sem("m_done"), 2 * KD + 2)
            for run in range(2):
                pe.wait_ge(sem("gate_diag_done"), run + 1)
                for f in range(2):
                    mm = pe.matmul(ps[:, 4 + 2 * run + f, :], ones, diag[:, 4 * f:4 * f + 4, :].rearrange("p k n -> p (k n)"),
                                   start=True, stop=True)
                mm.then_inc(sem("gate_row_prod"), 1)

            def merged_ready(half, c, j):
                if half == 0 and c == 0:
                    pe.wait_ge(sem("merged_split"), 2 * j + 2)
                if half == 0 and c == 1 and j == 0:
                    pe.wait_ge(sem("gate_rows_done"), 2)

            out_projection(R10, 1, "n4", act_hi, act_lo, merged_ready)
            ffn(R11, 1, "n4")

        @block.scalar
        def _(act):

            def norm_square(tag, t, src, place):
                n = NORM_AT[tag, t]
                if n >= 2:
                    act.wait_ge(sem("norm_sq_done"), n - 1)
                act.activation(place[n % 2][:], src[:, t, :], ACT.Square, accum_out=ssq[:, t:t + 1])\
                    .then_inc(sem("norm_sq_done"), 1)

            def norm_scale(tag, t):
                act.wait_ge(sem("norm_rstd_done"), NORM_AT[tag, t] + 1)
                act.activation(acc[:, t, :], resid[:, t, :], ACT.Copy, scale=rstd[:, t:t + 1])\
                    .then_inc(sem("norm_scaled"), 1)

            def pre_norm(tag, run, tiles):
                for t in tiles:
                    act.wait_ge(sem("resid_done"), NT * run + t + 1)
                    norm_square(tag, t, resid, junk)
                    if t > tiles[0]:
                        norm_scale(tag, t - 1)
                norm_scale(tag, tiles[-1])

            def norm_full(tag, h, hi, scale=None, bias=None, nk=KD):
                for k in range(nk):
                    n = h * nk + k
                    bank = ps[:, turn_bank(tag, h, k), :]
                    act.wait_ge(sem("turned"), TURNS[tag] + n + 1)
                    if bias:
                        if n >= 4:
                            act.wait_ge(sem("turn_split"), TURNS[tag] + n - 3)
                        ins = act.activation(norm_tmp[n % 4][:], bank, ACT.Identity, bias=bias(k), scale=scale(k))
                    elif scale:
                        ins = act.activation(hi[:, k, h * HALF:(h + 1) * HALF], bank, ACT.Copy, scale=scale(k))
                    else:
                        ins = act.copy(hi[:, k, h * HALF:(h + 1) * HALF], bank)
                    ins.then_inc(sem("turn_read"), 1)

            for h, tiles in enumerate((EARLY, LATE)):
                for t in tiles:
                    act.wait_ge(sem(f"x_in{t}"), 16)
                    norm_square("n1", t, x_tok, junk)
                if h == 0:
                    act.wait_ge(sem("vec_turned"), 1)
                    act.copy(vec[:], ps[:, 4, 0:N_VEC]).then_inc(sem("vec_cols_done"), 1)
                    act.copy(vec2[:], ps[:, 4, 256:256 + N_VEC2]).then_inc(sem("vec_cols_done"), 1)
                    act.wait_ge(sem("vec_cols_done"), 2)
                norm_full("n1", h, in_hi, mix_pre_gain)

            for t in range(NT):
                if t < NT - 1:
                    act.wait_ge(sem("gate_prod"), t + 1)
                else:
                    R1.panel_done(act, 0, 3)
                if t >= 2:
                    act.wait_ge(sem("gate_silu"), t - 1)
                act.activation(gate_tanh[t % 2][:], ps[:, t, :], ACT.Tanh, scale=0.5).then_inc(sem("gate_tanh_done"), 1)
            for t in range(NT):
                if t < NT - 1:
                    act.wait_ge(sem("tail_prod"), t + 1)
                else:
                    R1.panel_done(act, 0, 7)
                act.copy(lat[:, t, 0:TAIL_W], ps[:, t, 0:TAIL_W]).then_inc(sem("lat_done"), 1)

            for t in range(NT):
                act.wait_ge(sem("lat_done"), t + 1)
                if t >= 2:
                    act.wait_ge(sem("lat_sq_done"), 2 * t - 2)
                act.activation(lat_junk[t % 2][:, 0:Q_RANK], lat[:, t, LAT_CQ:LAT_CKV], ACT.Square,
                               accum_out=lat_ss[:, t:t + 1]).then_inc(sem("lat_sq_done"), 1)
                act.activation(lat_junk[t % 2][:, Q_RANK:], lat[:, t, LAT_CKV:LAT_KR], ACT.Square,
                               accum_out=lat_ss[:, NT + t:NT + t + 1]).then_inc(sem("lat_sq_done"), 1)
            act.wait_ge(sem("rope_arg_done"), 1)
            act.activation(trig[NOPE:P, :], trig[NOPE:P, :], ACT.Sin).then_inc(sem("rope_sin_done"), 1)
            act.wait_ge(sem("g_min_done"), 1)
            act.activation(g_exp[:], g_la[:], ACT.Exp).then_inc(sem("g_exp_done"), 1)
            act.activation(ea_b[:], a_log_b[:], ACT.Exp).then_inc(sem("g_exp_done"), 1)
            act.wait_ge(sem("g_exp1_done"), 1)
            act.activation(g_sp[:], g_u[:], ACT.Ln).then_inc(sem("g_exp_done"), 1)
            act.activation(g_beta[:], lat[:, :, GDN_HEADS:2 * GDN_HEADS], ACT.Tanh, scale=0.5)\
                .then_inc(sem("g_exp_done"), 1)

            with act.Fori(0, GDN_PANELS // 3) as i:
                for j in range(3):
                    p = 3 * i + j
                    b = 2 * j
                    act.wait_ge(sem("panel_half"), p + 1)
                    act.wait_ge(sem("conv_done"), p + 1)
                    act.copy(xpad[:, CONV_W - 1:CONV_W - 1 + HALF], ps[:, b, :])
                    R2.panel_done(act, 3 * i, j)
                    act.copy(xpad[:, CONV_W - 1 + HALF:], ps[:, b + 1, :]).then_inc(sem("conv_in_done"), 1)
                    act.wait_ge(sem("conv_done"), p + 2)
                    act.wait_ge(sem("ss_prod"), p + 1)
                    act.activation(conv_t[:], conv_y[:], ACT.Tanh, scale=0.5).then_inc(sem("conv_tanh_done"), 1)
                    act.wait_ge(sem("conv_silu_done"), p + 1)
                    act.activation(conv_t[:], qkv[:, p, :], ACT.Square)\
                        .then_inc(sem("conv_sq_done"), 1)
            for n in range(6):
                kind, h = n // 2, n % 2
                dst = (cq_f[:, 0, :], cq_f[:, 1, :], ckv_f[:])[kind][:, h * HALF:(h + 1) * HALF]
                gain = V_QN + kind if kind < 2 else V_KVN
                act.wait_ge(sem("lat_turned"), n + 1)
                act.activation(dst, ps[:, LAT_BANKS[n], :], ACT.Copy, scale=vec[:, gain:gain + 1]).then_inc(sem("lat_feat_done"), 1)
            for t in range(NT):
                act.wait_ge(sem("v_prod"), t + 1)
                act.copy(v_t[:, t, :, :].rearrange("p h e -> p (h e)"), ps[:, t, :]).then_inc(sem("v_done"), 1)
            act.wait_ge(sem("cumsum_prod"), 1)
            n_gh = NT * GDN_HEADS
            act.copy(g_cum[:].rearrange("p t h -> p (t h)"), ps[:, 0, 0:n_gh]).then_inc(sem("cumsum_done"), 1)
            act.copy(g_tot[:].rearrange("p t h -> p (t h)"), ps[:, 0, n_gh:2 * n_gh]).then_inc(sem("cumsum_done"), 1)
            act.wait_ge(sem("cumsum_done"), 2)
            act.activation(g_eg[:], g_cum[:], ACT.Exp).then_inc(sem("g_exps_done"), 1)
            act.wait_ge(sem("g_tail_done"), 1)
            act.activation(g_ekd[:], g_ekd[:], ACT.Exp).then_inc(sem("g_exps_done"), 1)

            scale = float(DQK) ** -0.5
            def mla_take(i, h, n):
                a = h % 2
                act.wait_ge(sem("mla_proj"), 8 * i + (4 * h + n + 6))
                act.copy((q_f if n < 2 else k_f)[a][0:NOPE, n % 2 * HALF:(n % 2 + 1) * HALF], ps[0:NOPE, 7, :])\
                    .then_inc(sem("proj_read"), 1)

            def mla_exp(i, s, before):
                t, a = mla_tile(s), s // NT
                n = (t + 1) * P
                act.wait_ge(sem("mla_max_done"), MLA_ITEMS * i + s + 1)
                if slot := lagged(i, before, s, PROBS, MLA_ITEMS):
                    act.wait_ge(sem("mla_turned"), MLA_GROUPS * slot[0] + (mla_groups(slot[1])[-1] + 1))
                act.activation(probs[s % PROBS][:, 0:n], ps[:, 2 * (s % 2):2 * (s % 2) + 2, :].rearrange("p b n -> p (b n)")[:, 0:n],
                               ACT.Exp, bias=sm_neg[a][:, t:t + 1], scale=scale, accum_out=sm_sum[a][:, t:t + 1])\
                    .then_inc(sem("mla_exp_done"), 1)

            def mla_probs_out(i, s):
                for n, g in enumerate(mla_groups(s)):
                    w = min(4, mla_tile(s) + 1 - 4 * n) * P
                    act.wait_ge(sem("mla_turned"), MLA_GROUPS * i + (g + 1))
                    act.wait_ge(sem("mla_pv"), MLA_GROUPS * i + (g + 1))
                    act.copy(probs_t[g % 2][:, 0:w], ps[:, 4 + g % 2, 0:w]).then_inc(sem("mla_pt_done"), 1)

            def mla_pair(i, before, last):
                for s in range(MLA_ITEMS):
                    mla_exp(i, s, before)
                    if 2 <= s <= 5:
                        mla_take(i, 1, s - 2)
                    elif 9 <= s <= 12 and not last:
                        mla_take(i, 2, s - 9)
                    if late := lagged(i, before, s, MLA_LAG_TURN, MLA_ITEMS):
                        mla_probs_out(*late)

            for n in range(4):
                mla_take(0, 0, n)
            mla_pair(0, None, False)
            with act.Fori(0, MLA_PAIRS - 2) as i:
                mla_pair(i + 1, i, False)
            mla_pair(MLA_PAIRS - 1, MLA_PAIRS - 2, True)
            for s in range(MLA_ITEMS - MLA_LAG_TURN, MLA_ITEMS):
                mla_probs_out(MLA_PAIRS - 1, s)

            def gdn_flat(tile):
                return tile[:].rearrange("p h t -> p (h t)")

            def gdn_squares(i, a):
                act.wait_ge(sem("o_taken"), 2 * i + a + 2)
                act.wait_ge(sem("o_ss_done"), 2 * i + a + 1)
                for h in range(GDN_HEADS):
                    ins = act.activation(o_sq[:, h, :], o_s[:, h, :], ACT.Square, accum_out=o_ss[:, h:h + 1])
                ins.then_inc(sem("o_ss_done"), 1)

            def gdn_pair(i, before):
                for a in range(2):
                    act.wait_ge(sem("g_row_prod"), 2 * i + a + 1)
                    act.activation(gdn_flat(e_g[a]), ps[:, 3 * a, :], ACT.Exp).then_inc(sem("e_g_done"), 1)
                for a in range(2):
                    act.wait_ge(sem("decay_arg_done"), 2 * i + a + 1)
                    act.activation(e_d[a][:], e_d[a][:], ACT.Exp).then_inc(sem("decay_done"), 1)
                for a in range(2):
                    act.wait_ge(sem("t0_turned"), 2 * i + a + 1)
                    act.copy(gdn_flat(t_f[0][a]), ps[:, 1 + a, :]).then_inc(sem("t0_done"), 1)
                for n in range(1, len(LEVELS)):
                    for a in range(2):
                        act.wait_ge(sem("y_prod"), 10 * i + (2 * (n - 1) + a + 1))
                        act.copy(gdn_flat(y_s[a]), ps[:, a, :]).then_inc(sem("y_done"), 1)
                    if before is not None and n == 3:
                        gdn_squares(before, 0)
                if before is not None:
                    gdn_squares(before, 1)
                    act.wait_ge(sem("state_done"), 4 * i + 1)
                for a in range(2):
                    act.copy(e_last[a][:], e_g[a][:, :, CHUNK - 1::CHUNK]).then_inc(sem("e_last_done"), 1)
                for a in range(2):
                    for n, dst in enumerate((w_t, u_s)):
                        act.wait_ge(sem("wu_prod"), 4 * i + 2 * a + n + 1)
                        act.copy(gdn_flat(dst[a]), ps[:, (0, 1, 2, 4)[2 * a + n], :]).then_inc(sem("wu_done"), 1)

            gdn_pair(0, None)
            with act.Fori(0, GDN_PAIRS - 1) as i:
                gdn_pair(i + 1, i)
            for a in range(2):
                gdn_squares(GDN_PAIRS - 1, a)

            for h in range(2):
                norm_full("mixt", h, mixt_hi)

            def out_projection(ring, run, post, pre, scale, bias=None):
                def take(half, c, t):
                    if t < 3:
                        act.wait_ge(sem("mixed_prod"), 12 * run + 3 * (2 * half + c) + t + 1)
                    else:
                        ring.panel_done(act, 0, 8 * half + 4 * c + 3)
                    act.copy(acc[:, 4 * half + t, c * HALF:(c + 1) * HALF], ps[:, 4 * c + t, :]).then_inc(sem("mixed_done"), 1)

                for c in range(2):
                    for t in range(4):
                        take(0, c, t)
                act.wait_ge(sem("mixed_done"), 16 * run + 8)
                for t in EARLY:
                    norm_square(post, t, acc, junk)
                pre_norm(pre, 2 * run, EARLY)
                for t in range(4):
                    take(1, 0, t)
                norm_full(pre, 0, act_hi, scale, bias)
                for t in range(4):
                    take(1, 1, t)
                    act.wait_ge(sem("mixed_done"), 16 * run + 12 + t + 1)
                    norm_square(post, 4 + t, acc, junk)
                pre_norm(pre, 2 * run, LATE)
                norm_full(pre, 1, act_hi, scale, bias)

            out_projection(R3, 0, "mix_post", "n2", lambda k: vec[:, V_FFNPRE + k:V_FFNPRE + k + 1])

            def ffn_relu(ring, run):
                def ada_load(i, j):
                    slab = w_ada[:, :, bass.ds((ADA_STEP * i + j) * P, P)]
                    act.wait_ge(sem("ada_used"), ADA_STEP * i + (2, 1, 3)[j])
                    act.dma_start(ada[j % 2][:], slab).then_inc(sem(f"ada_in{j % 2}"), 16)

                def step(i):
                    if run == 0:
                        ada_load(i, 0)
                        ada_load(i, 1)
                    for q in range(4):
                        j, f = q % 2, q // 2
                        if f == 0:
                            act.wait_ge(sem("ffn_half"), 2 * i + (2 * FFN_STEPS * run + j + 1))
                        else:
                            ring.panel_done(act, 4 * i, j)
                        act.wait_ge(sem("ffn_hid"), 4 * i + (4 * FFN_STEPS * run + q - 1 + FFN_CREDIT))
                        act.activation(relu_t[q % 2][:], ps[:, q, :], ACT.Relu).then_inc(sem("ffn_relu"), 1)
                        act.wait_ge(sem("ffn_relu"), 4 * i + (4 * FFN_STEPS * run + q + 1))
                        act.activation(hid_hi[:, j, f * HALF:(f + 1) * HALF], relu_t[q % 2][:], ACT.Square)\
                            .then_inc(sem("ffn_hid_hi"), 1)
                        if run == 0 and q == 2:
                            ada_load(i, 2)

                def take_modulation(i):
                    act.wait_ge(sem("ada_used"), ADA_STEP * i + ADA_STEP + 2)
                    act.copy(mod[:, bass.ds(ADA_STEP * i, ADA_STEP)], ps[:, 0, 0:ADA_STEP]).then_inc(sem("ada_read"), 1)

                with act.Fori(0, FFN_STEPS - 1) as i:
                    step(i)
                    if run == 0:
                        take_modulation(i)
                step(FFN_STEPS - 1)
                return take_modulation

            def ffn_square(run, tag, t):
                act.wait_ge(sem("ffn_acc"), (run + 1) * (16 * FFN_STEPS + 4) - 16 + 2 * t + 2)
                norm_square(tag, t, acc, junk_ffn)

            take_modulation = ffn_relu(R4, 0)
            act.wait_ge(sem("ada_used"), N_MOD * KD + 1)
            act.dma_start(ffn_post_row[:], d["ffn_post_norm"][0].partition_broadcast(P)).then_inc(sem("post_gain_in"), 16)

            def spill(t):
                act.dma_start(x1_spill[t], resid[:, t, :]).then_inc(sem("x1_stored"), 16)

            def shift_norm(h):
                norm_full("n3", h, act_hi, lambda k: scale2[:, k:k + 1], lambda k: mod[:, k:k + 1])

            for tag, t in FFN_NORMS:
                if tag == "ffn_post":
                    if t == 3:
                        take_modulation(FFN_STEPS - 1)
                    ffn_square(0, tag, t)
                    continue
                if t == 4:
                    norm_scale("n3", 3)
                    act.wait_ge(sem("mod_scales_done"), 1)
                    shift_norm(0)
                act.wait_ge(sem("resid_done"), NT + t + 1)
                spill(t)
                norm_square(tag, t, resid, junk_ffn if t < 4 else junk)
                if t % 4:
                    norm_scale(tag, t - 1)
            norm_scale("n3", NT - 1)
            shift_norm(1)
            with act.Fori(0, CONV2_PANELS) as i:
                R5.panel_done(act, 3 * i, 0)
                act.wait_ge(sem("c2_v_done"), i + 1)
                act.copy(cg_t[:], ps[:, 0:2, :].rearrange("p b n -> p (b n)")).then_inc(sem("c2_cg_read"), 1)
                act.wait_ge(sem("c2_y_done"), i + 2)
                act.copy(y_hi[:, i, :], conv2_y[:]).then_inc(sem("c2_hi_done"), 1)

            def merge_gates(ring, run, gates):
                with act.Fori(0, KD // 2) as i:
                    for j in range(2):
                        ring.panel_done(act, 4 * i, j)
                        act.wait_ge(sem("m_done"), 2 * i + (KD * run + j + 1))
                        act.activation(gates[j][:], ps[:, MERGE_GATES[run][j]:MERGE_GATES[run][j] + 2, :].rearrange("p b n -> p (b n)"), ACT.Tanh,
                                       scale=0.5).then_inc(sem("m_gate_read"), 1)

            merge_gates(R6, 0, conv_gate)
            for t in range(NT):
                if t < NT - 1:
                    act.wait_ge(sem("v2_prod"), t + 1)
                else:
                    R7.panel_done(act, 0, 3)
                act.copy(v2[:, t, :, :].rearrange("p h e -> p (h e)"), ps[:, t, :]).then_inc(sem("v2_done"), 1)

            act.preload_act_table_set("natural_log_exp_and_others")

            def sb_take_projection(i, n):
                j, h = n // 2, n % 2
                if n == 0 and not isinstance(i, int):
                    act.wait_ge(sem("sb_qk_done"), 4 * i)
                if h == 0:
                    act.wait_ge(sem("panel_half"), 2 * i + (GDN_PANELS + j + 1))
                else:
                    R8.panel_done(act, 2 * i, j)
                act.copy((q2_next, k2_next)[j][:, h * HALF:(h + 1) * HALF], ps[:, 7, :]).then_inc(sem("proj_read"), 1)

            ach = Chain(act, sem("act_chain"))

            def sb_softplus(i, s, before):
                n = (s // 2 + 1) * P
                l = sb_w[s % SB_SLOTS][:, 0:n]
                act.wait_ge(sem("sb_z_done"), SB_ITEMS * i + s + 3)
                if slot := lagged(i, before, s, SB_SLOTS, SB_ITEMS):
                    act.wait_ge(sem("sb_turned"), SB_GROUPS * slot[0] + (sb_groups(slot[1])[-1] + 1))
                ach.link(act.activation(l, sb_z[s % 2][:, 0:n], ACT.Abs))
                ach.link(act.activation(l, l, ACT.Exp, scale=-1.0))
                act.activation(l, l, ACT.Ln, bias=1.0).then_inc(sem("sb_ln_done"), 1)

            def sb_weights_out(i, s):
                for n, g in enumerate(sb_groups(s)):
                    w = min(4, s // 2 + 1 - 4 * n) * P
                    act.wait_ge(sem("sb_turned"), SB_GROUPS * i + g + 1)
                    act.wait_ge(sem("sb_pv"), SB_GROUPS * i + g + 1)
                    act.copy(sb_at[g % 2][:, 0:w], ps[:, 4 + g % 2, 0:w]).then_inc(sem("sb_at_done"), 1)

            def sb_exp(i, s):
                a = sb_w[s % SB_SLOTS][:, 0:(s // 2 + 1) * P]
                act.wait_ge(sem("sb_arg_done"), SB_ITEMS * i + s + 1)
                act.activation(a, a, ACT.Exp).then_inc(sem("sb_weights_done"), 1)

            def sb_pair(i, before, last):
                for s in range(SB_ITEMS):
                    if late := lagged(i, before, s, SB_LAG_EXP, SB_ITEMS):
                        sb_exp(*late)
                    sb_softplus(i, s, before)
                    if late := lagged(i, before, s, SB_LAG_TURN, SB_ITEMS):
                        sb_weights_out(*late)
                    if s - 1 in SB_PROJECT and not last:
                        sb_take_projection(i + 1, SB_PROJECT.index(s - 1))

            for n in range(4):
                sb_take_projection(0, n)
            sb_pair(0, None, False)
            with act.Fori(0, SB_PAIRS - 2) as i:
                ach.loop(i, 2 * SB_ITEMS)
                sb_pair(i + 1, i, False)
            ach.end(SB_PAIRS - 2)
            sb_pair(SB_PAIRS - 1, SB_PAIRS - 2, True)
            for s in range(SB_ITEMS, SB_ITEMS + SB_LAG_TURN):
                if s < SB_ITEMS + SB_LAG_EXP:
                    sb_exp(SB_PAIRS - 1, s - SB_LAG_EXP)
                sb_weights_out(SB_PAIRS - 1, s - SB_LAG_TURN)

            for h in range(2):
                norm_full("sb_o", h, o2_hi, nk=CONV2_PANELS)
            merge_gates(R9, 1, attn_gate)
            act.wait_ge(R9.split_done, R9.SLOTS + R9.base + R9.total)
            for run, gain in enumerate(("g_post_mix_2", "g_post_mlp_2")):
                act.dma_start(gate_rows[run][:], d[gain][0].partition_broadcast(P)).then_inc(sem("post_gain_in"), 16)
            R9.panel_done(act, 0, 2 * KD - 3)
            for k in range(KD):
                act.wait_ge(sem("m_done"), KD + 2 + k + 1)
                act.activation(act_hi[:, k, :], merged[:, k, :], ACT.Copy, scale=0.5).then_inc(sem("merged_hi_done"), 1)
            act.wait_ge(sem("merged_split"), KD)
            act.wait_ge(sem("x1_stored"), 16 * NT)
            for t in range(NT):
                act.dma_start(resid[:, t, :], x1_spill[t]).then_inc(sem(f"x_in{t}"), 16)
            out_projection(R10, 1, "mix_post2", "n4", lambda k: scale2[:, KD + k:KD + k + 1],
                           lambda k: mod[:, 3 * KD + k:3 * KD + k + 1])
            act.wait_ge(sem("turn_split"), TURNS["n4"] + 2 * KD)
            ffn_relu(R11, 1)
            for t in range(NT):
                ffn_square(1, "ffn_post2", t)

        @block.vector
        def _(dve):
            ch = Chain(dve, sem("dve_chain"))

            def norm_split(tag, h, hi, lo, gain=None, nk=KD):
                cols = slice(h * HALF, (h + 1) * HALF)
                for k in range(nk):
                    n = h * nk + k
                    bank, upper = ps[:, turn_bank(tag, h, k), :], hi[:, k, cols].bitcast(F32)
                    if tag in SHIFTED:
                        dve.wait_ge(sem("turn_hi_done"), 2 * KD * SHIFTED.index(tag) + n + 1)
                        ins = dve.tensor_tensor(lo[:, k, cols], norm_tmp[n % 4][:], upper, ALU.subtract)
                    else:
                        dve.wait_ge(sem("turn_read"), TURNS[tag] + n + 1)
                        if gain:
                            ins = dve.scalar_tensor_tensor(lo[:, k, cols], bank, gain(k), upper, ALU.mult, ALU.subtract)
                        else:
                            ins = dve.tensor_tensor(lo[:, k, cols], bank, upper, ALU.subtract)
                    ins.then_inc(sem("turn_split"), 1)

            for h, tiles in enumerate((EARLY, LATE)):
                for t in tiles:
                    dve.wait_ge(sem("norm_rstd_done"), NORM_AT["n1", t] + 1)
                    dve.tensor_scalar(x_tok[:, t, :], x_tok[:, t, :], rstd[:, t:t + 1], None, ALU.mult)\
                        .then_inc(sem("norm_scaled"), 1)
                if h == 0:
                    dve.wait_ge(sem("vec_cols_done"), 2)
                norm_split("n1", h, in_hi, in_lo, mix_pre_gain)

            dve.wait_ge(sem("gdn_vec_in"), 48)
            ch.link(dve.tensor_scalar(out_norm_row[:], out_norm_row[:], 0.5, None, ALU.mult))
            for t in range(NT):
                dve.wait_ge(sem("gate_tanh_done"), t + 1)
                dve.scalar_tensor_tensor(gate[:, t, :], gate_tanh[t % 2][:], 1.0, ps[:, t, :], ALU.add, ALU.mult)\
                    .then_inc(sem("gate_silu"), 1)
                dve.wait_ge(sem("gate_silu"), t + 1)
                gh = gate[:, t, :].rearrange("p (h e) -> p h e", h=GDN_HEADS)
                ch.link(dve.tensor_tensor(gh, gh, out_norm_row[:].unsqueeze(1).broadcast_to([P, GDN_HEADS, P]), ALU.mult))

            rot = slice(NOPE, P)
            dve.wait_ge(sem("pos_in"), 16)
            ch.link(dve.tensor_copy(ang[rot, :], pos_i[rot, :]))
            ch.link(dve.tensor_scalar(ang[rot, :], ang[rot, :], consts[rot, C_FREQ:C_FREQ + 1], None, ALU.mult))
            ch.link(dve.tensor_scalar(turns[rot, :], ang[rot, :], 1.0 / TWO_PI, consts[rot, C_QUARTER:C_QUARTER + 1],
                                      ALU.mult, ALU.add))
            ch.link(dve.tensor_scalar(turns[rot, :], turns[rot, :], ROUND, ROUND, ALU.add, ALU.subtract))
            src = ang
            for part in TWO_PI_PARTS:
                ch.link(dve.scalar_tensor_tensor(trig[rot, :], turns[rot, :], -part, src[rot, :], ALU.mult, ALU.add))
                src = trig
            ch.link(dve.tensor_scalar(trig[rot, :], trig[rot, :], consts[rot, C_QUARTER_ANGLE:C_QUARTER_ANGLE + 1],
                                      PI_BELOW, ALU.add, ALU.min))
            dve.tensor_scalar(trig[rot, :], trig[rot, :], -PI_BELOW, None, ALU.max).then_inc(sem("rope_arg_done"), 1)
            dve.memset(conv_t[:], 0.0).then_inc(sem("conv_sq_done"), 1)

            dve.wait_ge(sem("lat_done"), NT)
            dtb = dt_b[:].unsqueeze(1).broadcast_to([P, NT, GDN_HEADS])
            ch.link(dve.tensor_tensor(g_arg[:], lat[:, :, 0:GDN_HEADS], dtb, ALU.add))
            dve.tensor_scalar(g_la[:], g_arg[:], 40.0, None, ALU.min).then_inc(sem("g_min_done"), 1)
            dve.wait_ge(sem("g_exp_done"), 1)
            dve.tensor_scalar(g_u[:], g_exp[:], 1.0, None, ALU.add).then_inc(sem("g_exp1_done"), 1)
            dve.wait_ge(sem("g_exp1_done"), 1)
            ch.link(dve.scalar_tensor_tensor(g_exp[:], g_u[:], -1.0, g_exp[:], ALU.add, ALU.subtract))
            dve.wait_ge(sem("g_exp_done"), 3)
            ch.link(dve.reciprocal(g_u[:], g_u[:]))
            ch.link(dve.tensor_tensor(g_exp[:], g_exp[:], g_u[:], ALU.mult))
            ch.link(dve.tensor_tensor(g_sp[:], g_sp[:], g_exp[:], ALU.subtract))
            ch.link(dve.tensor_tensor(g_sp[:], g_sp[:], g_arg[:], ALU.max))
            eab = ea_b[:].unsqueeze(1).broadcast_to([P, NT, GDN_HEADS])
            dve.scalar_tensor_tensor(g_la[:], g_sp[:], -1.0, eab, ALU.mult, ALU.mult).then_inc(sem("log_a_done"), 1)
            dve.wait_ge(sem("g_exp_done"), 4)
            ch.link(dve.tensor_scalar(g_beta[:], g_beta[:], 0.5, 0.5, ALU.mult, ALU.add))

            dve.wait_ge(sem("lat_rstd_done"), 1)

            def by_tile(col, n):
                return lat_rstd[:, col:col + NT].unsqueeze(2).broadcast_to([P, NT, n])

            half = ROPE // 2
            dve.tensor_tensor(lat[:, :, LAT_CQ:LAT_CKV], lat[:, :, LAT_CQ:LAT_CKV], by_tile(0, Q_RANK), ALU.mult)
            dve.tensor_tensor(lat[:, :, LAT_CKV:LAT_KR], lat[:, :, LAT_CKV:LAT_KR], by_tile(NT, KV_RANK), ALU.mult)
            dve.tensor_copy(lat[:, :, TAIL_W:TAIL_W + half], lat[:, :, LAT_KR + half:LAT_KR + ROPE])
            dve.tensor_copy(lat[:, :, TAIL_W + half:TAIL_W + ROPE], lat[:, :, LAT_KR:LAT_KR + half])\
                .then_inc(sem("lat_norm_done"), 1)
            dve.wait_ge(sem("rope_sin_done"), 1)
            ch.link(dve.tensor_scalar(trig[rot, :], trig[rot, :], consts[rot, C_SIGN:C_SIGN + 1], None, ALU.mult))
            dve.wait_ge(sem("lat_sq_done"), 2 * NT)
            ch.link(dve.memset(xpad[:, 0:CONV_W - 1], 0.0))

            with dve.Fori(0, GDN_PANELS // 3) as i:
                ch.loop(i, 9)
                for j in range(3):
                    p = 3 * i + j
                    dve.wait_ge(sem("conv_in_done"), p + 3)

                    def tap(w):
                        return vec[:, bass.ds(V_CONV + w * GDN_PANELS + p, 1)]

                    ch.link(dve.tensor_scalar(conv_y[:], xpad[:, 0:SEQ], tap(0), None, ALU.mult))
                    for w in range(1, CONV_W):
                        ins = dve.scalar_tensor_tensor(conv_y[:], xpad[:, w:w + SEQ], tap(w), conv_y[:],
                                                       ALU.mult, ALU.add)
                        if w < CONV_W - 1:
                            ch.link(ins)
                        else:
                            ins.then_inc(sem("conv_done"), 1)
                    dve.wait_ge(sem("conv_tanh_done"), p + 1)
                    dve.scalar_tensor_tensor(qkv[:, p, :], conv_t[:], 1.0, conv_y[:], ALU.add, ALU.mult)\
                        .then_inc(sem("conv_silu_done"), 1)
                    dve.wait_ge(sem("ss_prod"), p + 1)
                    dve.tensor_copy(ss_gdn[:, :, p], ps[:, 6, 0:NT]).then_inc(sem("ss_gdn_done"), 1)
                ch.end(GDN_PANELS // 3)
            rr, swap = slice(NOPE, DQK), slice(DQK, P)
            dve.wait_ge(sem("conv_sq_done"), GDN_PANELS + 1)
            for h in range(2):
                cols = slice(h * HALF, (h + 1) * HALF)
                dve.wait_ge(sem("lat_turned"), 7 + h)
                b = LAT_BANKS[6 + h]
                dve.tensor_tensor(rope_t[rr, cols], ps[swap, b, :], trig[swap, cols], ALU.mult)
                ch.link(dve.tensor_tensor(k_f[0][rr, cols], ps[rr, b, :], trig[rr, cols], ALU.mult))
            dve.tensor_tensor(k_f[0][rr, :], k_f[0][rr, :], rope_t[rr, :], ALU.add).then_inc(sem("mla_k_rope_done"), 1)
            dve.wait_ge(sem("mla_k_rope_done"), 1)
            dve.tensor_copy(k_f[1][rr, :], k_f[0][rr, :]).then_inc(sem("mla_k_rope_done"), 1)
            dve.wait_ge(sem("cumsum_done"), 2)
            dve.tensor_tensor(g_ekd[:], g_tot[:], g_cum[:], ALU.subtract).then_inc(sem("g_tail_done"), 1)

            scale = float(DQK) ** -0.5

            def mla_rotate(i, h, n):
                a, cols = h % 2, slice(n * HALF, (n + 1) * HALF)
                dve.wait_ge(sem("mla_proj"), 8 * i + (4 * h + n + 6))
                dve.tensor_tensor(rope_t[rr, cols], ps[swap, 7, :], trig[swap, cols], ALU.mult)
                ch.link(dve.tensor_tensor(q_f[a][rr, cols], ps[rr, 7, :], trig[rr, cols], ALU.mult))
                dve.tensor_tensor(q_f[a][rr, cols], q_f[a][rr, cols], rope_t[rr, cols], ALU.add)\
                    .then_inc(sem("mla_rope_done"), 1)
                dve.wait_ge(sem("mla_rope_done"), 4 * i + (2 * h + n + 1))

            def mla_max(i, s):
                t, a = mla_tile(s), s // NT
                n = (t + 1) * P
                z = ps[:, 2 * (s % 2):2 * (s % 2) + 2, :].rearrange("p b n -> p (b n)")
                dve.wait_ge(sem("mla_scores"), MLA_ITEMS * i + s + 1)
                ch.link(dve.memset(z[0:CHUNK, n - CHUNK:n], -1e30))
                ch.link(dve.tensor_reduce(sm_max[a][:, t:t + 1], z[:, 0:n], AX_X, ALU.max))
                dve.tensor_scalar(sm_neg[a][:, t:t + 1], sm_max[a][:, t:t + 1], -scale, None, ALU.mult)\
                    .then_inc(sem("mla_max_done"), 1)

            def mla_out(i, a):
                dve.wait_ge(sem("mla_pv"), MLA_GROUPS * i + (mla_groups(a * NT + NT - 1)[-1] + 3))
                ch.link(dve.reciprocal(sm_rec[a][:], sm_sum[a][:]))
                dve.tensor_tensor(mix[:, :, bass.ds(2 * V_DIM * i + (GDN_W + a * V_DIM), V_DIM)],
                                  ps[:, 6, :].rearrange("p (t e) -> p t e", e=V_DIM),
                                  sm_rec[a][:].unsqueeze(2).broadcast_to([P, NT, V_DIM]), ALU.mult)\
                    .then_inc(sem("mla_o_done"), 1)

            def mla_pair(i, before, last):
                for s in range(MLA_ITEMS):
                    mla_max(i, s)
                    if before is not None and s == MLA_LAG_PV:
                        mla_out(before, 1)
                    if s == NT + MLA_LAG_PV:
                        mla_out(i, 0)
                    if 2 <= s <= 3:
                        mla_rotate(i, 1, s - 2)
                    elif 9 <= s <= 10 and not last:
                        mla_rotate(i, 2, s - 9)

            for n in range(2):
                mla_rotate(0, 0, n)
            dve.wait_ge(sem("qk_norm_done"), 2)
            ch.link(dve.tensor_tensor(g_bk[:], g_beta[:], g_rk[:], ALU.mult))
            dve.wait_ge(sem("g_exps_done"), 2)
            dve.tensor_scalar(g_cv[:], g_beta[:], 0.5, None, ALU.mult)
            dve.tensor_tensor(g_cd[:], g_rk[:], g_ekd[:], ALU.mult)
            dve.tensor_tensor(g_cw[:], g_bk[:], g_eg[:], ALU.mult).then_inc(sem("g_scales_done"), 1)

            mla_pair(0, None, False)
            with dve.Fori(0, MLA_PAIRS - 2) as i:
                ch.loop(i, 2 * MLA_ITEMS + 2 + 4)
                mla_pair(i + 1, i, False)
            ch.end(MLA_PAIRS - 2)
            mla_pair(MLA_PAIRS - 1, MLA_PAIRS - 2, True)
            mla_out(MLA_PAIRS - 1, 1)

            def by_head(cols):
                return cols.unsqueeze(2).broadcast_to([P, GDN_HEADS, P])

            def each_head(mask):
                return consts[:, mask:mask + P].unsqueeze(1).broadcast_to([P, GDN_HEADS, P])

            def bank(n):
                return ps[:, n, :].rearrange("p (h t) -> p h t", h=GDN_HEADS)

            def gdn_decay(i):
                for a in range(2):
                    cols = bass.ds((2 * i + a) * P, P)
                    dve.tensor_copy(k_s[a][:], qkv[:, GDN_HEADS:2 * GDN_HEADS, cols]).then_inc(sem("gdn_k_in"), 1)
                for a in range(2):
                    dve.wait_ge(sem("e_g_done"), 2 * i + a + 1)
                    ch.link(dve.tensor_tensor(e_d[a][:], bank(3 * a), by_head(g_cum[:, 2 * i + a, :]), ALU.subtract))
                    dve.tensor_scalar(e_d[a][:], e_d[a][:], 0.0, None, ALU.min).then_inc(sem("decay_arg_done"), 1)
                for a, (b_b, b_k) in enumerate(((1, 2), (4, 0))):
                    dve.wait_ge(sem("decay_done"), 2 * i + a + 1)
                    rk = g_rk[:, 2 * i + a, :]
                    ch.link(dve.tensor_tensor(e_d[a][:], e_d[a][:], by_head(rk), ALU.mult))
                    dve.wait_ge(sem("kk_prod"), 2 * i + a + 2)
                    ch.link(dve.tensor_tensor(a_t[a][:], bank(b_b), e_d[a][:], ALU.mult))
                    dve.tensor_tensor(a_t[a][:], bank(b_k), a_t[a][:], ALU.mult).then_inc(sem("a_t_done"), 1)
                    dve.wait_ge(sem("a_t_done"), 2 * i + a + 1)
                    ch.link(dve.tensor_tensor(t_r[0][a][:], a_t[a][:], each_head(C_LEVEL), ALU.mult))
                    dve.tensor_tensor(t_r[0][a][:], each_head(C_ID), t_r[0][a][:], ALU.subtract).then_inc(sem("tr0_done"), 1)
                for a in range(2):
                    dve.tensor_copy(v_s[a][:], qkv[:, 2 * GDN_HEADS:3 * GDN_HEADS, bass.ds((2 * i + a) * P, P)])

            def gdn_new_values(i, k):
                a, rows = k // 2, slice(k % 2 * CHUNK, (k % 2 + 1) * CHUNK)
                dve.wait_ge(sem("ws_prod"), 4 * i + k + 1)
                dve.tensor_tensor(v_n[rows, :, :], u_s[a][rows, :, :], bank(5)[rows], ALU.subtract)\
                    .then_inc(sem("v_new_done"), 1)

            def gdn_new_state(i, k):
                dve.wait_ge(sem("ds_prod"), 4 * i + k + 1)
                dve.wait_ge(sem("s_dec_done"), 4 * i + k + 1)
                dve.tensor_tensor(state[1 - k % 2][:], s_dec[:], bank(5), ALU.add).then_inc(sem("state_done"), 1)

            def gdn_take_out(i, a):
                dve.wait_ge(sem("o_prod"), 2 * i + a + 1)
                dve.tensor_tensor(o_s[:], bank(6), by_head(g_rq[:, 2 * i + a, :]), ALU.mult).then_inc(sem("o_taken"), 1)

            def gdn_out(i, a):
                t = 2 * i + a
                dve.wait_ge(sem("o_rstd_done"), t + 1)
                ch.link(dve.tensor_tensor(o_s[:], o_s[:], by_head(o_rstd[:]), ALU.mult))
                dve.tensor_tensor(mix[:, t, 0:GDN_W].rearrange("p (h e) -> p h e", h=GDN_HEADS), o_s[:],
                                  gate[:, t, :].rearrange("p (h e) -> p h e", h=GDN_HEADS), ALU.mult)\
                    .then_inc(sem("gdn_out_done"), 1)
                dve.wait_ge(sem("gdn_out_done"), t + 1)

            def gdn_scaled(i, a):
                t = 2 * i + a
                dve.wait_ge(sem("gdn_turned"), 6 * i + 3 * a + 3)
                dve.tensor_tensor(q_d[a][:], qkv[:, 0:GDN_HEADS, bass.ds(t * P, P)], e_g[a][:], ALU.mult)
                dve.tensor_tensor(k_w[a][:], bank(3), by_head(g_cw[:, t, :]), ALU.mult)
                dve.tensor_tensor(k_d[a][:], bank(3), by_head(g_cd[:, t, :]), ALU.mult).then_inc(sem("gdn_turn_read"), 1)
                dve.tensor_tensor(v_b[a][:], bank(7), by_head(g_cv[:, t, :]), ALU.mult).then_inc(sem("gdn_turn_read"), 1)
                dve.wait_ge(sem("p_decay_done"), t + 1)
                dve.tensor_tensor(p_t[a][:], bank(5), e_d[a][:], ALU.mult).then_inc(sem("gdn_turn_read"), 1)

            def gdn_pair(i, before):
                if before is not None:
                    dve.wait_ge(sem("wu_prod"), 4 * i)
                gdn_decay(i)
                for n in range(1, len(LEVELS)):
                    old, new, last = (n - 1) % 2, n % 2, n == len(LEVELS) - 1
                    if before is not None and not last:
                        gdn_new_values(before, n - 1)
                    if last:
                        gdn_scaled(i, 0)
                    for a in range(2):
                        dve.wait_ge(sem("zt_prod"), 10 * i + (2 * (n - 1) + a + 1))
                        ins = dve.tensor_tensor(t_r[new][a][:], t_r[old][a][:], bank(2 + 2 * a), ALU.subtract)
                        if last:
                            ins.then_inc(sem("t_last_done"), 1)
                        else:
                            dve.wait_ge(sem("z_prod"), 8 * i + (2 * (n - 1) + a + 1))
                            dve.tensor_tensor(t_f[new][a][:], t_f[old][a][:], bank(3 + 4 * a), ALU.subtract)\
                                .then_inc(sem("t_done"), 1)
                            if a == 0 and before is not None:
                                gdn_new_state(before, n - 1)
                    if before is not None and n == 2:
                        gdn_take_out(before, 0)
                    if before is not None and n == 4:
                        gdn_out(before, 0)
                        gdn_take_out(before, 1)
                gdn_scaled(i, 1)
                if before is not None:
                    gdn_out(before, 1)

            dve.memset(state[0][:], 0.0).then_inc(sem("state_done"), 1)
            gdn_pair(0, None)
            with dve.Fori(0, GDN_PAIRS - 1) as i:
                ch.loop(i, 8 + 2)
                gdn_pair(i + 1, i)
            ch.end(GDN_PAIRS - 1)
            for k in range(4):
                gdn_new_values(GDN_PAIRS - 1, k)
                gdn_new_state(GDN_PAIRS - 1, k)
                if k % 2:
                    gdn_take_out(GDN_PAIRS - 1, k // 2)
                    gdn_out(GDN_PAIRS - 1, k // 2)

            for h in range(2):
                norm_split("mixt", h, mixt_hi, mixt_lo)

            def post_norm(tag, row, tiles, ready=None):
                for t in tiles:
                    if ready:
                        ready(t)
                    dve.wait_ge(sem("norm_rstd_done"), NORM_AT[tag, t] + 1)
                    ch.link(dve.scalar_tensor_tensor(acc[:, t, :], acc[:, t, :], rstd[:, t:t + 1], row[:], ALU.mult, ALU.mult))
                    dve.tensor_tensor(resid[:, t, :], resid[:, t, :], acc[:, t, :], ALU.add).then_inc(sem("resid_done"), 1)

            def ffn_pre_gain(k):
                return vec[:, V_FFNPRE + k:V_FFNPRE + k + 1]

            dve.wait_ge(sem("post_gain_in"), 16)
            for h, tiles in enumerate((EARLY, LATE)):
                post_norm("mix_post", mix_post_row, tiles, lambda t: dve.wait_ge(sem(f"x_in{t}"), 32))
                norm_split("n2", h, act_hi, act_lo, ffn_pre_gain)

            def modulation(i, j):
                w = ada[j % 2]
                dve.wait_ge(sem(f"ada_in{j % 2}"), (32 if j % 2 == 0 else 16) * i + (j // 2 + 1) * 16)
                c = vec2[:, N_BADA:N_VEC2].unsqueeze(2).broadcast_to([P, KD, P])
                ch.link(dve.tensor_tensor(w[:], w[:], c, ALU.mult))
                ch.link(dve.tensor_tensor(w[:, 0:4, :], w[:, 0:4, :], w[:, 4:8, :], ALU.add))
                ch.link(dve.tensor_tensor(w[:, 0:2, :], w[:, 0:2, :], w[:, 2:4, :], ALU.add))
                dve.tensor_tensor(w[:, 0, :], w[:, 0, :], w[:, 1, :], ALU.add).then_inc(sem("ada_sum"), 1)

            def post_scale(tag, row, t):
                dve.wait_ge(sem("norm_rstd_done"), NORM_AT[tag, t] + 1)
                dve.scalar_tensor_tensor(acc[:, t, :], acc[:, t, :], rstd[:, t:t + 1], row[:], ALU.mult, ALU.mult)\
                    .then_inc(sem("post_scaled"), 1)

            def post_late(run, tag, row):
                dve.wait_ge(sem("resid_done"), NT * (2 * run + 1) + len(EARLY))
                for t in LATE:
                    if t >= NT - 2:
                        post_scale(tag, row, t)
                    dve.wait_ge(sem("post_scaled"), NT * run + t + 1)
                    dve.tensor_tensor(resid[:, t, :], resid[:, t, :], acc[:, t, :], ALU.add).then_inc(sem("resid_done"), 1)

            def ffn_sums(ring, run, tag, row, before_last):
                def step(i, last):
                    if run == 0:
                        modulation(i, 0)
                        modulation(i, 1)
                    for q in range(4):
                        j, cols = q % 2, slice((q // 2) * HALF, (q // 2 + 1) * HALF)
                        dve.wait_ge(sem("ffn_relu"), 4 * i + (4 * FFN_STEPS * run + q + 1))
                        dve.wait_ge(sem("ffn_hid"), 4 * i + (4 * FFN_STEPS * run + q + FFN_CREDIT))
                        ch.link(dve.tensor_tensor(relu_sq[:], relu_t[q % 2][:], relu_t[q % 2][:], ALU.mult))
                        dve.wait_ge(sem("ffn_hid_hi"), 4 * i + (4 * FFN_STEPS * run + q + 1))
                        dve.tensor_tensor(hid_lo[:, j, cols], relu_sq[:], hid_hi[:, j, cols].bitcast(F32), ALU.subtract)\
                            .then_inc(sem("ffn_hid"), 1)
                    dve.wait_ge(sem("ffn_acc"), 16 * i + ((16 * FFN_STEPS + 4) * run + 4))
                    for g in range(16):
                        t, cols = g // 2, slice((g % 2) * HALF, (g % 2 + 1) * HALF)
                        if g < 15:
                            dve.wait_ge(sem("ffn_down"), 15 * i + (15 * FFN_STEPS * run + g + 1))
                        else:
                            ring.panel_done(dve, 4 * i, 3)
                        dve.tensor_tensor(acc[:, t, cols], ps[:, 4 + g % 4, :], acc[:, t, cols], ALU.add)\
                            .then_inc(sem("ffn_acc"), 1)
                        if run == 0 and g == 3:
                            modulation(i, 2)
                        if last and g == 3:
                            before_last()
                        if last and g % 2 and t >= 2:
                            post_scale(tag, row, t - 2)
                    dve.wait_ge(sem("ffn_acc"), 16 * i + ((16 * FFN_STEPS + 4) * run + 20))

                with dve.Fori(0, FFN_STEPS - 1) as i:
                    ch.loop(i, 4 if run else 4 + 3 * ADA_STEP)
                    step(i, False)
                ch.end(FFN_STEPS - 1)
                step(FFN_STEPS - 1, True)

            ffn_sums(R4, 0, "ffn_post", ffn_post_row, lambda: dve.wait_ge(sem("post_gain_in"), 32))
            def modulation_scales():
                dve.wait_ge(sem("ada_read"), FFN_STEPS + 1)
                ch.link(dve.tensor_tensor(mod[:], mod[:], vec2[:, 0:N_BADA], ALU.add))
                for n, (gain, col) in enumerate(((V_GPREMIX2, KD), (V_GPREMLP2, 4 * KD))):
                    ch.link(dve.scalar_tensor_tensor(scale2[:, n * KD:(n + 1) * KD], mod[:, col:col + KD], 1.0,
                                                     vec[:, gain:gain + KD], ALU.add, ALU.mult))
                dve.sem_inc(sem("mod_scales_done"), 1)

            modulation_scales()
            post_late(0, "ffn_post", ffn_post_row)
            for h in range(2):
                norm_split("n3", h, act_hi, act_lo)

            dve.wait_ge(sem("turn_split"), TURNS["n3"] + 2 * KD)
            ch.link(dve.memset(vpad[:, 0:CONV2_TAPS - 1], 0.0))
            with dve.Fori(0, CONV2_PANELS) as i:
                ch.loop(i, 3)

                def tap(w):
                    return vec[:, bass.ds(V_CONV2 + w * CONV2_PANELS + i, 1)]

                R5.panel_done(dve, 3 * i, 1)
                dve.wait_ge(sem("c2_cg_read"), i + 2)
                dve.tensor_tensor(vpad[:, CONV2_TAPS - 1:], ps[:, 2:4, :].rearrange("p b n -> p (b n)"), cg_t[:], ALU.mult)\
                    .then_inc(sem("c2_v_done"), 1)
                dve.wait_ge(sem("c2_v_done"), i + 2)
                ch.link(dve.tensor_scalar(conv2_y[:], vpad[:, 0:SEQ], tap(0), None, ALU.mult))
                for w in range(1, CONV2_TAPS):
                    ch.link(dve.scalar_tensor_tensor(conv2_y[:], vpad[:, w:w + SEQ], tap(w), conv2_y[:], ALU.mult, ALU.add))
                R5.panel_done(dve, 3 * i, 2)
                dve.tensor_tensor(conv2_y[:], ps[:, 4:6, :].rearrange("p b n -> p (b n)"), conv2_y[:], ALU.mult)\
                    .then_inc(sem("c2_y_done"), 1)
                dve.wait_ge(sem("c2_hi_done"), i + 1)
                dve.wait_ge(sem("c2_y_done"), i + 2)
                dve.tensor_tensor(y_lo[:, i, :], conv2_y[:], y_hi[:, i, :].bitcast(F32), ALU.subtract)\
                    .then_inc(sem("c2_split"), 1)
                dve.wait_ge(sem("c2_split"), i + 1)
            ch.end(CONV2_PANELS)

            dve.wait_ge(sem("x1_stored"), 16 * NT)
            with dve.Fori(0, KD // 2) as i:
                for j in range(2):
                    R6.panel_done(dve, 4 * i, 2 + j)
                    dve.wait_ge(sem("m_gate_read"), 2 * i + (j + 3))
                    dve.scalar_tensor_tensor(merged[:, 2 * i + j, :], conv_gate[j][:], 1.0,
                                             ps[:, MERGE_PROJS[0][j]:MERGE_PROJS[0][j] + 2, :].rearrange("p b n -> p (b n)"), ALU.add, ALU.mult)\
                        .then_inc(sem("m_done"), 1)

            z_scale = float(SB_DIM) ** -0.5

            def sb_take(i, s):
                t = s // 2
                n, z = (t + 1) * P, sb_z[s % 2]
                dve.wait_ge(sem("sb_scores"), SB_ITEMS * i + s + 1)
                ch.link(dve.tensor_scalar(z[:, 0:n], ps[:, 2 * (s % 2):2 * (s % 2) + 2, :].rearrange("p b n -> p (b n)")[:, 0:n],
                                          z_scale, None, ALU.mult))
                dve.tensor_tensor(z[:, t * P:n], z[:, t * P:n], consts[:, C_KEYCAP:C_KEYCAP + P], ALU.min)\
                    .then_inc(sem("sb_z_done"), 1)

            def sb_log_weights(i, s):
                n = (s // 2 + 1) * P
                z, l = sb_z[s % 2][:, 0:n], sb_w[s % SB_SLOTS][:, 0:n]
                dve.wait_ge(sem("sb_ln_done"), SB_ITEMS * i + s + 1)
                ch.link(dve.scalar_tensor_tensor(l, z, 0.0, l, ALU.max, ALU.add))
                ch.link(dve.tensor_tensor_scan(l[:, ::-1], l[:, ::-1], l[:, ::-1], 0.0, ALU.add, ALU.bypass))
                dve.tensor_tensor(l, z, l, ALU.subtract).then_inc(sem("sb_arg_done"), 1)
                dve.wait_ge(sem("sb_arg_done"), SB_ITEMS * i + s + 1)

            def sb_out(i, half):
                dve.wait_ge(sem("sb_pv"), SB_GROUPS * i + (sb_groups(half * NT + NT - 1)[-1] + 3))
                dve.tensor_copy(o2[:, 4 * half:4 * half + 4, bass.ds(P * i, P)],
                                ps[:, 6, :].rearrange("p (t e) -> p t e", t=4)).then_inc(sem("sb_o_done"), 1)

            def sb_pair(i, before):
                for s in range(SB_ITEMS):
                    sb_take(i, s)
                    if late := lagged(i, before, s, SB_LAG_ARG, SB_ITEMS):
                        sb_log_weights(*late)
                    if before is not None and s == SB_LAG_PV - 1:
                        sb_out(before, 1)
                    if s == NT + SB_LAG_PV - 1:
                        sb_out(i, 0)

            sb_pair(0, None)
            with dve.Fori(0, SB_PAIRS - 2) as i:
                ch.loop(i, 3 * SB_ITEMS)
                sb_pair(i + 1, i)
            ch.end(SB_PAIRS - 2)
            sb_pair(SB_PAIRS - 1, SB_PAIRS - 2)
            sb_log_weights(SB_PAIRS - 1, SB_ITEMS - SB_LAG_ARG)
            sb_out(SB_PAIRS - 1, 1)

            for h in range(2):
                norm_split("sb_o", h, o2_hi, o2_lo, nk=CONV2_PANELS)

            def gate_diag(run):
                col = mod[:, (2 + 3 * run) * KD:(3 + 3 * run) * KD]
                dve.tensor_tensor(diag[:], consts[:, C_ID:C_ID + P].unsqueeze(1).broadcast_to([P, KD, P]),
                                  col.unsqueeze(2).broadcast_to([P, KD, P]), ALU.mult).then_inc(sem("gate_diag_done"), 1)

            gate_diag(0)
            with dve.Fori(0, KD // 2) as i:
                ch.loop(i, 2)
                for j in range(2):
                    p = 2 * i + j
                    R9.panel_done(dve, 4 * i, 2 + j)
                    dve.wait_ge(sem("m_gate_read"), p + KD + 3)
                    ch.link(dve.scalar_tensor_tensor(attn_part[j][:], attn_gate[j][:], 1.0,
                                                     ps[:, MERGE_PROJS[1][j]:MERGE_PROJS[1][j] + 2, :].rearrange("p b n -> p (b n)"),
                                                     ALU.add, ALU.mult))
                    dve.tensor_tensor(merged[:, p, :], merged[:, p, :], attn_part[j][:], ALU.add).then_inc(sem("m_done"), 1)
                    dve.wait_ge(sem("m_done"), p + KD + 3)
            ch.end(KD // 2)
            dve.wait_ge(sem("gate_row_prod"), 1)
            gate_diag(1)
            R9.panel_done(dve, 0, 2 * KD - 3)
            for k in range(KD):
                dve.wait_ge(sem("merged_hi_done"), k + 1)
                dve.scalar_tensor_tensor(act_lo[:, k, :], merged[:, k, :], 0.5, act_hi[:, k, :].bitcast(F32),
                                         ALU.mult, ALU.subtract).then_inc(sem("merged_split"), 1)

            dve.wait_ge(sem("post_gain_in"), 64)
            for run in range(2):
                dve.wait_ge(sem("gate_row_prod"), run + 1)
                dve.tensor_tensor(gate_rows[run][:], ps[:, 4 + 2 * run:6 + 2 * run, :].rearrange("p b n -> p (b n)"),
                                  gate_rows[run][:], ALU.mult).then_inc(sem("gate_rows_done"), 1)
            dve.wait_ge(sem("gate_rows_done"), 2)
            for h, tiles in enumerate((EARLY, LATE)):
                post_norm("mix_post2", gate_rows[0], tiles, lambda t: dve.wait_ge(sem(f"x_in{t}"), 48))
                norm_split("n4", h, act_hi, act_lo)
            ffn_sums(R11, 1, "ffn_post2", gate_rows[1], lambda: None)
            post_late(1, "ffn_post2", gate_rows[1])


def kernel(**inputs):
    from concourse import bacc
    from concourse.bass_utils import run_bass_kernel_spmd

    nc = bacc.Bacc("TRN2", target_bir_lowering=False, num_devices=1)
    arrays, d = {}, {}
    for name, value in list(inputs.items()) + [("consts", constants())]:
        a = np.ascontiguousarray(value)
        arrays[f"in_{name}"] = a
        d[name] = nc.dram_tensor(f"in_{name}", a.shape, mybir.dt.from_np(a.dtype), kind="ExternalInput").ap()
    out = nc.dram_tensor("out_0", [1, SEQ, D], F32, kind="ExternalOutput").ap()
    two_blocks(nc, d, out)
    r = run_bass_kernel_spmd(nc, [arrays], core_ids=[0])
    return r.results[0]["out_0"]
```
